# Optimizing a Trainium2 kernel written in Bass

```python
import math
import jax, jax.numpy as jnp
from jax import lax
import numpy as np
import jax
import jax.numpy as jnp

D_MODEL = 1024
BATCH = 1
SEQ = 512
DEPTH = 1

SSD_EXPAND = 2
D_SSD = SSD_EXPAND * D_MODEL
SSD_HEADDIM = 64
SSD_HEADS = D_SSD // SSD_HEADDIM
SSD_GROUPS = 8
SSD_STATE = 128
SSD_CONV = 4
SSD_CHUNK = 128
D_XBC = D_SSD + 2 * SSD_GROUPS * SSD_STATE
POOL_WINDOWS = (2, 4, 8, 16)
POOL_GROUPS = len(POOL_WINDOWS)
D_POOL = D_MODEL
POOL_GDIM = D_POOL // POOL_GROUPS
N_BRANCHES = 2
SPLIT_OFFSETS = (D_SSD, D_SSD + D_XBC, D_SSD + D_XBC + SSD_HEADS, D_SSD + D_XBC + SSD_HEADS + D_POOL)
D_IN_PROJ = D_SSD + D_XBC + SSD_HEADS + D_POOL + N_BRANCHES * D_MODEL
N_EXPERTS = 64
TOP_K = 8
N_EXPERT_GROUPS = 8
EXPERTS_PER_GROUP = N_EXPERTS // N_EXPERT_GROUPS
TOPK_GROUPS = 4
D_EXPERT = 256
D_SHARED = 256
ROUTED_SCALE = 2.5
MOE_BLOCK = 128
N_ADA = 6
EPS = 1e-6


def rmsnorm(x, g):
    xf = x.astype(jnp.float32)
    inv = lax.rsqrt(jnp.mean(xf * xf, axis=-1, keepdims=True) + EPS)
    return (xf * inv * g.astype(jnp.float32)).astype(x.dtype)

def modulate(x, shift, scale):
    return x * (1 + scale[:, None, :]) + shift[:, None, :]

def causal_dwconv(x, w, b):
    K, C = w.shape
    y = lax.conv_general_dilated(x, w[:, None, :].astype(x.dtype), window_strides=(1,),
                                 padding=[(K - 1, 0)], dimension_numbers=('NWC', 'WIO', 'NWC'),
                                 feature_group_count=C)
    return y + b

def segsum_exp(a):
    Q = a.shape[-1]
    cs = jnp.cumsum(a, axis=-1)
    diff = cs[..., :, None] - cs[..., None, :]
    mask = jnp.tril(jnp.ones((Q, Q), dtype=bool))
    return jnp.where(mask, jnp.exp(jnp.where(mask, diff, 0.0)), 0.0)

def ssd_chunked(xh, dt, A, Bm, Cm):
    Bsz, S, H, P = xh.shape
    G, N = Bm.shape[-2:]
    R = H // G
    Q = SSD_CHUNK
    nc = S // Q
    x = (xh * dt[..., None]).reshape(Bsz, nc, Q, G, R, P)
    a = (dt * A).reshape(Bsz, nc, Q, G, R).transpose(0, 1, 3, 4, 2)
    Bc = Bm.reshape(Bsz, nc, Q, G, N)
    Cc = Cm.reshape(Bsz, nc, Q, G, N)
    a_cs = jnp.cumsum(a, axis=-1)
    L = segsum_exp(a)
    CB = jnp.einsum('bclgn,bcsgn->bcgls', Cc, Bc)
    y_diag = jnp.einsum('bcgls,bcgrls,bcsgrp->bclgrp', CB, L, x)
    decay_states = jnp.exp(a_cs[..., -1:] - a_cs)
    states = jnp.einsum('bclgn,bcgrl,bclgrp->bcgrpn', Bc, decay_states, x)
    chunk_decay = jnp.exp(a_cs[..., -1])

    def step(carry, inp):
        st, dec = inp
        return carry * dec[..., None, None] + st, carry

    init = jnp.zeros(states.shape[:1] + states.shape[2:], states.dtype)
    _, prev = lax.scan(step, init, (jnp.moveaxis(states, 1, 0), jnp.moveaxis(chunk_decay, 1, 0)))
    prev = jnp.moveaxis(prev, 0, 1)
    y_off = jnp.einsum('bclgn,bcgrpn,bcgrl->bclgrp', Cc, prev, jnp.exp(a_cs))
    return (y_diag + y_off).reshape(Bsz, S, H, P)

def ssd_branch(z, xbc, dt_raw, conv_w, conv_b, dt_bias, A_log, D_skip, norm_g):
    xbc = jax.nn.silu(causal_dwconv(xbc, conv_w, conv_b))
    Bsz, S, _ = xbc.shape
    GN = SSD_GROUPS * SSD_STATE
    xs = xbc[..., :D_SSD].reshape(Bsz, S, SSD_HEADS, SSD_HEADDIM)
    Bm = xbc[..., D_SSD:D_SSD + GN].reshape(Bsz, S, SSD_GROUPS, SSD_STATE)
    Cm = xbc[..., D_SSD + GN:].reshape(Bsz, S, SSD_GROUPS, SSD_STATE)
    dt = jax.nn.softplus((dt_raw + dt_bias).astype(jnp.float32))
    A = -jnp.exp(A_log.astype(jnp.float32))
    y = ssd_chunked(xs, dt, A, Bm, Cm) + D_skip[:, None] * xs
    y = y.reshape(Bsz, S, D_SSD) * jax.nn.silu(z)
    y = rmsnorm(y.reshape(Bsz, S, SSD_GROUPS, D_SSD // SSD_GROUPS), norm_g.reshape(SSD_GROUPS, -1))
    return y.reshape(Bsz, S, D_SSD)

def pool_branch(xp, pool_w, pool_scale):
    Bsz, S, _ = xp.shape
    xg = xp.reshape(Bsz, S, POOL_GROUPS, POOL_GDIM).astype(jnp.float32)
    csp = jnp.pad(jnp.cumsum(xg, axis=1), ((0, 0), (1, 0), (0, 0), (0, 0)))
    pos = jnp.arange(1, S + 1, dtype=jnp.float32)
    outs = []
    for gi, w in enumerate(POOL_WINDOWS):
        c_g = csp[:, :, gi]
        lower = jnp.concatenate([jnp.zeros((Bsz, w - 1, POOL_GDIM), c_g.dtype), c_g[:, :S + 1 - w]], axis=1)
        mean = (c_g[:, 1:] - lower) / jnp.minimum(pos, w)[None, :, None]
        outs.append(mean - xg[:, :, gi])
    pooled = jnp.stack(outs, axis=2).astype(xp.dtype)
    mixed = jnp.einsum('bsgc,gcd->bsgd', pooled, pool_w)
    return mixed.reshape(Bsz, S, D_POOL) * pool_scale

def moe_ffn(u, w_router, router_bias, we_gate, we_up, we_down, ws_gate, ws_up, ws_down):
    Bsz, S, D = u.shape
    N = Bsz * S
    uf = u.reshape(N, D)
    scores = jax.nn.sigmoid((uf @ w_router).astype(jnp.float32))
    choice = scores + router_bias.astype(jnp.float32)
    grp = choice.reshape(N, N_EXPERT_GROUPS, EXPERTS_PER_GROUP)
    grp_score = lax.top_k(grp, 2)[0].sum(-1)
    _, top_grp = lax.top_k(grp_score, TOPK_GROUPS)
    grp_mask = jnp.any(top_grp[:, :, None] == jnp.arange(N_EXPERT_GROUPS)[None, None, :], axis=1)
    masked = jnp.where(jnp.repeat(grp_mask, EXPERTS_PER_GROUP, axis=1), choice, -jnp.inf)
    _, top_e = lax.top_k(masked, TOP_K)
    wts = jnp.take_along_axis(scores, top_e, axis=1)
    wts = wts / jnp.sum(wts, axis=-1, keepdims=True) * ROUTED_SCALE
    NK = N * TOP_K
    e_flat = top_e.reshape(NK).astype(jnp.int32)
    tok_flat = jnp.arange(NK, dtype=jnp.int32) // TOP_K
    order = jnp.argsort(e_flat)
    e_sorted = e_flat[order]
    counts = jax.ops.segment_sum(jnp.ones((NK,), jnp.int32), e_flat, num_segments=N_EXPERTS)
    padded = (counts + MOE_BLOCK - 1) // MOE_BLOCK * MOE_BLOCK
    starts = jnp.cumsum(counts) - counts
    pends = jnp.cumsum(padded)
    pstarts = pends - padded
    dest = pstarts[e_sorted] + jnp.arange(NK, dtype=jnp.int32) - starts[e_sorted]
    n_blocks = -(-NK // MOE_BLOCK) + N_EXPERTS
    n_slots = n_blocks * MOE_BLOCK
    slot_tok = jnp.full((n_slots,), N, jnp.int32).at[dest].set(tok_flat[order])
    slot_w = jnp.zeros((n_slots,), u.dtype).at[dest].set(wts.reshape(NK)[order].astype(u.dtype))
    block_e = jnp.minimum(jnp.searchsorted(pends, jnp.arange(n_blocks, dtype=jnp.int32) * MOE_BLOCK, side='right'),
                          N_EXPERTS - 1).astype(jnp.int32)
    u_pad = jnp.concatenate([uf, jnp.zeros((1, D), uf.dtype)], axis=0)

    def expert_block(args):
        toks, ws, e = args
        xb = u_pad[toks]
        hid = jax.nn.silu(xb @ we_gate[e]) * (xb @ we_up[e])
        return (hid @ we_down[e]) * ws[:, None]

    y_slots = lax.map(expert_block, (slot_tok.reshape(n_blocks, MOE_BLOCK),
                                     slot_w.reshape(n_blocks, MOE_BLOCK), block_e))
    routed = jax.ops.segment_sum(y_slots.reshape(n_slots, D), slot_tok, num_segments=N + 1)[:N]
    shared = (jax.nn.silu(uf @ ws_gate) * (uf @ ws_up)) @ ws_down
    return (routed + shared).reshape(Bsz, S, D)

def first_inputs(seed: int = 0) -> dict:
    key = jax.random.key(seed)
    ks = jax.random.split(key, 32)
    f32 = jnp.float32

    def nrm(k, shape, scale):
        return jax.random.normal(k, shape, f32) * scale

    dt0 = jnp.exp(jax.random.uniform(ks[8], (DEPTH, SSD_HEADS), f32, math.log(1e-3), math.log(1e-1)))
    return {
        'x': nrm(ks[0], (BATCH, SEQ, D_MODEL), 1.0),
        'c': nrm(ks[1], (BATCH, D_MODEL), 1.0),
        'w_ada': nrm(ks[2], (DEPTH, D_MODEL, N_ADA * D_MODEL), 0.5 * D_MODEL ** -0.5),
        'b_ada': nrm(ks[3], (DEPTH, N_ADA * D_MODEL), 0.02),
        'norm_mix_g': 1.0 + nrm(ks[4], (DEPTH, D_MODEL), 0.02),
        'w_in': nrm(ks[5], (DEPTH, D_MODEL, D_IN_PROJ), D_MODEL ** -0.5),
        'conv_w': nrm(ks[6], (DEPTH, SSD_CONV, D_XBC), SSD_CONV ** -0.5),
        'conv_b': nrm(ks[7], (DEPTH, D_XBC), 0.02),
        'dt_bias': dt0 + jnp.log(-jnp.expm1(-dt0)),
        'A_log': jnp.log(jax.random.uniform(ks[9], (DEPTH, SSD_HEADS), f32, 1.0, 16.0)),
        'D_skip': 1.0 + nrm(ks[10], (DEPTH, SSD_HEADS), 0.02),
        'ssd_norm_g': 1.0 + nrm(ks[11], (DEPTH, D_SSD), 0.02),
        'pool_w': nrm(ks[12], (DEPTH, POOL_GROUPS, POOL_GDIM, POOL_GDIM), POOL_GDIM ** -0.5),
        'pool_scale': 1.0 + nrm(ks[13], (DEPTH, D_POOL), 0.02),
        'w_br_ssd': nrm(ks[14], (DEPTH, D_SSD, D_MODEL), D_SSD ** -0.5),
        'w_br_pool': nrm(ks[15], (DEPTH, D_POOL, D_MODEL), D_POOL ** -0.5),
        'w_out': nrm(ks[16], (DEPTH, D_MODEL, D_MODEL), D_MODEL ** -0.5),
        'norm_ffn_g': 1.0 + nrm(ks[17], (DEPTH, D_MODEL), 0.02),
        'w_router': nrm(ks[18], (DEPTH, D_MODEL, N_EXPERTS), D_MODEL ** -0.5),
        'router_bias': nrm(ks[19], (DEPTH, N_EXPERTS), 0.01),
        'we_gate': nrm(ks[20], (DEPTH, N_EXPERTS, D_MODEL, D_EXPERT), D_MODEL ** -0.5),
        'we_up': nrm(ks[21], (DEPTH, N_EXPERTS, D_MODEL, D_EXPERT), D_MODEL ** -0.5),
        'we_down': nrm(ks[22], (DEPTH, N_EXPERTS, D_EXPERT, D_MODEL), D_EXPERT ** -0.5),
        'ws_gate': nrm(ks[23], (DEPTH, D_MODEL, D_SHARED), D_MODEL ** -0.5),
        'ws_up': nrm(ks[24], (DEPTH, D_MODEL, D_SHARED), D_MODEL ** -0.5),
        'ws_down': nrm(ks[25], (DEPTH, D_SHARED, D_MODEL), D_SHARED ** -0.5),
        'final_norm_g': 1.0 + nrm(ks[26], (D_MODEL,), 0.02),
    }

def first_block(x, c, w_ada, b_ada, norm_mix_g, w_in, conv_w, conv_b, dt_bias, A_log, D_skip, ssd_norm_g,
              pool_w, pool_scale, w_br_ssd, w_br_pool, w_out, norm_ffn_g, w_router, router_bias,
              we_gate, we_up, we_down, ws_gate, ws_up, ws_down, final_norm_g):
    h = x
    c_act = jax.nn.silu(c)
    for l in range(DEPTH):
        mod = c_act @ w_ada[l] + b_ada[l]
        sh1, sc1, g1, sh2, sc2, g2 = jnp.split(mod, N_ADA, axis=-1)
        u = modulate(rmsnorm(h, norm_mix_g[l]), sh1, sc1)
        proj = u @ w_in[l]
        z, xbc, dt_raw, xp, gts = jnp.split(proj, SPLIT_OFFSETS, axis=-1)
        y_ssd = ssd_branch(z, xbc, dt_raw, conv_w[l], conv_b[l], dt_bias[l], A_log[l], D_skip[l],
                           ssd_norm_g[l]) @ w_br_ssd[l]
        y_pool = pool_branch(xp, pool_w[l], pool_scale[l]) @ w_br_pool[l]
        g_ssd, g_pool = jnp.split(jax.nn.sigmoid(gts), N_BRANCHES, axis=-1)
        mixed = (g_ssd * y_ssd + g_pool * y_pool) @ w_out[l]
        h = h + g1[:, None, :] * mixed
        u2 = modulate(rmsnorm(h, norm_ffn_g[l]), sh2, sc2)
        h = h + g2[:, None, :] * moe_ffn(u2, w_router[l], router_bias[l], we_gate[l], we_up[l], we_down[l],
                                         ws_gate[l], ws_up[l], ws_down[l])
    return rmsnorm(h, final_norm_g)


DEPTH_2 = 2

N_A = DEPTH_2 // 2
N_B = DEPTH_2 - N_A
PLE_DIM = 256
RWKV_HEAD = 64
RWKV_HEADS = D_MODEL // RWKV_HEAD
DECAY_LORA = 64
ICLR_LORA = 64
GN_EPS = 64e-5
DIFF_HEAD = 64
DIFF_HEADS = D_MODEL // (2 * DIFF_HEAD)
ROPE_DIMS = DIFF_HEAD // 4
ROPE_THETA = 500000.0
Q_BLOCK = 128
NORM_EPS = 1e-6
SUBLN_EPS = 1e-5


def rms_norm(x, g, eps=NORM_EPS):
    xf = x.astype(jnp.float32)
    y = xf * lax.rsqrt(jnp.mean(xf * xf, axis=-1, keepdims=True) + eps)
    return (y * g.astype(jnp.float32)).astype(x.dtype)

def rwkv7_time_mix(xn, mu, w_in, w0, w1, w2, a0, a1, a2, k_k, k_a, r_k, lnx_g, lnx_b, w_out):
    B, S, D = xn.shape
    H, N = RWKV_HEADS, RWKV_HEAD
    f32 = jnp.float32
    x_prev = jnp.pad(xn, ((0, 0), (1, 0), (0, 0)))[:, :-1]
    xmix = xn[None] + (x_prev - xn)[None] * mu[:, None, None, :]
    rkvg = jnp.einsum('cbsd,cde->cbse', xmix[:4], w_in)
    r, k, v, g = rkvg[0], rkvg[1], rkvg[2], rkvg[3]
    xw, xa = xmix[4], xmix[5]
    w_pre = (w0 + jnp.tanh(xw @ w1) @ w2).astype(f32)
    decay = jnp.exp(-jnp.exp(-jax.nn.softplus(-w_pre) - 0.5))
    a = jax.nn.sigmoid((a0 + (xa @ a1) @ a2).astype(f32))
    heads = lambda t: t.astype(f32).reshape(B, S, H, N)
    r, k, v, decay, a = heads(r), heads(k), heads(v), heads(decay), heads(a)
    kk = k * k_k.astype(f32).reshape(H, N)
    kk = kk / jnp.maximum(jnp.linalg.norm(kk, axis=-1, keepdims=True), 1e-12)
    k = k * (1.0 + (a - 1.0) * k_a.astype(f32).reshape(H, N))

    def step(state, inp):
        r_t, w_t, k_t, v_t, kk_t, a_t = inp
        s_kk = jnp.einsum('bhij,bhj->bhi', state, kk_t)
        state = (state * w_t[:, :, None, :]
                 - s_kk[..., None] * (kk_t * a_t)[:, :, None, :]
                 + v_t[..., None] * k_t[:, :, None, :])
        return state, jnp.einsum('bhij,bhj->bhi', state, r_t)

    seq_first = lambda t: jnp.swapaxes(t, 0, 1)
    state0 = jnp.zeros((B, H, N, N), f32)
    _, y = lax.scan(step, state0, (seq_first(r), seq_first(decay), seq_first(k),
                                   seq_first(v), seq_first(kk), seq_first(a)))
    y = jnp.swapaxes(y, 0, 1)
    mean = jnp.mean(y, axis=-1, keepdims=True)
    var = jnp.mean(jnp.square(y - mean), axis=-1, keepdims=True)
    y = ((y - mean) * lax.rsqrt(var + GN_EPS) * lnx_g.astype(f32).reshape(H, N)
         + lnx_b.astype(f32).reshape(H, N))
    y = y + jnp.sum(r * k * r_k.astype(f32), axis=-1, keepdims=True) * v
    y = y.reshape(B, S, D).astype(xn.dtype) * jax.nn.silu(g)
    return y @ w_out

def rope_tables(S):
    inv = ROPE_THETA ** (-jnp.arange(0, ROPE_DIMS, 2, dtype=jnp.float32) / ROPE_DIMS)
    ang = jnp.arange(S, dtype=jnp.float32)[:, None] * inv[None, :]
    return jnp.cos(ang), jnp.sin(ang)

def partial_rope(x, cos, sin):
    half = ROPE_DIMS // 2
    c = cos[None, :, None, None, :].astype(x.dtype)
    s = sin[None, :, None, None, :].astype(x.dtype)
    x1, x2 = x[..., :half], x[..., half:ROPE_DIMS]
    return jnp.concatenate([x1 * c - x2 * s, x2 * c + x1 * s, x[..., ROPE_DIMS:]], axis=-1)

def shared_kv(h, kv_norm, kv_w, cos, sin):
    B, S, D = h.shape
    kv = rms_norm(h, kv_norm) @ kv_w
    k = partial_rope(kv[..., :D].reshape(B, S, DIFF_HEADS, 2, DIFF_HEAD), cos, sin)
    v = kv[..., D:].reshape(B, S, DIFF_HEADS, 2 * DIFF_HEAD)
    return k.transpose(0, 2, 3, 1, 4), v.transpose(0, 2, 1, 3)

def diff_attention_mix(xn, k_sh, v_sh, w_in, lam_qk, subln_g, w_out, lam_init, cos, sin):
    B, S, D = xn.shape
    H, Dh = DIFF_HEADS, DIFF_HEAD
    f32 = jnp.float32
    proj = xn @ w_in
    q = partial_rope(proj[..., :D].reshape(B, S, H, 2, Dh), cos, sin) * (Dh ** -0.5)
    gate = proj[..., D:]
    lq = lam_qk.astype(f32)
    lam = jnp.exp(jnp.sum(lq[0] * lq[1])) - jnp.exp(jnp.sum(lq[2] * lq[3])) + lam_init
    nblk = S // Q_BLOCK
    qb = q.reshape(B, nblk, Q_BLOCK, H, 2, Dh).transpose(1, 0, 3, 4, 2, 5)
    kf = k_sh.astype(f32)
    vf = v_sh.astype(f32)
    k_pos = jnp.arange(S)

    def block(args):
        q_blk, blk = args
        s = jnp.einsum('bhcqd,bhckd->bhcqk', q_blk.astype(f32), kf)
        q_pos = blk * Q_BLOCK + jnp.arange(Q_BLOCK)
        s = jnp.where(k_pos[None, :] <= q_pos[:, None], s, -1e30)
        prob = jax.nn.softmax(s, axis=-1)
        attn = prob[:, :, 0] - lam * prob[:, :, 1]
        return jnp.einsum('bhqk,bhkv->bhqv', attn, vf)

    o = lax.map(block, (qb, jnp.arange(nblk)))
    o = o.transpose(1, 0, 3, 2, 4).reshape(B, S, H, 2 * Dh)
    o = rms_norm(o, subln_g, SUBLN_EPS) * (1.0 - lam_init)
    o = o.reshape(B, S, D).astype(xn.dtype) * jax.nn.silu(gate)
    return o @ w_out

def second_inputs(seed: int = 0) -> dict:
    key = jax.random.key(seed)
    ks = iter(jax.random.split(key, 32))
    D, f32 = D_MODEL, jnp.float32
    nrm = lambda shape, scale: jax.random.normal(next(ks), shape, f32) * scale
    gain = lambda shape: 1.0 + nrm(shape, 0.02)
    return {
        'x': nrm((BATCH, SEQ, D), 1.0),
        'p': nrm((DEPTH_2, BATCH, SEQ, PLE_DIM), 1.0),
        'norm_pre': gain((DEPTH_2, D)),
        'norm_post': gain((DEPTH_2, D)),
        'a_mu': jax.random.uniform(next(ks), (N_A, 6, D), f32),
        'a_w_in': nrm((N_A, 4, D, D), D ** -0.5),
        'a_w0': jax.random.uniform(next(ks), (N_A, D), f32, -6.0, 1.0),
        'a_w1': nrm((N_A, D, DECAY_LORA), D ** -0.5),
        'a_w2': nrm((N_A, DECAY_LORA, D), 0.1),
        'a_a0': nrm((N_A, D), 0.5),
        'a_a1': nrm((N_A, D, ICLR_LORA), D ** -0.5),
        'a_a2': nrm((N_A, ICLR_LORA, D), 0.5 * ICLR_LORA ** -0.5),
        'a_k_k': 1.0 + nrm((N_A, D), 0.1),
        'a_k_a': 1.0 + nrm((N_A, D), 0.1),
        'a_r_k': nrm((N_A, RWKV_HEADS, RWKV_HEAD), 0.1),
        'a_lnx_g': gain((N_A, D)),
        'a_lnx_b': nrm((N_A, D), 0.02),
        'a_w_out': nrm((N_A, D, D), D ** -0.5),
        'kv_norm': gain((D,)),
        'kv_w': nrm((D, 2 * D), D ** -0.5),
        'b_w_in': nrm((N_B, D, 2 * D), D ** -0.5),
        'b_lambda': nrm((N_B, 4, DIFF_HEAD), 0.1),
        'b_subln': gain((N_B, 2 * DIFF_HEAD)),
        'b_w_out': nrm((N_B, D, D), D ** -0.5),
        'ple_w': nrm((DEPTH_2, PLE_DIM, D), PLE_DIM ** -0.5),
        'ple_gate': nrm((DEPTH_2, D, D), D ** -0.5),
        'ple_norm': gain((DEPTH_2, D)),
    }

def second_block(x, p, norm_pre, norm_post, a_mu, a_w_in, a_w0, a_w1, a_w2, a_a0, a_a1, a_a2,
              a_k_k, a_k_a, a_r_k, a_lnx_g, a_lnx_b, a_w_out, kv_norm, kv_w, b_w_in, b_lambda,
              b_subln, b_w_out, ple_w, ple_gate, ple_norm):
    S = x.shape[1]
    cos, sin = rope_tables(S)
    h = x
    k_sh = None
    v_sh = None
    for i in range(DEPTH_2):
        xn = rms_norm(h, norm_pre[i])
        if i < N_A:
            y = rwkv7_time_mix(xn, a_mu[i], a_w_in[i], a_w0[i], a_w1[i], a_w2[i], a_a0[i],
                               a_a1[i], a_a2[i], a_k_k[i], a_k_a[i], a_r_k[i], a_lnx_g[i],
                               a_lnx_b[i], a_w_out[i])
        else:
            if i == N_A:
                k_sh, v_sh = shared_kv(h, kv_norm, kv_w, cos, sin)
            j = i - N_A
            lam_init = 0.8 - 0.6 * math.exp(-0.3 * i)
            y = diff_attention_mix(xn, k_sh, v_sh, b_w_in[j], b_lambda[j], b_subln[j],
                                   b_w_out[j], lam_init, cos, sin)
        h = h + rms_norm(y, norm_post[i])
        e = p[i] @ ple_w[i]
        g = jax.nn.sigmoid(h @ ple_gate[i])
        h = h + rms_norm(g * e, ple_norm[i])
    return h


def setup_inputs(seed=0):
    out = dict(first_inputs(seed))
    for name, value in second_inputs(seed + 1).items():
        if name != "x":
            out[name + "_2"] = value
    return out


def reference(
    x, c, w_ada, b_ada, norm_mix_g, w_in, conv_w, conv_b, dt_bias, A_log, D_skip, ssd_norm_g,
    pool_w, pool_scale, w_br_ssd, w_br_pool, w_out, norm_ffn_g, w_router, router_bias, we_gate,
    we_up, we_down, ws_gate, ws_up, ws_down, final_norm_g, p_2, norm_pre_2, norm_post_2, a_mu_2,
    a_w_in_2, a_w0_2, a_w1_2, a_w2_2, a_a0_2, a_a1_2, a_a2_2, a_k_k_2, a_k_a_2, a_r_k_2,
    a_lnx_g_2, a_lnx_b_2, a_w_out_2, kv_norm_2, kv_w_2, b_w_in_2, b_lambda_2, b_subln_2,
    b_w_out_2, ple_w_2, ple_gate_2, ple_norm_2,
):
    x = first_block(
        x, c, w_ada, b_ada, norm_mix_g, w_in, conv_w, conv_b, dt_bias, A_log, D_skip,
        ssd_norm_g, pool_w, pool_scale, w_br_ssd, w_br_pool, w_out, norm_ffn_g, w_router,
        router_bias, we_gate, we_up, we_down, ws_gate, ws_up, ws_down, final_norm_g,
    )
    return second_block(
        x, p_2, norm_pre_2, norm_post_2, a_mu_2, a_w_in_2, a_w0_2, a_w1_2, a_w2_2, a_a0_2,
        a_a1_2, a_a2_2, a_k_k_2, a_k_a_2, a_r_k_2, a_lnx_g_2, a_lnx_b_2, a_w_out_2, kv_norm_2,
        kv_w_2, b_w_in_2, b_lambda_2, b_subln_2, b_w_out_2, ple_w_2, ple_gate_2, ple_norm_2,
    )


_drawn_inputs = setup_inputs


def setup_inputs(seed=0):
    import zlib

    import numpy as np

    out = dict(_drawn_inputs(seed))
    spreads = {}
    factors = {'D_skip': 3.647,
     'ssd_norm_g': 2.738,
     'pool_scale': 2.736,
     'norm_post_2': 3.162,
     'a_lnx_g_2': 3.975,
     'a_lnx_b_2': 2.958,
     'kv_norm_2': 3.965,
     'b_subln_2': 7.096,
     'ple_norm_2': 3.332}
    for name, (base, spread) in spreads.items():
        noise = np.random.default_rng([zlib.crc32(name.encode()), seed]).standard_normal(out[name].shape)
        drawn = base * np.exp(spread * noise) if base else spread * noise
        out[name] = jnp.asarray(drawn.astype(out[name].dtype))
    for name, factor in factors.items():
        out[name] = (out[name] * factor).astype(out[name].dtype)
    return out
```

```python
import numpy as np
import concourse.bass as bass
from concourse import mybir

F32 = mybir.dt.float32
ALU = mybir.AluOpType
ACT = mybir.ActivationFunctionType
AX = mybir.AxisListType
ds = bass.ds

P = 128
FIRST = 4096


class Mark:

    def __init__(self, count, n, loop=None, shift=0):
        self.count, self.n, self.loop, self.shift = count, n, loop, shift


class Count:

    def __init__(self, prog, name):
        self.prog, self.sem = prog, prog.nc.alloc_semaphore(name)
        self.n, self.start, self.per = 0, FIRST, 0
        if prog.begun:
            prog.nc.sync.sem_inc(self.sem, FIRST)
        prog.counts.append(self)

    def add(self, ins, by):
        self.n += by
        if ins is not None:
            ins.then_inc(self.sem, by)
        return self.mark()

    def mark(self):
        if self.prog.in_loop is None:
            return Mark(self, self.start + self.n)
        return Mark(self, self.n, self.prog.in_loop)

    def used(self):
        return self.start + self.n > FIRST

    def value(self, mark):
        if mark.loop is None:
            return mark.n
        assert mark.loop == self.prog.in_loop
        return (self.start - mark.shift * self.per + mark.n) + self.prog.iteration * self.per


def flat(marks):
    for m in marks:
        if isinstance(m, (list, tuple)):
            yield from flat(m)
        elif m is not None:
            yield m


class Lane:

    def __init__(self, prog, eng, name):
        self.prog, self.eng, self.count = prog, eng, Count(prog, f"{name}_done")
        prog.lanes.append(self)

    def wait(self, *marks):
        last = {}
        for m in flat(marks):
            place = (m.count, m.loop is not None)
            if place not in last or (-m.shift, m.n) > (-last[place].shift, last[place].n):
                last[place] = m
        for m in last.values():
            if not self.prog.dry:
                self.eng.wait_ge(m.count.sem, m.count.value(m))
                if self is self.prog.sp and m.loop is not None:
                    self.eng.sem_inc(self.prog.sp_waits, 1)

    def run(self, fn, *args, after=(), counted=True, **kw):
        self.wait(after, self.count.mark() if self is not self.prog.pe and self.count.used() else ())
        if self.prog.dry:
            return self.count.add(None, 1) if counted else None
        ins = fn(*args, **kw)
        return self.count.add(ins, 1) if counted else None

    def dma(self, slot, out, in_, after=()):
        self.wait(after)
        if not self.prog.dry:
            return slot.count.add(self.eng.dma_start(out, in_), 16)
        return slot.count.add(None, 16)


class Slot:

    def __init__(self, prog, tensor, name=None):
        self.t, self.free = tensor, []
        self.count = Count(prog, name) if name else None
        prog.slots.append(self)

    def __getitem__(self, key):
        return self.t[key]


class Ring:
    def __init__(self, prog, slots):
        self.slots, self.at = slots, 0
        prog.rings.append(self)

    def take(self, n=1):
        if self.at + n > len(self.slots):
            self.at = 0
        got = self.slots[self.at:self.at + n]
        self.at += n
        return got[0] if n == 1 else got


class Program:
    def __init__(self, nc):
        self.nc = nc
        self.counts, self.slots, self.rings, self.lanes = [], [], [], []
        self.in_loop, self.iteration, self.dry, self.loops = None, None, False, 0
        self.begun = False
        self.sp_waits = nc.alloc_semaphore("sp_waits")
        self.pe = None
        self.pe = Lane(self, nc.tensor, "pe")
        self.act = Lane(self, nc.scalar, "act")
        self.dve = Lane(self, nc.vector, "dve")
        self.pool = Lane(self, nc.gpsimd, "pool")
        self.sp = Lane(self, nc.sync, "sp")

    def arrivals(self, name):
        return Slot(self, None, f"{name}_{len(self.counts)}")

    def start(self):
        self.begun = True
        for c in self.counts:
            self.nc.sync.sem_inc(c.sem, FIRST)

    def _fresh(self):
        for r in self.rings:
            r.at = 0

    def loop(self, times, body):
        self._fresh()
        for c in self.counts:
            c.start, c.n = c.start + c.n, 0
        before = [list(s.free) for s in self.slots]
        self.loops += 1
        self.in_loop, self.dry = self.loops, True
        body(0)
        self.dry = False
        for c in self.counts:
            c.per, c.n = c.n, 0
        for s, b in zip(self.slots, before):
            s.free = b + [Mark(m.count, m.n, m.loop, 1) for m in s.free if m.loop is not None]
        self._fresh()
        with self.nc.Fori(0, times) as i:
            self.iteration = i
            body(i)
        self.in_loop = self.iteration = None
        for c in self.counts:
            c.start += (times - 1) * c.per
        for s in self.slots:
            s.free = [m if m.loop is None else Mark(m.count, m.count.start + m.n)
                      for m in s.free if not m.shift]
        for c in self.counts:
            c.start, c.n, c.per = c.start + c.n, 0, 0
        self._fresh()

    def join(self, *lanes):
        marks = [e.count.mark() for e in (self.pe, self.act, self.dve, self.pool) if e.count.used()]
        for lane in lanes:
            lane.wait(marks)

    def phase(self, *stores):
        marks = [e.count.mark() for e in (self.pe, self.act, self.dve, self.pool) if e.count.used()]
        for lane in self.lanes:
            lane.wait(marks, stores)
T = 512
D = 1024
KD = D // P
NT = T // P
ROUTED_SCALE = 2.5

BIG = 28160

CONST_COLS = {}


def const_table():
    parts = []

    def put(name, a):
        a = np.asarray(a, np.float32)
        start = sum(x.shape[1] for x in parts)
        CONST_COLS[name] = (start, a.shape[1])
        parts.append(a)

    r, c = np.arange(P)[:, None], np.arange(P)[None, :]
    t = np.arange(T)
    wide = np.ones((P, 1))
    put("ident", r == c)
    put("ones", np.ones((P, P)))
    put("upper", r <= c)
    put("same_head", r // 64 == c // 64)
    put("neg_up16", -1.0 * ((r < c) & (r // 16 == c // 16)))
    put("neg_low16", -1.0 * ((r > c) & (r // 16 == c // 16)))
    for b in (16, 32):
        put(f"neg_off{b}", -1.0 * ((r // (2 * b) == c // (2 * b)) & (r // b > c // b)))
    put("up64", (r < c) & (r // 64 == c // 64))
    put("upeq64", (r <= c) & (r // 64 == c // 64))
    put("future", np.where(c > r, -1e30, 0.0))
    g = np.arange(8)
    put("before8", wide * (g[None, :] < g[:, None]).reshape(1, 64))
    put("scan128", wide * (t % 128 != 0)[None, :])
    put("scan64", wide * (t % 64 != 0)[None, :])
    for w in (2, 4, 8, 16):
        put(f"inv{w}", wide * (1.0 / np.minimum(t + 1, w))[None, :])
    inv = np.float32(500000.0) ** (-np.arange(0, 16, 2, dtype=np.float32) / np.float32(16))
    ang = t.astype(np.float32)[:, None] * inv[None, :]
    cos, sin, turn = np.ones((P, T)), np.zeros((P, T)), np.zeros((P, P))
    for comp in (0, 64):
        for j in range(8):
            for half in (0, 8):
                cos[comp + half + j] = np.cos(ang[:, j])
                sin[comp + half + j] = np.sin(ang[:, j])
            turn[comp + 8 + j, comp + j] = -1.0
            turn[comp + j, comp + 8 + j] = 1.0
    put("cos", cos)
    put("sin", sin)
    put("turn", turn)
    put("head_cols", np.stack([np.arange(P) < 64, np.arange(P) >= 64], 1))
    return np.concatenate(parts, axis=1)


class Kernel:

    def __init__(self, nc, consts):
        self.nc = nc
        self.prog = p = Program(nc)
        self.PE, self.ACT, self.DVE, self.POOL, self.SP = p.pe, p.act, p.dve, p.pool, p.sp
        self.sbuf_names = 0
        self.psum = nc.alloc_psum_tensor("psum_all", [P, 8, 512], F32)
        self.banks = [Slot(p, self.psum[:, b, :]) for b in range(8)]
        self.bank_ring = Ring(p, self.banks)
        self.wslots = [Slot(p, self.sb(f"weights{n}", [P, 2048]), f"weights{n}_in") for n in range(6)]
        self.wring = Ring(p, self.wslots)
        self.consts = consts
        self.const = self.sb("const_sb", [P, 2 * P])
        self.at_hand = {"ident": self.const[:, 0:P], "ones": self.const[:, P:2 * P]}
        self.h = self.sb("h", [P, KD, T])
        self.u = self.sb("u", [P, KD, T])
        self.big = self.sb("big", [P, BIG])
        self.sq = [Slot(p, self.sb(f"sq{n}", [P, T])) for n in range(2)]
        self.rstd = self.sb("rstd", [P, T])
        self.sq_ring = Ring(p, self.sq)
        self.stat = self.sb("stat", [P, 64])
        self.big_at = 0

    def sb(self, name, shape, dt=F32):
        return self.nc.alloc_sbuf_tensor(name, shape, dt)

    def c(self, name):
        return self.at_hand[name]

    def fetch(self, *names):
        arrive = self.prog.arrivals("const")
        for name in names:
            a, n = CONST_COLS[name]
            where = self.const[:, (0 if name == "ident" else P):(P if name == "ident" else 2 * P)] \
                if name in ("ident", "ones") else self.carve(n)
            self.at_hand[name] = where
            m = self.SP.dma(arrive, where, self.consts[:, a:a + n])
        for lane in (self.PE, self.DVE, self.ACT):
            lane.wait(m)
        self.in_const = m

    def carve(self, *shape):
        n = int(np.prod(shape))
        a = self.big[:, self.big_at:self.big_at + n]
        self.big_at += n
        assert self.big_at <= BIG, self.big_at
        if len(shape) == 2:
            return a.rearrange("p (a b) -> p a b", b=shape[1])
        if len(shape) == 3:
            return a.rearrange("p (a b c) -> p a b c", b=shape[1], c=shape[2])
        return a

    def new_phase(self, keep=0, stores=()):
        self.prog.phase(stores)
        self.big_at = keep

    def bank(self, n=1):
        return self.bank_ring.take(n)

    def weights(self, view, cols, rows=KD, slot=None, lane=None):
        slot = slot or self.wring.take()
        n = view.shape[-1]
        dst = slot[:, 0:rows * n].rearrange("p (k n) -> p k n", n=n)
        m = (lane or self.SP).dma(slot, dst, view, after=slot.free)
        slot.free = []
        return slot, dst, m

    def matmuls(self, out, terms, after=()):
        for n, (lhsT, rhs) in enumerate(terms):
            last = n == len(terms) - 1
            m = self.PE.run(self.nc.tensor.matmul, out, lhsT, rhs, start=n == 0, stop=last,
                            after=after, counted=last)
            after = ()
        return m

    def project(self, w, j, src, k=KD, m_in=(), bank=None):
        b = bank or self.bank()
        m = self.matmuls(b[:, :], [(w[:, i, j * P:(j + 1) * P], src[:, i, :]) for i in range(k)],
                         after=[m_in, b.free])
        b.free = []
        return b, m

    def transposes(self, out_in, bank, after=()):
        after = [after, bank.free]
        for n, (o, i) in enumerate(out_in):
            k = i.shape[0]
            m = self.PE.run(self.nc.tensor.transpose, o, i, self.c("ident")[0:k, 0:k], after=after,
                            counted=n == len(out_in) - 1)
            after = ()
        bank.free = []
        return m

    def rms(self, chunks, width, eps, after=(), ones="ones"):
        nc = self.nc
        b = self.bank()
        n = len(chunks)
        for k, ch in enumerate(chunks):
            s = self.sq_ring.take()
            m = self.ACT.run(nc.scalar.activation, s[:, :], ch, ACT.Square, after=[after, s.free])
            m = self.PE.run(nc.tensor.matmul, b[:, :], self.c(ones), s[:, :], start=k == 0, stop=k == n - 1,
                            after=[m, b.free if k == 0 else ()])
            s.free = [m]
        m = self.DVE.run(nc.vector.tensor_scalar, self.rstd[:, :], b[:, :], 1.0 / width, eps,
                         ALU.mult, ALU.add, after=m)
        b.free = [m]
        m = self.ACT.run(nc.scalar.activation, self.rstd[:, :], self.rstd[:, :], ACT.Sqrt, after=m)
        return self.DVE.run(nc.vector.reciprocal, self.rstd[:, :], self.rstd[:, :], after=m)

    def scaled(self, out, chunks, gains, shifts=None, after=()):
        nc = self.nc
        for k, ch in enumerate(chunks):
            m = self.DVE.run(nc.vector.tensor_tensor, out[:, k, :], ch, self.rstd[:, :], ALU.mult, after=after)
            if shifts is None:
                m = self.DVE.run(nc.vector.tensor_scalar, out[:, k, :], out[:, k, :], gains[:, k:k + 1], None,
                                 ALU.mult)
            else:
                m = self.DVE.run(nc.vector.tensor_scalar, out[:, k, :], out[:, k, :], gains[:, k:k + 1],
                                 shifts[:, k:k + 1], ALU.mult, ALU.add)
        return m

    def load_columns(self, vectors):
        nc = self.nc
        self.cols = {}
        total = sum(a.shape[0] for _, a in vectors)
        tiles = -(-total // P) + 1
        self.columns = self.sb("columns", [P, tiles * P])
        rows = self.big[:, 0:tiles * P]
        m0 = self.DVE.run(nc.vector.memset, rows, 0.0)
        at = 0
        arrive = self.prog.arrivals("vectors")
        for name, a in vectors:
            n = a.shape[0]
            if at % P + n > P:
                at += P - at % P
            self.cols[name] = (at, n)
            t, r = at // P, at % P
            m = self.SP.dma(arrive, rows[r:r + n, t * P:(t + 1) * P], a, after=m0)
            at += n
        assert at <= tiles * P
        for t in range(tiles):
            b = self.bank()
            m1 = self.transposes([(b[:, 0:P], rows[:, t * P:(t + 1) * P])], b, after=[m, self.in_const])
            m1 = self.DVE.run(nc.vector.tensor_copy, self.columns[:, t * P:(t + 1) * P], b[:, 0:P], after=m1)
            b.free = [m1]
        return m1

    def col(self, name, k=None):
        a, n = self.cols[name]
        return self.columns[:, a:a + n] if k is None else self.columns[:, a + k:a + k + 1]

    def load_x(self, x):
        nc = self.nc
        for t in range(NT):
            s = self.wring.take()
            m = self.SP.dma(s, s[:, 0:D], x[t * P:(t + 1) * P, :], after=s.free)
            for half in range(2):
                b = self.bank()
                m1 = self.transposes([(b[:, j * P:(j + 1) * P], s[:, (4 * half + j) * P:(4 * half + j + 1) * P])
                                      for j in range(4)], b, after=[m, self.in_const])
                m2 = self.DVE.run(nc.vector.tensor_copy, self.h[:, 4 * half:4 * half + 4, t * P:(t + 1) * P],
                                  b[:, :].rearrange("p (a b) -> p a b", b=P), after=m1)
                b.free = [m2]
            s.free = [m1]
        return m2

    def store_h(self, out):
        nc = self.nc
        for t in range(NT):
            s = self.wring.take()
            for half in range(2):
                b = self.bank()
                m1 = self.transposes([(b[:, j * P:(j + 1) * P], self.h[:, 4 * half + j, t * P:(t + 1) * P])
                                      for j in range(4)], b, after=self.DVE.count.mark())
                m2 = self.DVE.run(nc.vector.tensor_copy, s[:, 512 * half:512 * half + 512], b[:, :],
                                  after=[m1, s.free])
                b.free = [m2]
            m = self.SP.dma(s, out[t * P:(t + 1) * P, :], s[:, 0:D], after=m2)
            s.free = [m]
        self.SP.wait([s.count.mark() for s in self.wslots if s.count.used()])
def adaln(K, w_ada):
    nc, prog = K.nc, K.prog
    K.mod = K.sb("mod", [P, 48])
    K.c_act = K.sb("c_act", [P, KD])
    acc = K.carve(2048)
    K.ACT.run(nc.scalar.activation, K.c_act[:, :], K.col("c"), ACT.Silu, after=K.DVE.count.mark())
    m_c = K.ACT.count.mark()
    view = w_ada.rearrange("(k p) n -> p k n", p=P)
    acc_slot = Slot(prog, acc)
    acc_slot.free = []
    K.DVE.wait(m_c)

    def group(g):
        for k in range(KD):
            s, w, m = K.weights(view[:, k:k + 1, ds(g * 2048, 2048)], None, rows=1)
            if k == 0:
                m = K.DVE.run(nc.vector.tensor_scalar, acc, w[:, 0, :], K.c_act[:, 0:1], None, ALU.mult,
                              after=[m, acc_slot.free])
            else:
                m = K.DVE.run(nc.vector.scalar_tensor_tensor, acc, w[:, 0, :], K.c_act[:, k:k + 1], acc,
                              ALU.mult, ALU.add, after=m)
            s.free = [m]
        b = K.bank()
        for j in range(16):
            m = K.PE.run(nc.tensor.matmul, b[:, j:j + 1], acc[:, j * P:(j + 1) * P], K.c("ones")[:, 0:1],
                         start=True, stop=True, after=[m, b.free if j == 0 else ()], counted=j == 15) or m
        acc_slot.free = [m]
        a = K.cols["b_ada"][0]
        m = K.DVE.run(nc.vector.tensor_tensor, K.mod[:, ds(g * 16, 16)], b[:, 0:16],
                      K.columns[:, ds(a + g * 16, 16)], ALU.add, after=m)
        b.free = [m]

    prog.loop(3, group)


def modulated_norm(K, gain, shift_at, scale_at, out):
    nc = K.nc
    g = K.stat[:, 0:KD]
    m = K.rms([K.h[:, k, :] for k in range(KD)], D, 1e-6, after=K.DVE.count.mark())
    K.DVE.run(nc.vector.tensor_scalar, g, K.mod[:, scale_at:scale_at + KD], 1.0, None, ALU.add)
    K.DVE.run(nc.vector.tensor_tensor, g, g, K.col(gain), ALU.mult)
    return K.scaled(out, [K.h[:, k, :] for k in range(KD)], g, K.mod[:, shift_at:shift_at + KD])


def ssd_decays(K, w_in, dt_bias, A_log, cs_dram, cd_dram):
    nc, V, S = K.nc, K.DVE, K.ACT
    H = 32
    K.headq = K.carve(4, NT, H)
    K.cdb = K.carve(NT, H)
    K.kept_ssd = K.big_at
    sc = K.carve(12, T)
    K.fetch("scan128")
    q = lambda n: sc[0:H, n, :]
    s, w, m = K.weights(w_in.rearrange("(k p) n -> p k n", p=P)[:, :, 6144:6144 + H], None)
    small = K.stat[0:H, 16:20]
    io = K.prog.arrivals("head_vectors")
    m1 = K.SP.dma(io, small[:, 0:1], dt_bias.rearrange("(h a) -> h a", a=1))
    m1 = K.SP.dma(io, small[:, 1:2], A_log.rearrange("(h a) -> h a", a=1))
    b = K.bank()
    m = K.matmuls(b[0:H, :], [(w[:, k, :], K.u[:, k, :]) for k in range(KD)], after=[m, b.free, V.count.mark()])
    s.free = [m]
    x, ax, e, z, z2, acc, dt, cs, e1, dd, tmp = (q(n) for n in range(11))
    ts, tt, stt = nc.vector.tensor_scalar, nc.vector.tensor_tensor, nc.vector.scalar_tensor_tensor
    m = V.run(ts, x, b[0:H, :], small[:, 0:1], None, ALU.add, after=[m, m1])
    b.free = [m]
    V.run(ts, tmp, x, -1.0, None, ALU.mult)
    m = V.run(tt, ax, x, tmp, ALU.min)
    m = S.run(nc.scalar.activation, e, ax, ACT.Exp, after=m)
    V.run(ts, z, e, 2.0, None, ALU.add, after=m)
    V.run(nc.vector.reciprocal, z, z)
    V.run(tt, z, z, e, ALU.mult)
    V.run(tt, z2, z, z, ALU.mult)
    V.run(ts, acc, z2, 1.0 / 17, 1.0 / 15, ALU.mult, ALU.add)
    for d in (13, 11, 9, 7, 5, 3, 1):
        V.run(tt, acc, acc, z2, ALU.mult)
        V.run(ts, acc, acc, 1.0 / d, None, ALU.add)
    V.run(tt, acc, acc, z, ALU.mult)
    V.run(ts, tmp, x, 0.0, None, ALU.max)
    m = V.run(stt, dt, acc, 2.0, tmp, ALU.mult, ALU.add)
    m = S.run(nc.scalar.activation, small[:, 2:3], small[:, 1:2], ACT.Exp, after=m)
    m = V.run(ts, small[:, 2:3], small[:, 2:3], -1.0, None, ALU.mult, after=m)
    V.run(ts, tmp, dt, small[:, 2:3], None, ALU.mult)
    m = V.run(nc.vector.tensor_tensor_scan, cs, K.c("scan128")[0:H, :], tmp, 0.0, ALU.mult, ALU.add)
    m_cs = K.SP.dma(K.prog.arrivals("cs_out"), cs_dram, cs, after=m)
    m = S.run(nc.scalar.activation, e1, cs, ACT.Exp, after=m)
    for c in range(NT):
        end = cs[:, (c + 1) * P - 1:(c + 1) * P]
        m = V.run(ts, dd[:, c * P:(c + 1) * P], cs[:, c * P:(c + 1) * P], -1.0, end, ALU.mult, ALU.add)
    m = S.run(nc.scalar.activation, dd, dd, ACT.Exp, after=m)
    m = V.run(tt, dd, dd, dt, ALU.mult, after=m)
    diag = sc[0:H, 11, 0:P].rearrange("h (c g) -> h c g", g=H)
    for c in range(NT):
        m = V.run(ts, diag[:, c, :], K.c("ident")[0:H, 0:H], e1[:, (c + 1) * P - 1:(c + 1) * P], None, ALU.mult)
    b = K.bank()
    m = K.matmuls(b[:, 0:P], [(K.c("ones")[0:H, :], sc[0:H, 11, 0:P])], after=[m, b.free])
    m = V.run(nc.vector.tensor_copy, K.cdb, b[:, 0:P].rearrange("p (c g) -> p c g", g=H), after=m)
    b.free = [m]
    b = K.bank()
    m = K.transposes([(b[:, (i * NT + c) * H:(i * NT + c + 1) * H], src[:, c * P:(c + 1) * P])
                      for i, src in enumerate((dt, cs, e1, dd)) for c in range(NT)], b, after=m)
    m = V.run(nc.vector.tensor_copy, K.headq.rearrange("p a c h -> p (a c h)"), b[:, :], after=m)
    b.free = [m]
    K.m_cs = m_cs


def ssd_groups(K, w_in, cs_dram, D_skip, y):
    nc, V, S, prog = K.nc, K.DVE, K.ACT, K.prog
    ts, tt, stt = nc.vector.tensor_scalar, nc.vector.tensor_tensor, nc.vector.scalar_tensor_tensor
    act = nc.scalar.activation
    pre = [Slot(prog, K.carve(T + 3)) for _ in range(2)]
    pre_ring = Ring(prog, pre)
    post = K.carve(4, T)
    xs_tok, xdt, xdec = K.carve(NT, 256), K.carve(NT, 256), K.carve(NT, 256)
    B_tok = K.carve(NT, P)
    CB = K.carve(NT, P)
    prev = K.carve(NT, 256)
    zs = K.carve(NT, 256)
    cs_all = Slot(prog, K.carve(4, T), "cs_all_in")
    W = K.carve(4, NT, P)
    ytok, t1 = K.carve(NT, 256), K.carve(NT, 256)
    gcol = K.carve(64)
    hq = K.carve(4 * NT, 4)
    cd = K.carve(NT, 4)
    Dsk = K.carve(32)
    Dg, ss, nss = K.carve(4), K.carve(4), K.carve(4)
    m_D = K.SP.dma(K.prog.arrivals("D_skip"), Dsk, D_skip.partition_broadcast(P))
    for p_ in pre:
        V.run(nc.vector.memset, p_[:, 0:3], 0.0)
    V.run(nc.vector.memset, prev[:, 0, :], 0.0)
    V.wait(m_D)
    wv = w_in.rearrange("(k p) n -> p k n", p=P)
    cwa, cba, nga = K.cols["conv_w"][0], K.cols["conv_b"][0], K.cols["ssd_norm_g"][0]
    cw = K.columns[:, cwa:cwa + 128].rearrange("p (i c) -> p i c", i=4)
    gw = gcol[:, 0:16].rearrange("p (i c) -> p i c", i=4)
    K.SP.wait(K.m_cs)

    def group(g):
        prog.join(V, S)
        cp = nc.vector.tensor_copy
        V.run(cp, gw[:, :, 0:2], cw[:, :, ds(2 * g, 2)])
        V.run(cp, gw[:, :, 2:3], cw[:, :, ds(16 + g, 1)])
        V.run(cp, gw[:, :, 3:4], cw[:, :, ds(24 + g, 1)])
        V.run(cp, gcol[:, 16:18], K.columns[:, ds(cba + 2 * g, 2)])
        V.run(cp, gcol[:, 18:19], K.columns[:, ds(cba + 16 + g, 1)])
        V.run(cp, gcol[:, 19:20], K.columns[:, ds(cba + 24 + g, 1)])
        V.run(cp, gcol[:, 20:22], K.columns[:, ds(nga + 2 * g, 2)])
        V.run(cp, Dg, Dsk[:, ds(4 * g, 4)])
        V.run(cp, cd, K.cdb[:, :, ds(4 * g, 4)])
        V.run(cp, hq, K.headq.rearrange("p a c h -> p (a c) h")[:, :, ds(4 * g, 4)])
        m_csb = K.SP.dma(cs_all, cs_all.t, cs_dram[ds(4 * g, 4), :].partition_broadcast(P), after=cs_all.free)
        sx, wx, mx = K.weights(wv[:, :, ds(2048 + 256 * g, 256)], None)
        sbc = K.wring.take()
        wbc = sbc[:, :].rearrange("p (a k n) -> p a k n", a=2, k=KD)
        K.SP.dma(sbc, wbc[:, 0], wv[:, :, ds(4096 + 128 * g, 128)], after=sbc.free)
        mbc = K.SP.dma(sbc, wbc[:, 1], wv[:, :, ds(5120 + 128 * g, 128)])
        sz, wz, mz = K.weights(wv[:, :, ds(256 * g, 256)], None)
        for j in range(4):
            w, i, m_w = (wx, j, mx) if j < 2 else (wbc[:, j - 2], 0, mbc)
            b, m = K.project(w, i, K.u, m_in=m_w)
            if j == 1:
                sx.free = [m]
            if j == 3:
                sbc.free = [m]
            p_ = pre_ring.take()
            m = S.run(act, p_[:, 3:3 + T], b[:, :], ACT.Copy, after=[m, p_.free])
            b.free = [m]
            m = V.run(ts, post[:, j, :], p_[:, 0:T], gw[:, 0, j:j + 1], gcol[:, 16 + j:17 + j], ALU.mult, ALU.add,
                      after=[m, post_free[0]])
            for i in range(1, 4):
                m = V.run(stt, post[:, j, :], p_[:, i:i + T], gw[:, i, j:j + 1], post[:, j, :], ALU.mult, ALU.add)
            p_.free = [m]
            m_post = S.run(act, post[:, j, :], post[:, j, :], ACT.Silu, after=m)
        zb = K.bank(2)
        for c in range(NT):
            b = zb[c // 2]
            m = K.matmuls(b[:, c % 2 * 256:c % 2 * 256 + 256],
                          [(K.u[:, k, c * P:(c + 1) * P], wz[:, k, :]) for k in range(KD)],
                          after=[mz, b.free if c % 2 == 0 else ()])
        sz.free = [m]
        for i, b in enumerate(zb):
            m = S.run(act, zs[:, 2 * i:2 * i + 2, :].rearrange("p a b -> p (a b)"), b[:, :], ACT.Silu, after=m)
            b.free = [m]
        m_z = m
        xb = K.bank(2)
        for i, b in enumerate(xb):
            m = K.transposes([(b[:, (c * 2 + j) * P:(c * 2 + j + 1) * P], post[:, j, (2 * i + c) * P:(2 * i + c + 1) * P])
                              for c in range(2) for j in range(2)], b, after=m_post)
            m = S.run(act, xs_tok[:, 2 * i:2 * i + 2, :].rearrange("p a b -> p (a b)"), b[:, :], ACT.Copy, after=m)
            b.free = [m]
        bb = K.bank()
        m1 = K.transposes([(bb[:, c * P:(c + 1) * P], post[:, 2, c * P:(c + 1) * P]) for c in range(NT)], bb)
        m1 = S.run(act, B_tok.rearrange("p a b -> p (a b)"), bb[:, :], ACT.Copy, after=m1)
        bb.free = [m1]
        xh = xs_tok.rearrange("p c (h d) -> p (c h) d", d=64)
        per_head = lambda a: hq[:, 4 * a:4 * a + 4, :].rearrange("p c h -> p (c h)").unsqueeze(2).to_broadcast([P, 16, 64])
        V.run(tt, xdt.rearrange("p c (h d) -> p (c h) d", d=64), xh, per_head(0), ALU.mult, after=m)
        m_x = V.run(tt, xdec.rearrange("p c (h d) -> p (c h) d", d=64), xh, per_head(3), ALU.mult)
        cb = K.bank()
        for c in range(NT):
            m = K.matmuls(cb[:, c * P:(c + 1) * P], [(post[:, 2, c * P:(c + 1) * P], post[:, 3, c * P:(c + 1) * P])],
                          after=cb.free if c == 0 else ())
        m = V.run(tt, CB, cb[:, :].rearrange("p (c l) -> p c l", l=P),
                  K.c("upper").unsqueeze(1).to_broadcast([P, NT, P]), ALU.mult, after=m)
        cb.free = [m]
        for r in range(4):
            V.run(tt, W[:, r], cs_all.t[:, r, :].rearrange("p (c l) -> p c l", l=P),
                  hq[:, 4:8, r].unsqueeze(2).to_broadcast([P, NT, P]), ALU.subtract, after=m_csb)
        Wf = W.rearrange("p r c l -> p (r c l)")
        m = V.run(ts, Wf, Wf, 0.0, None, ALU.min)
        cs_all.free = [m]
        m = S.run(act, Wf, Wf, ACT.Exp, after=m)
        for r in range(4):
            m = V.run(tt, W[:, r], W[:, r], CB, ALU.mult, after=m)
        m_W = m
        sbk = K.bank(2)
        for c in range(3):
            b = sbk[c // 2]
            m = K.matmuls(b[:, c % 2 * 256:c % 2 * 256 + 256], [(B_tok[:, c, :], xdec[:, c, :])],
                          after=[m1, m_x, b.free if c % 2 == 0 else ()])
        for c in range(3):
            b = sbk[c // 2]
            add = b[:, c % 2 * 256:c % 2 * 256 + 256]
            if c == 0:
                m = V.run(cp, prev[:, 1, :], add, after=[m, prev_free[0]])
            else:
                V.run(tt, prev[:, c + 1, :].rearrange("p (h d) -> p h d", d=64),
                      prev[:, c, :].rearrange("p (h d) -> p h d", d=64),
                      cd[:, c, :].unsqueeze(2).to_broadcast([P, 4, 64]), ALU.mult)
                m = V.run(tt, prev[:, c + 1, :], prev[:, c + 1, :], add, ALU.add)
            b.free = [m]
        yd, yo = K.bank(2), K.bank(2)
        for c in range(NT):
            b, o = yo[c // 2], c % 2 * 256
            m = K.matmuls(b[:, o:o + 256], [(post[:, 3, c * P:(c + 1) * P], prev[:, c, :])],
                          after=[m, b.free if c % 2 == 0 else ()])
            b = yd[c // 2]
            for r in range(4):
                m = K.matmuls(b[:, o + 64 * r:o + 64 * r + 64], [(W[:, r, c, :], xdt[:, c, 64 * r:64 * r + 64])],
                              after=[m_W, b.free if c % 2 == 0 and r == 0 else ()])
        post_free[0] = prev_free[0] = None
        for i in range(2):
            o = yo[i]
            h4 = lambda a: a.rearrange("p (x d) -> p x d", d=64)
            m2 = V.run(tt, t1[:, 2 * i:2 * i + 2, :].rearrange("p c (h d) -> p (c h) d", d=64), h4(o[:, :]),
                       hq[:, 8 + 2 * i:10 + 2 * i, :].rearrange("p c h -> p (c h)").unsqueeze(2).to_broadcast([P, 8, 64]),
                       ALU.mult, after=m)
            o.free = [m2]
            f = lambda a: a[:, 2 * i:2 * i + 2, :].rearrange("p a b -> p (a b)")
            m2 = V.run(tt, f(t1), f(t1), yd[i][:, :], ALU.add)
            yd[i].free = [m2]
        for c in range(NT):
            V.run(tt, ytok[:, c, :].rearrange("p (h d) -> p h d", d=64), xs_tok[:, c, :].rearrange("p (h d) -> p h d", d=64),
                  Dg.unsqueeze(2).to_broadcast([P, 4, 64]), ALU.mult)
        V.run(tt, ytok, ytok, t1, ALU.add)
        V.run(tt, ytok, ytok, zs, ALU.mult, after=m_z)
        V.run(tt, t1, ytok, ytok, ALU.mult)
        V.run(nc.vector.tensor_reduce, ss, t1, AX.X, ALU.add)
        m = V.run(ts, ss, ss, 1.0 / 256, 1e-6, ALU.mult, ALU.add)
        m = S.run(act, nss, ss, ACT.Sqrt, after=m)
        V.run(nc.vector.reciprocal, nss, nss, after=m)
        m = V.run(tt, ytok, ytok, nss.unsqueeze(2).to_broadcast([P, NT, 256]), ALU.mult)
        for j in range(2):
            b = K.bank()
            m = K.transposes([(b[:, c * P:(c + 1) * P], ytok[:, c, j * P:(j + 1) * P]) for c in range(NT)], b, after=m)
            m = S.run(act, y[:, ds(2 * g + j, 1), :], b[:, :].unsqueeze(1), ACT.Copy, scale=gcol[:, 20 + j:21 + j], after=m)
            b.free = [m]

    post_free, prev_free = [None], [None]
    prog.loop(8, group)


def pool_branch(K, w_in, pool_w, mixed):
    nc, V, S, prog = K.nc, K.DVE, K.ACT, K.prog
    tt, stt = nc.vector.tensor_tensor, nc.vector.scalar_tensor_tensor
    PADW = 16
    xp = [Slot(prog, K.carve(PADW + T)) for _ in range(2)]
    sums = [K.carve(PADW + T) for _ in range(2)]
    pooled = Slot(prog, K.carve(2, T))
    for a in [x.t for x in xp] + sums:
        V.run(nc.vector.memset, a[:, 0:PADW], 0.0)
    wv = w_in.rearrange("(k p) n -> p k n", p=P)
    for gi, win in enumerate((2, 4, 8, 16)):
        s, w, m_w = K.weights(wv[:, :, 6176 + 256 * gi:6176 + 256 * gi + 256], None)
        sp, wp, m_p = K.weights(pool_w[gi].rearrange("(k p) n -> p k n", p=P), None, rows=2)
        pf = pooled.free
        for j in range(2):
            b, m = K.project(w, j, K.u, m_in=m_w)
            s.free = [m]
            x = xp[j]
            m = S.run(nc.scalar.activation, x[:, PADW:], b[:, :], ACT.Copy, after=[m, x.free])
            b.free = [m]
            cur, step, n = x.t, 1, 0
            while step < win:
                nxt = sums[n % 2]
                V.run(tt, nxt[:, PADW:], cur[:, PADW:], cur[:, PADW - step:PADW - step + T], ALU.add, after=m)
                cur, step, n = nxt, 2 * step, n + 1
            other = sums[n % 2]
            V.run(tt, other[:, PADW:], cur[:, PADW:], K.c(f"inv{win}"), ALU.mult)
            m = V.run(tt, pooled[:, j, :], other[:, PADW:], x[:, PADW:], ALU.subtract, after=pf)
            x.free = [m]
        for j in range(2):
            b, m1 = K.project(wp, j, pooled.t, k=2, m_in=[m_p, m])
            sp.free = pooled.free = [m1]
            m1 = S.run(nc.scalar.activation, mixed[:, 2 * gi + j, :], b[:, :], ACT.Copy,
                      scale=K.col("pool_scale", 2 * gi + j), after=m1)
            b.free = [m1]


def combine(K, w_in, w_br_ssd, w_br_pool, w_out, y, pooled, merged):
    nc, V, S, prog = K.nc, K.DVE, K.ACT, K.prog
    tt, stt = nc.vector.tensor_tensor, nc.vector.scalar_tensor_tensor
    wv = w_in.rearrange("(k p) n -> p k n", p=P)
    wsv = w_br_ssd.rearrange("(k p) n -> p k n", p=P)
    wpv = w_br_pool.rearrange("(k p) n -> p k n", p=P)
    gate = [Slot(prog, K.carve(T)) for _ in range(2)]

    def column(j):
        ss, ws, m_s = K.weights(wsv[:, :, ds(j * P, P)], None, rows=16)
        sp, wp, m_p = K.weights(wpv[:, :, ds(j * P, P)], None)
        sg = K.wring.take()
        wg = sg[:, :].rearrange("p (a k n) -> p a k n", a=2, k=KD)
        K.SP.dma(sg, wg[:, 0], wv[:, :, ds(7200 + j * P, P)], after=sg.free)
        m_g = K.SP.dma(sg, wg[:, 1], wv[:, :, ds(8224 + j * P, P)])
        for i in range(2):
            b, m = K.project(wg[:, i], 0, K.u, m_in=m_g)
            sg.free = [m]
            m = S.run(nc.scalar.activation, gate[i][:, :], b[:, :], ACT.Sigmoid, after=[m, gate[i].free])
            b.free = [m]
        b1, m1 = K.project(ws, 0, y, k=16, m_in=m_s)
        ss.free = [m1]
        b2, m2 = K.project(wp, 0, pooled, m_in=m_p)
        sp.free = [m2]
        V.run(tt, gate[0][:, :], gate[0][:, :], b1[:, :], ALU.mult, after=[m, m1])
        b1.free = [V.count.mark()]
        V.run(tt, gate[1][:, :], gate[1][:, :], b2[:, :], ALU.mult, after=m2)
        b2.free = [V.count.mark()]
        m = V.run(tt, merged[:, ds(j, 1), :], gate[0][:, :].unsqueeze(1), gate[1][:, :].unsqueeze(1), ALU.add)
        gate[0].free = gate[1].free = [m]

    prog.loop(KD, column)
    residual_product(K, w_out, merged, 16)


def residual_product(K, w, src, gate_at):
    nc, V = K.nc, K.DVE
    wv = w.rearrange("(k p) n -> p k n", p=P)
    K.PE.wait(K.DVE.count.mark(), K.ACT.count.mark())

    def pair(j2):
        s, w_, m_w = K.weights(wv[:, :, ds(j2 * 256, 256)], None)
        for j in range(2):
            b, m = K.project(w_, j, src, m_in=m_w)
            s.free = [m]
            hj = K.h[:, ds(2 * j2 + j, 1), :]
            m = V.run(nc.vector.scalar_tensor_tensor, hj, b[:, :].unsqueeze(1), K.mod[:, ds(gate_at + 2 * j2 + j, 1)],
                      hj, ALU.mult, ALU.add, after=m)
            b.free = [m]

    K.prog.loop(KD // 2, pair)
E_ALL, TOP, F_E = 64, 8, 256


def router(K, w_router, router_bias, wt_dram):
    nc, V, S = K.nc, K.DVE, K.ACT
    ts, tt = nc.vector.tensor_scalar, nc.vector.tensor_tensor
    G = 8
    score, choice, masked, rep = (K.carve(NT, E_ALL) for _ in range(4))
    top = K.carve(NT * G, 8)
    gs, gm, pen = K.carve(NT, G), K.carve(NT, G), K.carve(NT, G)
    cmp1, cmp2 = K.carve(NT, G, G), K.carve(NT, G, G)
    bias, total = K.carve(E_ALL), K.carve(NT)
    wT = K.carve(T)
    K.fetch("before8")
    m_b = K.SP.dma(K.prog.arrivals("router_bias"), bias, router_bias.partition_broadcast(P))
    s, w, m = K.weights(w_router.rearrange("(k p) n -> p k n", p=P), None)
    b = K.bank()
    for t in range(NT):
        m = K.matmuls(b[:, t * E_ALL:(t + 1) * E_ALL], [(K.u[:, k, t * P:(t + 1) * P], w[:, k, :]) for k in range(KD)],
                      after=[m, V.count.mark(), b.free if t == 0 else ()])
    s.free = [m]
    merge = lambda a: a.rearrange("p a b -> p (a b)")
    m = S.run(nc.scalar.activation, merge(score), b[:, 0:NT * E_ALL], ACT.Sigmoid, after=m)
    b.free = [m]
    V.run(tt, choice, score, bias.unsqueeze(1).to_broadcast([P, NT, E_ALL]), ALU.add, after=[m, m_b])
    for t in range(NT):
        for g in range(G):
            V.run(nc.vector.max, top[:, t * G + g, :], choice[:, t, g * 8:(g + 1) * 8])
    V.run(tt, merge(gs), top[:, :, 0], top[:, :, 1], ALU.add)
    other = gs.unsqueeze(2).to_broadcast([P, NT, G, G])
    this = gs.unsqueeze(3).to_broadcast([P, NT, G, G])
    for t in range(NT):
        V.run(tt, cmp1[:, t], other[:, t], this[:, t], ALU.is_gt)
        V.run(tt, cmp2[:, t], other[:, t], this[:, t], ALU.is_equal)
        V.run(tt, cmp2[:, t], cmp2[:, t], K.c("before8").rearrange("p (j i) -> p j i", i=G), ALU.mult)
    V.run(tt, cmp1, cmp1, cmp2, ALU.add)
    V.run(nc.vector.tensor_reduce, gs, cmp1, AX.X, ALU.add)
    V.run(ts, gm, gs, 4.0, None, ALU.is_lt)
    V.run(ts, pen, gm, 1.0, 1e30, ALU.subtract, ALU.mult)
    e8 = lambda a: a.rearrange("p t (g e) -> p (t g) e", e=8)
    wide = lambda a: merge(a).unsqueeze(2).to_broadcast([P, NT * G, 8])
    V.run(tt, e8(masked), e8(choice), wide(gm), ALU.mult)
    V.run(tt, e8(masked), e8(masked), wide(pen), ALU.add)
    for t in range(NT):
        V.run(nc.vector.max, top[:, t, :], masked[:, t, :])
        V.run(nc.vector.match_replace, rep[:, t, :], top[:, t, :], masked[:, t, :], -3e30)
    V.run(tt, rep, rep, masked, ALU.not_equal)
    V.run(tt, score, score, rep, ALU.mult)
    V.run(nc.vector.tensor_reduce, total, score, AX.X, ALU.add)
    V.run(nc.vector.reciprocal, total, total)
    V.run(ts, total, total, ROUTED_SCALE, None, ALU.mult)
    m = V.run(tt, score, score, total.unsqueeze(2).to_broadcast([P, NT, E_ALL]), ALU.mult)
    b = K.bank()
    m = K.transposes([(b[0:E_ALL, t * P:(t + 1) * P], score[:, t, :]) for t in range(NT)], b, after=m)
    m = V.run(nc.vector.tensor_copy, wT[0:E_ALL, :], b[0:E_ALL, :], after=m)
    b.free = [m]
    return K.SP.dma(K.prog.arrivals("wt_out"), wt_dram, wT[0:E_ALL, :], after=m)


def swiglu(K, gate, m_g, up, m_u, hid, act, extra=None, after=()):
    nc, V, S = K.nc, K.DVE, K.ACT
    for j in range(2):
        bg, m = K.project(gate, j, K.u, m_in=m_g)
        bu, m1 = K.project(up, j, K.u, m_in=m_u)
        a = act.take()
        m = S.run(nc.scalar.activation, a[:, :], bg[:, :], ACT.Silu, after=[m, a.free])
        bg.free = [m]
        m = V.run(nc.vector.tensor_tensor, hid[:, j, :], a[:, :], bu[:, :], ALU.mult, after=[m, m1, hid.free, after])
        bu.free = a.free = [m]
        if extra is not None:
            m = V.run(nc.vector.tensor_tensor, hid[:, j, :], hid[:, j, :], extra, ALU.mult)
    return m, m1


def experts(K, A, wt_dram, m_wt, total):
    nc, V, S, prog = K.nc, K.DVE, K.ACT, K.prog
    hid = [Slot(prog, K.carve(2, T)) for _ in range(2)]
    act = Ring(prog, [Slot(prog, K.carve(T)) for _ in range(2)])
    wt = [Slot(prog, K.carve(T), f"wt{n}_in") for n in range(2)]
    K.SP.wait(m_wt)

    def expert(h, wg, wu, wd, extra, first):
        sg, g, mg = K.weights(wg.rearrange("(k p) n -> p k n", p=P), None)
        su, u, mu = K.weights(wu.rearrange("(k p) n -> p k n", p=P), None)
        sd, d, md = K.weights(wd.rearrange("(k p) n -> p k n", p=P), None, rows=2)
        m, m_pe = swiglu(K, g, mg, u, mu, h, act, *extra)
        sg.free = su.free = [m_pe]
        for j in range(KD):
            b, m1 = K.project(d, j, h.t, k=2, m_in=[m, md])
            sd.free = h.free = [m1]
            if first:
                m2 = V.run(nc.vector.tensor_copy, total[:, j, :], b[:, :], after=m1)
            else:
                m2 = V.run(nc.vector.tensor_tensor, total[:, j, :], total[:, j, :], b[:, :], ALU.add, after=m1)
            b.free = [m2]
        return m

    expert(hid[0], A["ws_gate"][0], A["ws_up"][0], A["ws_down"][0], (), True)
    wg, wu, wd = (A[n][0].rearrange("e k n -> (e k) n") for n in ("we_gate", "we_up", "we_down"))

    def two(i):
        for n in range(2):
            e = 2 * i + n
            w = wt[n]
            m_w = K.SP.dma(w, w.t, wt_dram[ds(e, 1), :].partition_broadcast(P), after=w.free)
            m = expert(hid[n], wg[ds(e * D, D), :], wu[ds(e * D, D), :], wd[ds(e * F_E, F_E), :], (w.t, m_w), False)
            w.free = [m]

    prog.loop(E_ALL // 2, two)


def moe(K, A):
    nc, V = K.nc, K.DVE
    modulated_norm(K, "norm_ffn_g", 24, 32, K.u)
    K.new_phase()
    total = K.carve(KD, T)
    m_wt = router(K, A["w_router"][0], A["router_bias"][0], K.wt_dram)
    K.new_phase(KD * T, m_wt)
    experts(K, A, K.wt_dram, m_wt, total)
    for j in range(KD):
        V.run(nc.vector.scalar_tensor_tensor, K.h[:, j, :], total[:, j, :], K.mod[:, 40 + j:41 + j], K.h[:, j, :],
              ALU.mult, ALU.add)
    K.new_phase()
    K.rms([K.h[:, k, :] for k in range(KD)], D, 1e-6, after=V.count.mark())
    K.scaled(K.h, [K.h[:, k, :] for k in range(KD)], K.col("final_norm_g"))
    K.new_phase()
HEAD = 64
R_, K_, V_, G_, W_, A_ = range(6)


def rwkv_inputs(K, A, scratch):
    nc, V, S, prog = K.nc, K.DVE, K.ACT, K.prog
    m = K.rms([K.h[:, k, :] for k in range(KD)], D, 1e-6, after=V.count.mark())
    K.scaled(K.u, [K.h[:, k, :] for k in range(KD)], K.columns[:, K.cols["norm_pre"][0]:K.cols["norm_pre"][0] + KD])
    dx = K.carve(KD, T)
    V.run(nc.vector.tensor_tensor, dx[:, :, 1:T], K.u[:, :, 0:T - 1], K.u[:, :, 1:T], ALU.subtract)
    V.run(nc.vector.tensor_scalar, dx[:, :, 0:1], K.u[:, :, 0:1], -1.0, None, ALU.mult)
    mix = [Slot(prog, K.carve(KD, T)) for _ in range(2)]
    out = Ring(prog, [Slot(prog, K.carve(T), f"rwkv_out{n}") for n in range(4)])
    small = Slot(prog, K.carve(T))
    mu = K.cols["a_mu"][0]

    def mixed(slot, c):
        for k in range(KD):
            m = V.run(nc.vector.scalar_tensor_tensor, slot[:, k, :], dx[:, k, :], K.columns[:, ds(mu + c * KD + k, 1)],
                      K.u[:, k, :], ALU.mult, ALU.add, after=slot.free)
        return m

    def two(i):
        for n in range(2):
            c, x = 2 * i + n, mix[n]
            m_x = mixed(x, c)
            wv = A["a_w_in_2"][0].rearrange("c k n -> (c k) n")[ds(c * D, D), :].rearrange("(k p) n -> p k n", p=P)
            for q in range(4):
                s, w, m_w = K.weights(wv[:, :, q * 256:(q + 1) * 256], None)
                for j in range(2):
                    b, m = K.project(w, j, x.t, m_in=[m_w, m_x])
                    s.free = x.free = [m]
                    o = out.take()
                    m = S.run(nc.scalar.activation, o[:, :], b[:, :], ACT.Copy, after=[m, o.free])
                    b.free = [m]
                    o.free = [K.SP.dma(o, scratch[2 * q + j].rearrange("p w t -> w p t")[ds(c, 1)]
                                       .rearrange("w p t -> (w p) t"), o.t, after=m)]

    prog.loop(2, two)
    for which, w1, w2, bias, func in ((W_, "a_w1_2", "a_w2_2", "w0", ACT.Tanh), (A_, "a_a1_2", "a_a2_2", "a0", ACT.Copy)):
        x = mix[which % 2]
        m_x = mixed(x, which)
        s, w, m_w = K.weights(A[w1][0].rearrange("(k p) n -> p k n", p=P), None)
        b = K.bank()
        m = K.matmuls(b[0:HEAD, :], [(w[:, k, :], x[:, k, :]) for k in range(KD)], after=[m_w, m_x, b.free])
        s.free = x.free = [m]
        m_s = S.run(nc.scalar.activation, small[0:HEAD, :], b[0:HEAD, :], func, after=[m, small.free])
        b.free = [m_s]
        s = K.wring.take()
        m_w = K.SP.dma(s, s[0:HEAD, 0:D], A[w2][0], after=s.free)
        for j in range(KD):
            b = K.bank()
            m = K.matmuls(b[:, :], [(s[0:HEAD, j * P:(j + 1) * P], small[0:HEAD, :])], after=[m_w, m_s, b.free])
            s.free = small.free = [m]
            o = out.take()
            m = S.run(nc.scalar.activation, o[:, :], b[:, :], ACT.Sigmoid, bias=K.col(bias, j), after=[m, o.free])
            b.free = [m]
            o.free = [K.SP.dma(o, scratch[j, :, which, :], o.t, after=m)]
    return [o.count.mark() for o in out.slots]


def rwkv_pairs(K, scratch, y_out):
    nc, V, S, prog = K.nc, K.DVE, K.ACT, K.prog
    ts, tt, stt = nc.vector.tensor_scalar, nc.vector.tensor_tensor, nc.vector.scalar_tensor_tensor
    act, cp = nc.scalar.activation, nc.vector.tensor_copy
    K.fetch("same_head", "neg_up16", "neg_low16", "neg_off16", "neg_off32", "up64", "upeq64", "scan64", "head_cols")
    ins = Ring(prog, [Slot(prog, K.carve(6, T), f"pair{n}_in") for n in range(2)])
    names = "L Em Ep En kk k2 al0 al1 be ka rh rh0 rh1 rkr vt kat bet al0t al1t TaT X2 Wv nU yt yf dv lw gs"
    buf = {n: K.carve(T) for n in names.split()}
    St, SP_, St2 = K.carve(P), K.carve(P), K.carve(P)
    pcol = K.carve(16)
    spare = [K.wslots[n][:, T * q:T * (q + 1)] for n in range(6) for q in range(4)]
    mats = {}
    for h in range(2):
        for n in "M MT N NT X O16 O32 ak qb qk G".split():
            mats[n, h] = spare.pop()
    tile = lambda a, t: a[:, t * P:(t + 1) * P]
    tiles = lambda a: a.rearrange("p (t n) -> p t n", n=P)
    wide = lambda name: K.c(name).unsqueeze(1).to_broadcast([P, NT, P])
    col = lambda name, p: K.columns[:, ds(K.cols[name][0] + p, 1)]
    B = buf

    def mm_tiles(pairs, after):
        b = K.bank()
        for t in range(NT):
            m = K.PE.run(nc.tensor.matmul, b[:, t * P:(t + 1) * P], tile(pairs[0], t), tile(pairs[1], t), start=True,
                         stop=True, after=[after, b.free] if t == 0 else (), counted=t == NT - 1)
        b.free = []
        return b, m

    def body(i):
        for n in range(2):
            pair(2 * i + n)

    def pair(p):
        prog.join(V, S)
        x = ins.take()
        m_in = K.SP.dma(x, x.t.rearrange("p w t -> p (w t)"), scratch.rearrange("c p w t -> (c p) (w t)")[ds(p * P, P), :],
                        after=x.free)
        r, k, v, g, sg, a = (x[:, n, :] for n in range(6))
        for n, name in enumerate(("k_k", "k_a", "r_k", "lnx_g", "lnx_b")):
            V.run(cp, pcol[:, n:n + 1], col(name, p))
        V.run(ts, pcol[:, 5:6], pcol[:, 1:2], -1.0, 1.0, ALU.mult, ALU.add)
        V.run(ts, B["lw"], sg, -float(np.exp(-0.5)), None, ALU.mult, after=m_in)
        m = V.run(nc.vector.tensor_tensor_scan, B["L"], K.c("scan64"), B["lw"], 0.0, ALU.mult, ALU.add)
        m1 = V.run(tt, B["Em"], B["L"], B["lw"], ALU.subtract)
        S.run(act, B["Ep"], B["L"], ACT.Exp, after=m)
        S.run(act, B["En"], B["L"], ACT.Exp, scale=-1.0)
        m_e = S.run(act, B["Em"], B["Em"], ACT.Exp, after=m1)
        m = V.run(ts, B["kk"], k, pcol[:, 0:1], None, ALU.mult)
        m = V.run(tt, B["dv"], B["kk"], B["kk"], ALU.mult)
        b = K.bank()
        m = K.matmuls(b[:, :], [(K.c("same_head"), B["dv"])], after=[m, b.free])
        m = S.run(act, B["gs"], b[:, :], ACT.Sqrt, after=m)
        b.free = [m]
        V.run(ts, B["gs"], B["gs"], 1e-12, None, ALU.max, after=m)
        V.run(nc.vector.reciprocal, B["gs"], B["gs"])
        V.run(tt, B["kk"], B["kk"], B["gs"], ALU.mult)
        V.run(ts, B["k2"], a, pcol[:, 1:2], pcol[:, 5:6], ALU.mult, ALU.add)
        V.run(tt, B["k2"], B["k2"], k, ALU.mult)
        V.run(tt, B["be"], B["kk"], a, ALU.mult, after=m_e)
        V.run(tt, B["be"], B["be"], B["En"], ALU.mult)
        V.run(tt, B["ka"], B["k2"], B["En"], ALU.mult)
        V.run(tt, B["rh"], r, B["Ep"], ALU.mult)
        for h in range(2):
            hc = K.c("head_cols")[:, h:h + 1]
            V.run(stt, B[f"al{h}"], B["kk"], hc, B["Em"], ALU.mult, ALU.mult)
            V.run(ts, B[f"rh{h}"], B["rh"], hc, None, ALU.mult)
        m = V.run(stt, B["rkr"], r, pcol[:, 2:3], B["k2"], ALU.mult, ALU.mult)
        b = K.bank()
        m1 = K.matmuls(b[:, :], [(K.c("same_head"), B["rkr"])], after=[m, b.free])
        m1 = V.run(tt, B["rkr"], b[:, :], v, ALU.mult, after=m1)
        b.free = [m1]
        for src, dst in ((v, "vt"), (B["ka"], "kat"), (B["be"], "bet"), (B["al0"], "al0t"), (B["al1"], "al1t")):
            b = K.bank()
            m1 = K.transposes([(b[:, t * P:(t + 1) * P], tile(src, t)) for t in range(NT)], b, after=m)
            m_t = S.run(act, B[dst], b[:, :], ACT.Copy, after=m1)
            b.free = [m_t]
        for h in range(2):
            al, rh = B[f"al{h}"], B[f"rh{h}"]
            for lhs, rhs, outs in ((B["be"], al, [("M", "neg_up16")]),
                                   (al, B["be"], [("MT", "neg_low16"), ("O16", "neg_off16"), ("O32", "neg_off32")]),
                                   (B["ka"], al, [("ak", "up64")]),
                                   (B["be"], rh, [("qb", "upeq64")]), (B["ka"], rh, [("qk", "upeq64")])):
                b, m1 = mm_tiles((lhs, rhs), m)
                for n, mask in outs:
                    m2 = V.run(tt, tiles(mats[n, h]), tiles(b[:, :]), wide(mask), ALU.mult, after=m1)
                b.free = [m2]
            m_A = V.run(tt, tiles(mats["X", h]), tiles(mats["M", h]), wide("ident"), ALU.add)

        def copy_out(dst, pairs, after):
            b, m1 = mm_tiles(pairs, after)
            m2 = S.run(act, dst, b[:, :], ACT.Copy, after=m1)
            b.free = [m2]
            return m2

        def add_to_X(h, pairs, after):
            b, m1 = mm_tiles(pairs, after)
            m2 = V.run(tt, mats["X", h], mats["X", h], b[:, :], ALU.add, after=m1)
            b.free = [m2]
            return m2

        m_sq, m_X = [m_A, m_A], [m_A, m_A]
        for step in range(3):
            src, dst = (("M", "MT"), ("N", "NT")) if step % 2 == 0 else (("N", "NT"), ("M", "MT"))
            for h in range(2):
                M, MT = mats[src[0], h], mats[src[1], h]
                if step < 2:
                    copy_out(mats[dst[0], h], (MT, M), [m_sq[h], m_X[h]])
                m_sq[h] = copy_out(mats[dst[1], h], (M, MT), [m_sq[h], m_X[h]])
            for h in range(2):
                m_X[h] = add_to_X(h, (mats[dst[1], h], mats["X", h]), [m_sq[h], m_X[h]])
        for off in ("O16", "O32"):
            m_G = [None, None]
            for h in range(2):
                b = K.bank()
                m1 = K.transposes([(b[:, t * P:(t + 1) * P], tile(mats["X", h], t)) for t in range(NT)], b, after=m_X[h])
                m1 = S.run(act, mats["N", h], b[:, :], ACT.Copy, after=m1)
                b.free = [m1]
                m_G[h] = copy_out(mats["G", h], (mats[off, h], mats["X", h]), m_X[h])
            for h in range(2):
                m_X[h] = add_to_X(h, (mats["N", h], mats["G", h]), m_G[h])
        hs = lambda arr, t, h: arr[:, t * P + h * HEAD:t * P + (h + 1) * HEAD]

        def by_head(dst, mat, rhs, after, engine):
            b = K.bank()
            for t in range(NT):
                for h in range(2):
                    m1 = K.PE.run(nc.tensor.matmul, hs(b, t, h), tile(mats[mat, h], t), hs(rhs, t, h), start=True,
                                  stop=True, after=[after, b.free] if t + h == 0 else (), counted=t == NT - 1 and h == 1)
            m2 = S.run(act, dst, b[:, :], ACT.Copy, after=m1)
            b.free = [m2]
            return m2

        m1 = by_head(B["X2"], "ak", B["vt"], [m_t, m_A], S)
        m_W = by_head(B["Wv"], "X", B["X2"], [m1, m_X], S)
        b = K.bank()
        for t in range(NT):
            m1 = K.matmuls(b[:, t * P:(t + 1) * P], [(tile(B[f"al{h}t"], t), tile(mats["X", h], t)) for h in range(2)],
                           after=[m_t, m_X, b.free if t == 0 else ()])
        m1 = S.run(act, B["TaT"], b[:, :], ACT.Copy, after=m1)
        b.free = [m1]
        m_S = V.run(nc.vector.memset, St, 0.0)
        for c in range(T // HEAD):
            t, q = c // 2, c % 2
            rows = slice(HEAD * q, HEAD * q + HEAD)
            b = K.bank()
            K.PE.run(nc.tensor.matmul, b[:, 0:P], tile(B["TaT"], t), St, start=True, stop=True,
                     after=[m1, m_S, b.free], counted=False)
            m2 = K.PE.run(nc.tensor.matmul, b[:, P:2 * P], tile(B["rh"], t), St, start=True, stop=True)
            m_U = V.run(stt, tile(B["nU"], t)[rows], b[rows, 0:P], -1.0, tile(B["Wv"], t)[rows], ALU.mult, ALU.subtract,
                        after=[m2, m_W])
            m3 = V.run(cp, tile(B["yt"], t)[rows], b[rows, P:2 * P])
            b.free = [m3]
            if c == T // HEAD - 1:
                break
            end = B["Ep"][:, HEAD * c + HEAD - 1:HEAD * c + HEAD]
            V.run(ts, SP_, St, end, None, ALU.mult)
            b = K.bank()
            m2 = K.matmuls(b[:, 0:P], [(tile(B["bet"], t)[rows], tile(B["nU"], t)[rows]),
                                       (tile(B["kat"], t)[rows], tile(B["vt"], t)[rows])], after=[m_U, b.free])
            m3 = V.run(stt, St2, b[:, 0:P], end, K.c("same_head"), ALU.mult, ALU.mult, after=m2)
            b.free = [m3]
            m_S = V.run(tt, St, St2, SP_, ALU.add)
        b = K.bank()
        for t in range(NT):
            for h in range(2):
                m2 = K.matmuls(hs(b, t, h), [(tile(mats["qb", h], t), hs(B["nU"], t, h)),
                                             (tile(mats["qk", h], t), hs(B["vt"], t, h))],
                               after=[m_U, b.free if t + h == 0 else ()])
        m2 = V.run(tt, B["yt"], B["yt"], b[:, :], ALU.add, after=m2)
        b.free = [m2]
        b = K.bank()
        m2 = K.transposes([(b[:, t * P:(t + 1) * P], tile(B["yt"], t)) for t in range(NT)], b, after=m2)
        m2 = V.run(cp, B["yf"], b[:, :], after=m2)
        b.free = [m2]
        b = K.bank()
        m2 = K.matmuls(b[:, :], [(K.c("same_head"), B["yf"])], after=[m2, b.free])
        m2 = V.run(stt, B["dv"], b[:, :], -1.0 / HEAD, B["yf"], ALU.mult, ALU.add, after=m2)
        b.free = [m2]
        m2 = S.run(act, B["yf"], B["dv"], ACT.Square, after=m2)
        b = K.bank()
        m2 = K.matmuls(b[:, :], [(K.c("same_head"), B["yf"])], after=[m2, b.free])
        m2 = V.run(ts, B["gs"], b[:, :], 1.0 / HEAD, 64e-5, ALU.mult, ALU.add, after=m2)
        b.free = [m2]
        m2 = S.run(act, B["gs"], B["gs"], ACT.Sqrt, after=m2)
        m3 = S.run(act, B["yf"], g, ACT.Silu)
        V.run(nc.vector.reciprocal, B["gs"], B["gs"], after=m2)
        V.run(tt, B["dv"], B["dv"], B["gs"], ALU.mult)
        V.run(ts, B["dv"], B["dv"], pcol[:, 3:4], pcol[:, 4:5], ALU.mult, ALU.add)
        V.run(tt, B["dv"], B["dv"], B["rkr"], ALU.add)
        m2 = V.run(tt, y_out[:, ds(p, 1), :], B["dv"].unsqueeze(1), B["yf"].unsqueeze(1), ALU.mult, after=m3)
        x.free = [m2]

    prog.loop(KD // 2, body)


def columns_of(K, name, n):
    a = K.cols[name][0] + n * KD
    return K.columns[:, a:a + KD]


def post_and_ple(K, A, n, w_out, src):
    nc, V, S, prog = K.nc, K.DVE, K.ACT, K.prog
    stt, tt = nc.vector.scalar_tensor_tensor, nc.vector.tensor_tensor
    out = K.carve(KD, T)
    pT = K.carve(2, T)
    sig = Ring(prog, [Slot(prog, K.carve(T)) for _ in range(2)])
    p_in = A["p_2"][n, 0]
    s = K.wring.take()
    m = K.SP.dma(s, s[:, 0:4 * 256].rearrange("p (t d) -> p t d", d=256), p_in.rearrange("(t p) d -> p t d", p=P),
                 after=s.free)
    for j in range(2):
        b = K.bank()
        m1 = K.transposes([(b[:, t * P:(t + 1) * P], s[:, t * 256 + j * P:t * 256 + (j + 1) * P]) for t in range(NT)], b,
                          after=m)
        m1 = V.run(nc.vector.tensor_copy, pT[:, j, :], b[:, :], after=m1)
        b.free = [m1]
    s.free = [m1]
    wv = w_out.rearrange("(k p) n -> p k n", p=P)

    def add_normed(gains):
        K.rms([out[:, k, :] for k in range(KD)], D, 1e-6, after=[V.count.mark(), S.count.mark()])
        for k in range(KD):
            V.run(tt, out[:, k, :], out[:, k, :], K.rstd[:, :], ALU.mult)
            V.run(stt, K.h[:, k, :], out[:, k, :], gains[:, k:k + 1], K.h[:, k, :], ALU.mult, ALU.add)

    prog.phase()

    def columns(i):
        s, w, m_w = K.weights(wv[:, :, ds(i * 256, 256)], None)
        for j in range(2):
            b, m = K.project(w, j, src, m_in=m_w)
            s.free = [m]
            m = S.run(nc.scalar.activation, out[:, ds(2 * i + j, 1), :], b[:, :].unsqueeze(1), ACT.Copy, after=m)
            b.free = [m]

    prog.loop(KD // 2, columns)
    add_normed(columns_of(K, "norm_post", n))
    prog.phase()
    pgv = A["ple_gate_2"][n].rearrange("(k p) n -> p k n", p=P)
    pwv = A["ple_w_2"][n].rearrange("(k p) n -> p k n", p=P)

    def ple(i):
        s, w, m_w = K.weights(pgv[:, :, ds(i * 256, 256)], None)
        s2, w2, m_w2 = K.weights(pwv[:, :, ds(i * 256, 256)], None, rows=2)
        for j in range(2):
            b, m = K.project(w, j, K.h, m_in=m_w)
            b2, m2 = K.project(w2, j, pT, k=2, m_in=m_w2)
            s.free, s2.free = [m], [m2]
            a = sig.take()
            m = S.run(nc.scalar.activation, a[:, :], b[:, :], ACT.Sigmoid, after=[m, a.free])
            b.free = [m]
            m = V.run(tt, out[:, ds(2 * i + j, 1), :], a[:, :].unsqueeze(1), b2[:, :].unsqueeze(1), ALU.mult, after=[m, m2])
            b2.free = a.free = [m]

    prog.loop(KD // 2, ple)
    add_normed(columns_of(K, "ple_norm", n))
    K.new_phase()


LAM_INIT = 0.8 - 0.6 * float(np.exp(-0.3))


def attention(K, A, o_out):
    nc, V, S, prog = K.nc, K.DVE, K.ACT, K.prog
    ts, tt, stt = nc.vector.tensor_scalar, nc.vector.tensor_tensor, nc.vector.scalar_tensor_tensor
    act, cp = nc.scalar.activation, nc.vector.tensor_copy
    K.fetch("cos", "sin", "turn", "future")
    hk = K.carve(KD, T)
    chunks = [K.h[:, k, :] for k in range(KD)]
    K.rms(chunks, D, 1e-6, after=V.count.mark())
    K.scaled(K.u, chunks, columns_of(K, "norm_pre", 1))
    K.scaled(hk, chunks, columns_of(K, "kv_norm", 0))
    lq = K.carve(4, HEAD)
    lam = K.carve(8)
    m = K.SP.dma(prog.arrivals("lambda"), lq.rearrange("p a d -> p (a d)"),
                 A["b_lambda_2"][0].rearrange("a d -> (a d)").partition_broadcast(P))
    V.run(tt, lq[:, 0:2, :], lq[:, 0:4:2, :], lq[:, 1:4:2, :], ALU.mult, after=m)
    m = V.run(nc.vector.tensor_reduce, lam[:, 0:2], lq[:, 0:2, :], AX.X, ALU.add)
    m = S.run(act, lam[:, 0:2], lam[:, 0:2], ACT.Exp, after=m)
    V.run(tt, lam[:, 2:3], lam[:, 1:2], lam[:, 0:1], ALU.subtract, after=m)
    V.run(ts, lam[:, 2:3], lam[:, 2:3], LAM_INIT, None, ALU.subtract)
    V.run(ts, lam[:, 3:4], K.col("subln"), 1.0 - LAM_INIT, None, ALU.mult)
    q, k, qr = K.carve(T), K.carve(T), K.carve(T)
    vtok, gate, of = K.carve(T), K.carve(T), K.carve(T)
    probs = [Slot(prog, K.carve(T)) for _ in range(4)]
    pT = [Slot(prog, K.carve(T)) for _ in range(2)]
    st = K.carve(4, 2, 4)
    prog.phase()
    qv = A["b_w_in_2"][0].rearrange("(k p) n -> p k n", p=P)
    kv = A["kv_w_2"].rearrange("(k p) n -> p k n", p=P)

    def head(h):
        prog.join(V, S)
        slots = [K.wring.take(), K.wring.take()]
        w, m_w = [], []
        for s, v in zip(slots, (qv, kv)):
            w.append(s[:, :].rearrange("p (a k n) -> p a k n", a=2, k=KD))
            K.SP.dma(s, w[-1][:, 0], v[:, :, ds(h * P, P)], after=s.free)
            m_w.append(K.SP.dma(s, w[-1][:, 1], v[:, :, ds(D + h * P, P)]))
        for dst, wi, src, scale in ((q, w[0], K.u, HEAD ** -0.5), (k, w[1], hk, 1.0)):
            b, m = K.project(wi[:, 0], 0, src, m_in=m_w)
            m = S.run(act, dst, b[:, :], ACT.Copy, scale=scale, after=m)
            b.free = [m]
            b = K.bank()
            m = K.matmuls(b[:, :], [(K.c("turn"), dst)], after=[m, b.free])
            V.run(tt, qr, b[:, :], K.c("sin"), ALU.mult, after=m)
            b.free = [V.count.mark()]
            V.run(tt, dst, dst, K.c("cos"), ALU.mult)
            m_qk = V.run(tt, dst, dst, qr, ALU.add)
        b, m = K.project(w[0][:, 1], 0, K.u)
        slots[0].free = [m]
        m_g = S.run(act, gate, b[:, :], ACT.Silu, after=m)
        b.free = [m_g]
        b = K.bank()
        for t in range(NT):
            m = K.matmuls(b[:, t * P:(t + 1) * P], [(hk[:, i, t * P:(t + 1) * P], w[1][:, 1, i, :]) for i in range(KD)],
                          after=b.free if t == 0 else ())
        slots[1].free = [m]
        m_v = S.run(act, vtok, b[:, :], ACT.Copy, after=m)
        b.free = [m_v]
        ob = K.bank()
        for qb in range(NT):
            n = (qb + 1) * P
            pr = probs[2 * (qb % 2):2 * (qb % 2) + 2]
            for c in range(2):
                rows = slice(HEAD * c, HEAD * c + HEAD)
                b = K.bank()
                if b is ob:
                    b = K.bank()
                m = K.matmuls(b[:, 0:n], [(q[rows, qb * P:n], k[rows, 0:n])], after=[m_qk, b.free])
                m = V.run(tt, b[:, qb * P:n], b[:, qb * P:n], K.c("future"), ALU.add, after=m)
                m = V.run(nc.vector.tensor_reduce, st[:, qb, c, 0:1], b[:, 0:n], AX.X, ALU.max, negate=True)
                m = S.run(act, pr[c][:, 0:n], b[:, 0:n], ACT.Exp, bias=st[:, qb, c, 0:1], accum_out=st[:, qb, c, 1:2],
                          after=[m, pr[c].free])
                b.free = [m]
            V.run(nc.vector.reciprocal, st[:, qb, :, 2:3], st[:, qb, :, 1:2], after=m)
            V.run(tt, st[:, qb, 1, 3:4], st[:, qb, 1, 2:3], lam[:, 2:3], ALU.mult)
            V.run(ts, pr[0][:, 0:n], pr[0][:, 0:n], st[:, qb, 0, 2:3], None, ALU.mult)
            m = V.run(stt, pr[0][:, 0:n], pr[1][:, 0:n], st[:, qb, 1, 3:4], pr[0][:, 0:n], ALU.mult, ALU.add)
            b = K.bank()
            if b is ob:
                b = K.bank()
            m = K.transposes([(b[:, kb * P:(kb + 1) * P], pr[0][:, kb * P:(kb + 1) * P]) for kb in range(qb + 1)], b,
                             after=m)
            pr[0].free = pr[1].free = [m]
            pt = pT[qb % 2]
            m = S.run(act, pt[:, 0:n], b[:, 0:n], ACT.Copy, after=[m, pt.free])
            b.free = [m]
            m = K.matmuls(ob[:, qb * P:n], [(vtok[:, kb * P:(kb + 1) * P], pt[:, kb * P:(kb + 1) * P])
                                            for kb in range(qb + 1)], after=[m, m_v, ob.free if qb == 0 else ()])
            pt.free = [m]
        m = V.run(cp, of, ob[:, :], after=m)
        ob.free = [m]
        m = S.run(act, qr, of, ACT.Square, after=m)
        b = K.bank()
        m = K.matmuls(b[:, :], [(K.c("ones"), qr)], after=[m, b.free])
        m = V.run(ts, qr, b[:, :], 1.0 / P, 1e-5, ALU.mult, ALU.add, after=m)
        b.free = [m]
        m = S.run(act, qr, qr, ACT.Sqrt, after=m)
        V.run(nc.vector.reciprocal, qr, qr, after=m)
        V.run(tt, of, of, qr, ALU.mult)
        V.run(stt, o_out[:, ds(h, 1), :], of.unsqueeze(1), lam[:, 3:4], gate.unsqueeze(1), ALU.mult, ALU.mult, after=m_g)

    prog.loop(KD, head)
    K.prog.phase()


def block2(K, A, scratch):
    K.new_phase(0, rwkv_inputs(K, A, scratch))
    rwkv_pairs(K, scratch, K.u)
    K.new_phase()
    post_and_ple(K, A, 0, A["a_w_out_2"][0], K.u)
    o_out = K.carve(KD, T)
    attention(K, A, o_out)
    K.big_at = KD * T
    post_and_ple(K, A, 1, A["b_w_out_2"][0], o_out)
def block1_mixer(K, A):
    r = lambda a: a.rearrange("(k p) -> k p", p=P)
    adaln(K, A["w_ada"][0])
    K.new_phase()
    modulated_norm(K, "norm_mix_g", 0, 8, K.u)
    K.new_phase()
    w_in = A["w_in"][0]
    K.fetch("upper")
    K.big_const = K.big_at
    y = K.carve(16, T)
    K.y_ssd = y
    keep_y = K.big_at
    ssd_decays(K, w_in, A["dt_bias"][0], A["A_log"][0], K.cs_dram, None)
    K.new_phase(K.kept_ssd, K.m_cs)
    ssd_groups(K, w_in, K.cs_dram, A["D_skip"][0], y)
    K.new_phase(keep_y)
    K.fetch("inv2", "inv4", "inv8", "inv16")
    used = K.big_at
    pooled = K.carve(KD, T)
    merged = K.carve(KD, T)
    pool_branch(K, w_in, A["pool_w"][0], pooled)
    K.prog.phase()
    K.big_at = used + 16 * T
    combine(K, w_in, A["w_br_ssd"][0], A["w_br_pool"][0], A["w_out"][0], y, pooled, merged)
    K.new_phase()


def vector_list(A):
    f = lambda a: a.rearrange("(k p) -> k p", p=P)
    f2 = lambda a: a.rearrange("i (k p) -> (i k) p", p=P)
    names = [("conv_w", f2(A["conv_w"][0])), ("conv_b", f(A["conv_b"][0])), ("ssd_norm_g", f(A["ssd_norm_g"][0])),
             ("b_ada", f(A["b_ada"][0])), ("c", f2(A["c"])), ("norm_mix_g", f(A["norm_mix_g"][0])),
             ("norm_ffn_g", f(A["norm_ffn_g"][0])), ("final_norm_g", f(A["final_norm_g"])),
             ("pool_scale", f(A["pool_scale"][0]))]
    names += [("a_mu", A["a_mu_2"][0].rearrange("i (k p) -> (i k) p", p=P)),
              ("norm_pre", f2(A["norm_pre_2"])), ("norm_post", f2(A["norm_post_2"])), ("ple_norm", f2(A["ple_norm_2"])),
              ("kv_norm", f(A["kv_norm_2"])), ("subln", f2(A["b_subln_2"]))]
    names += [(n, f(A[f"a_{n}_2"][0])) for n in ("w0", "a0", "k_k", "k_a", "lnx_g", "lnx_b")]
    names += [("r_k", A["a_r_k_2"][0].rearrange("(k a) n -> k (a n)", a=2))]
    return names


def build_program(nc, A, consts, out):
    K = Kernel(nc, consts)
    K.cs_dram = nc.dram_tensor("ssd_sums", [32, T], F32, kind="Internal").ap()
    K.wt_dram = nc.dram_tensor("routing_weights", [E_ALL, T], F32, kind="Internal").ap()
    rwkv_dram = nc.dram_tensor("rwkv_inputs", [KD, P, 6, T], F32, kind="Internal").ap()
    K.prog.start()
    K.fetch("ident", "ones")
    K.load_columns(vector_list(A))
    K.load_x(A["x"][0])
    K.prog.phase()
    block1_mixer(K, A)
    moe(K, A)
    block2(K, A, rwkv_dram)
    K.store_h(out[0])


def kernel(**inputs):
    import concourse.bacc as bacc
    from concourse.bass_utils import run_bass_kernel_spmd

    nc = bacc.Bacc("TRN2", target_bir_lowering=False, num_devices=1)
    arrays, A = {}, {}
    for name, value in inputs.items():
        arrays[f"in_{name}"] = np.ascontiguousarray(value)
        A[name] = nc.dram_tensor(f"in_{name}", arrays[f"in_{name}"].shape, F32, kind="ExternalInput").ap()
    arrays["shape_consts"] = const_table()
    consts = nc.dram_tensor("shape_consts", arrays["shape_consts"].shape, F32, kind="ExternalInput").ap()
    out = nc.dram_tensor("out_h", (1, T, D), F32, kind="ExternalOutput").ap()
    build_program(nc, A, consts, out)
    r = run_bass_kernel_spmd(nc, [arrays], core_ids=[0])
    return r.results[0]["out_h"]
```

```python
import numpy as np
import concourse.bass as bass
from concourse import mybir

F32 = mybir.dt.float32
ALU = mybir.AluOpType
ACT = mybir.ActivationFunctionType
AX = mybir.AxisListType
ds = bass.ds

P = 128
FIRST = 4096


class Mark:

    def __init__(self, count, n, loop=None, shift=0):
        self.count, self.n, self.loop, self.shift = count, n, loop, shift


class Count:

    def __init__(self, prog, name, first=FIRST):
        self.prog, self.sem, self.first = prog, prog.nc.alloc_semaphore(name), first
        self.n, self.start, self.per = 0, first, 0
        if prog.begun and first:
            prog.nc.sync.sem_inc(self.sem, first)
        prog.counts.append(self)

    def add(self, ins, by):
        self.n += by
        if ins is not None:
            ins.then_inc(self.sem, by)
        return self.mark()

    def mark(self):
        if self.prog.in_loop is None:
            return Mark(self, self.start + self.n)
        return Mark(self, self.n, self.prog.in_loop)

    def used(self):
        return self.start + self.n > self.first or self.prog.in_loop is not None

    def value(self, mark):
        if mark.loop is None:
            return mark.n
        assert mark.loop == self.prog.in_loop
        return (self.start - mark.shift * self.per + mark.n) + self.prog.iteration * self.per


def flat(marks):
    for m in marks:
        if isinstance(m, (list, tuple)):
            yield from flat(m)
        elif m is not None:
            yield m


class Lane:

    def __init__(self, prog, eng, name):
        self.prog, self.eng, self.count = prog, eng, Count(prog, f"{name}_done")
        prog.lanes.append(self)

    def wait(self, *marks):
        last = {}
        for m in flat(marks):
            place = (m.count, m.loop is not None)
            if place not in last or (-m.shift, m.n) > (-last[place].shift, last[place].n):
                last[place] = m
        for m in last.values():
            if not self.prog.dry:
                self.eng.wait_ge(m.count.sem, m.count.value(m))
                if self in (self.prog.sp, self.prog.pool) and m.loop is not None:
                    self.eng.sem_inc(self.prog.waits_alone, 1)

    def run(self, fn, *args, after=(), counted=True, **kw):
        self.wait(after, self.count.mark() if self is not self.prog.pe and self.count.used() else ())
        if self.prog.dry:
            return self.count.add(None, 1) if counted else None
        ins = fn(*args, **kw)
        return self.count.add(ins, 1) if counted else None

    def dma(self, slot, out, in_, after=()):
        self.wait(after)
        if not self.prog.dry:
            return slot.count.add(self.eng.dma_start(out, in_), 16)
        return slot.count.add(None, 16)


    def indirect(self, slot, fn, *args, **kw):
        return slot.count.add(None if self.prog.dry else fn(*args, **kw), 16)


class Slot:

    def __init__(self, prog, tensor, name=None, first=FIRST):
        self.t, self.free = tensor, []
        self.count = Count(prog, name, first) if name else None
        prog.slots.append(self)

    def __getitem__(self, key):
        return self.t[key]


class Ring:
    def __init__(self, prog, slots):
        self.slots, self.at = slots, 0
        prog.rings.append(self)

    def take(self, n=1):
        if self.at + n > len(self.slots):
            self.at = 0
        got = self.slots[self.at:self.at + n]
        self.at += n
        return got[0] if n == 1 else got


class Program:
    def __init__(self, nc):
        self.nc = nc
        self.counts, self.slots, self.rings, self.lanes = [], [], [], []
        self.in_loop, self.iteration, self.dry, self.loops = None, None, False, 0
        self.begun = False
        self.turn_sems, self.over = [], 0
        self.turns_over = nc.alloc_semaphore("turns_over")
        self.waits_alone = nc.alloc_semaphore("waits_alone")
        self.pe = None
        self.pe = Lane(self, nc.tensor, "pe")
        self.act = Lane(self, nc.scalar, "act")
        self.dve = Lane(self, nc.vector, "dve")
        self.pool = Lane(self, nc.gpsimd, "pool")
        self.sp = Lane(self, nc.sync, "sp")

    def arrivals(self, name):
        return Slot(self, None, f"{name}_{len(self.counts)}")

    def start(self):
        self.begun = True
        for c in self.counts:
            self.nc.sync.sem_inc(c.sem, FIRST)

    def _fresh(self):
        for r in self.rings:
            r.at = 0

    def loop(self, times, body):
        self._fresh()
        for c in self.counts:
            c.start, c.n = c.start + c.n, 0
        before = [list(s.free) for s in self.slots]
        self.loops += 1
        self.in_loop, self.dry = self.loops, True
        body(0)
        self.dry = False
        for c in self.counts:
            c.per, c.n = c.n, 0
        for s, b in zip(self.slots, before):
            s.free = b + [Mark(m.count, m.n, m.loop, 1) for m in s.free if m.loop is not None]
        self._fresh()
        with self.nc.Fori(0, times) as i:
            self.iteration = i
            body(i)
        self.in_loop = self.iteration = None
        for c in self.counts:
            c.start += (times - 1) * c.per
        for s in self.slots:
            s.free = [m if m.loop is None else Mark(m.count, m.count.start + m.n)
                      for m in s.free if not m.shift]
        for c in self.counts:
            c.start, c.n, c.per = c.start + c.n, 0, 0
        self._fresh()

    def loop_while(self, times, limit, body):
        self.phase()
        self.join(self.sp)
        for s in self.slots:
            s.free = []
        kept = [(c, c.sem, c.start + c.n) for c in self.counts]
        self.loops += 1
        self.in_loop, self.dry = self.loops, True
        for c in self.counts:
            c.start, c.n = c.first, 0
        self._fresh()
        body(0)
        self.dry = False
        for c in self.counts:
            c.per, c.n = c.n, 0
            if c.per:
                c.sem = self.nc.alloc_semaphore(f"turns_{len(self.turn_sems)}")
                self.turn_sems.append(c.sem)
                if c.first:
                    self.nc.sync.sem_inc(c.sem, c.first)
        for s in self.slots:
            s.free = [Mark(m.count, m.n, m.loop, 1) for m in s.free]
        self._fresh()
        with self.nc.Fori(0, times) as i:
            with self.nc.If(i < limit):
                self.iteration = i
                body(i)
        self.in_loop = self.iteration = None
        for c, sem, start in kept:
            c.sem, c.start, c.n, c.per = sem, start, 0, 0
        for s in self.slots:
            s.free = []
        self._fresh()
        for lane in self.lanes:
            lane.eng.drain().then_inc(self.turns_over, 1)
        self.over += len(self.lanes)
        for lane in self.lanes:
            lane.eng.wait_ge(self.turns_over, self.over)

    def join(self, *lanes):
        marks = [e.count.mark() for e in (self.pe, self.act, self.dve, self.pool) if e.count.used()]
        for lane in lanes:
            lane.wait(marks)

    def phase(self, *stores):
        marks = [e.count.mark() for e in (self.pe, self.act, self.dve, self.pool) if e.count.used()]
        for lane in self.lanes:
            if lane is not self.sp:
                lane.wait(marks, stores)
T = 512
D = 1024
KD = D // P
NT = T // P
ROUTED_SCALE = 2.5

BIG = 28160

CONST_COLS = {}


def const_table():
    parts = []

    def put(name, a):
        a = np.asarray(a, np.float32)
        start = sum(x.shape[1] for x in parts)
        CONST_COLS[name] = (start, a.shape[1])
        parts.append(a)

    r, c = np.arange(P)[:, None], np.arange(P)[None, :]
    t = np.arange(T)
    wide = np.ones((P, 1))
    put("ident", r == c)
    put("ones", np.ones((P, P)))
    put("upper", r <= c)
    put("same_head", r // 64 == c // 64)
    put("neg_up16", -1.0 * ((r < c) & (r // 16 == c // 16)))
    put("neg_low16", -1.0 * ((r > c) & (r // 16 == c // 16)))
    for b in (16, 32):
        put(f"neg_off{b}", -1.0 * ((r // (2 * b) == c // (2 * b)) & (r // b > c // b)))
    put("up64", (r < c) & (r // 64 == c // 64))
    put("upeq64", (r <= c) & (r // 64 == c // 64))
    put("future", np.where(c > r, -1e30, 0.0))
    g = np.arange(8)
    put("before8", wide * (g[None, :] < g[:, None]).reshape(1, 64))
    put("before", r < c)
    put("slot_row", np.broadcast_to(c, (P, P)))
    put("expert_row", wide * np.arange(64)[None, :])
    put("token_and_one", np.stack([r[:, 0] + P * (i // 2) if i % 2 == 0 else r[:, 0] * 0 + 1 for i in range(8)], 1))
    put("spare_row", T + r + 0 * c[:, 0:2])
    put("scan128", wide * (t % 128 != 0)[None, :])
    put("scan64", wide * (t % 64 != 0)[None, :])
    for w in (2, 4, 8, 16):
        put(f"inv{w}", wide * (1.0 / np.minimum(t + 1, w))[None, :])
    inv = np.float32(500000.0) ** (-np.arange(0, 16, 2, dtype=np.float32) / np.float32(16))
    ang = t.astype(np.float32)[:, None] * inv[None, :]
    cos, sin, turn = np.ones((P, T)), np.zeros((P, T)), np.zeros((P, P))
    for comp in (0, 64):
        for j in range(8):
            for half in (0, 8):
                cos[comp + half + j] = np.cos(ang[:, j])
                sin[comp + half + j] = np.sin(ang[:, j])
            turn[comp + 8 + j, comp + j] = -1.0
            turn[comp + j, comp + 8 + j] = 1.0
    put("cos", cos)
    put("sin", sin)
    put("turn", turn)
    put("head_cols", np.stack([np.arange(P) < 64, np.arange(P) >= 64], 1))
    return np.concatenate(parts, axis=1)


class Kernel:

    def __init__(self, nc, consts):
        self.nc = nc
        self.prog = p = Program(nc)
        self.PE, self.ACT, self.DVE, self.POOL, self.SP = p.pe, p.act, p.dve, p.pool, p.sp
        self.sbuf_names = 0
        self.psum = nc.alloc_psum_tensor("psum_all", [P, 8, 512], F32)
        self.banks = [Slot(p, self.psum[:, b, :]) for b in range(8)]
        self.bank_ring = Ring(p, self.banks)
        self.wslots = [Slot(p, self.sb(f"weights{n}", [P, 2048]), f"weights{n}_in") for n in range(6)]
        self.wring = Ring(p, self.wslots)
        self.consts = consts
        self.const = self.sb("const_sb", [P, 2 * P])
        self.at_hand = {"ident": self.const[:, 0:P], "ones": self.const[:, P:2 * P]}
        self.h = self.sb("h", [P, KD, T])
        self.u = self.sb("u", [P, KD, T])
        self.big = self.sb("big", [P, BIG])
        self.sq = [Slot(p, self.sb(f"sq{n}", [P, T])) for n in range(2)]
        self.rstd = self.sb("rstd", [P, T])
        self.sq_ring = Ring(p, self.sq)
        self.stat = self.sb("stat", [P, 64])
        self.big_at = 0

    def sb(self, name, shape, dt=F32):
        return self.nc.alloc_sbuf_tensor(name, shape, dt)

    def c(self, name):
        return self.at_hand[name]

    def fetch(self, *names):
        arrive = self.prog.arrivals("const")
        for name in names:
            a, n = CONST_COLS[name]
            where = self.const[:, (0 if name == "ident" else P):(P if name == "ident" else 2 * P)] \
                if name in ("ident", "ones") else self.carve(n)
            self.at_hand[name] = where
            m = self.ACT.dma(arrive, where, self.consts[:, a:a + n])
        for lane in (self.PE, self.DVE, self.ACT):
            lane.wait(m)
        self.in_const = m

    def carve(self, *shape):
        n = int(np.prod(shape))
        a = self.big[:, self.big_at:self.big_at + n]
        self.big_at += n
        assert self.big_at <= BIG, self.big_at
        if len(shape) == 2:
            return a.rearrange("p (a b) -> p a b", b=shape[1])
        if len(shape) == 3:
            return a.rearrange("p (a b c) -> p a b c", b=shape[1], c=shape[2])
        return a

    def new_phase(self, keep=0, stores=()):
        self.prog.phase(stores)
        self.big_at = keep

    def bank(self, n=1):
        return self.bank_ring.take(n)

    def weights(self, view, cols, rows=KD, slot=None, lane=None):
        slot = slot or self.wring.take()
        n = view.shape[-1]
        dst = slot[:, 0:rows * n].rearrange("p (k n) -> p k n", n=n)
        m = (lane or self.SP).dma(slot, dst, view, after=slot.free)
        slot.free = []
        return slot, dst, m

    def matmuls(self, out, terms, after=()):
        for n, (lhsT, rhs) in enumerate(terms):
            last = n == len(terms) - 1
            m = self.PE.run(self.nc.tensor.matmul, out, lhsT, rhs, start=n == 0, stop=last,
                            after=after, counted=last)
            after = ()
        return m

    def project(self, w, j, src, k=KD, m_in=(), bank=None):
        b = bank or self.bank()
        m = self.matmuls(b[:, :], [(w[:, i, j * P:(j + 1) * P], src[:, i, :]) for i in range(k)],
                         after=[m_in, b.free])
        b.free = []
        return b, m

    def transposes(self, out_in, bank, after=()):
        after = [after, bank.free]
        for n, (o, i) in enumerate(out_in):
            k = i.shape[0]
            m = self.PE.run(self.nc.tensor.transpose, o, i, self.c("ident")[0:k, 0:k], after=after,
                            counted=n == len(out_in) - 1)
            after = ()
        bank.free = []
        return m

    def rms(self, chunks, width, eps, after=(), ones="ones"):
        nc = self.nc
        b = self.bank()
        n = len(chunks)
        for k, ch in enumerate(chunks):
            s = self.sq_ring.take()
            m = self.ACT.run(nc.scalar.activation, s[:, :], ch, ACT.Square, after=[after, s.free])
            m = self.PE.run(nc.tensor.matmul, b[:, :], self.c(ones), s[:, :], start=k == 0, stop=k == n - 1,
                            after=[m, b.free if k == 0 else ()])
            s.free = [m]
        m = self.DVE.run(nc.vector.tensor_scalar, self.rstd[:, :], b[:, :], 1.0 / width, eps,
                         ALU.mult, ALU.add, after=m)
        b.free = [m]
        m = self.ACT.run(nc.scalar.activation, self.rstd[:, :], self.rstd[:, :], ACT.Sqrt, after=m)
        return self.DVE.run(nc.vector.reciprocal, self.rstd[:, :], self.rstd[:, :], after=m)

    def scaled(self, out, chunks, gains, shifts=None, after=()):
        nc = self.nc
        for k, ch in enumerate(chunks):
            m = self.DVE.run(nc.vector.tensor_tensor, out[:, k, :], ch, self.rstd[:, :], ALU.mult, after=after)
            if shifts is None:
                m = self.DVE.run(nc.vector.tensor_scalar, out[:, k, :], out[:, k, :], gains[:, k:k + 1], None,
                                 ALU.mult)
            else:
                m = self.DVE.run(nc.vector.tensor_scalar, out[:, k, :], out[:, k, :], gains[:, k:k + 1],
                                 shifts[:, k:k + 1], ALU.mult, ALU.add)
        return m

    def load_columns(self, vectors):
        nc = self.nc
        self.cols = {}
        total = sum(a.shape[0] for _, a in vectors)
        tiles = -(-total // P) + 1
        self.columns = self.sb("columns", [P, tiles * P])
        rows = self.big[:, 0:tiles * P]
        m0 = self.DVE.run(nc.vector.memset, rows, 0.0)
        at = 0
        arrive = self.prog.arrivals("vectors")
        for name, a in vectors:
            n = a.shape[0]
            if at % P + n > P:
                at += P - at % P
            self.cols[name] = (at, n)
            t, r = at // P, at % P
            m = self.SP.dma(arrive, rows[r:r + n, t * P:(t + 1) * P], a, after=m0)
            at += n
        assert at <= tiles * P
        for t in range(tiles):
            b = self.bank()
            m1 = self.transposes([(b[:, 0:P], rows[:, t * P:(t + 1) * P])], b, after=[m, self.in_const])
            m1 = self.DVE.run(nc.vector.tensor_copy, self.columns[:, t * P:(t + 1) * P], b[:, 0:P], after=m1)
            b.free = [m1]
        return m1

    def col(self, name, k=None):
        a, n = self.cols[name]
        return self.columns[:, a:a + n] if k is None else self.columns[:, a + k:a + k + 1]

    def load_x(self, x):
        nc = self.nc
        for t in range(NT):
            s = self.wring.take()
            m = self.SP.dma(s, s[:, 0:D], x[t * P:(t + 1) * P, :], after=s.free)
            for half in range(2):
                b = self.bank()
                m1 = self.transposes([(b[:, j * P:(j + 1) * P], s[:, (4 * half + j) * P:(4 * half + j + 1) * P])
                                      for j in range(4)], b, after=[m, self.in_const])
                m2 = self.DVE.run(nc.vector.tensor_copy, self.h[:, 4 * half:4 * half + 4, t * P:(t + 1) * P],
                                  b[:, :].rearrange("p (a b) -> p a b", b=P), after=m1)
                b.free = [m2]
            s.free = [m1]
        return m2

    def store_rows(self, src, out):
        nc, stores = self.nc, []
        for t in range(NT):
            s = self.wring.take()
            for half in range(2):
                b = self.bank()
                m1 = self.transposes([(b[:, j * P:(j + 1) * P], src[:, 4 * half + j, t * P:(t + 1) * P])
                                      for j in range(4)], b, after=self.DVE.count.mark())
                m2 = self.DVE.run(nc.vector.tensor_copy, s[:, 512 * half:512 * half + 512], b[:, :],
                                  after=[m1, s.free])
                b.free = [m2]
            m = self.SP.dma(s, out[t * P:(t + 1) * P, :], s[:, 0:D], after=m2)
            s.free = [m]
            stores.append(m)
        return stores
def adaln(K, w_ada):
    nc, prog = K.nc, K.prog
    K.mod = K.sb("mod", [P, 48])
    K.c_act = K.sb("c_act", [P, KD])
    acc = K.carve(2048)
    K.ACT.run(nc.scalar.activation, K.c_act[:, :], K.col("c"), ACT.Silu, after=K.DVE.count.mark())
    m_c = K.ACT.count.mark()
    view = w_ada.rearrange("(k p) n -> p k n", p=P)
    acc_slot = Slot(prog, acc)
    acc_slot.free = []
    K.DVE.wait(m_c)

    def group(g):
        for k in range(KD):
            s, w, m = K.weights(view[:, k:k + 1, ds(g * 2048, 2048)], None, rows=1)
            if k == 0:
                m = K.DVE.run(nc.vector.tensor_scalar, acc, w[:, 0, :], K.c_act[:, 0:1], None, ALU.mult,
                              after=[m, acc_slot.free])
            else:
                m = K.DVE.run(nc.vector.scalar_tensor_tensor, acc, w[:, 0, :], K.c_act[:, k:k + 1], acc,
                              ALU.mult, ALU.add, after=m)
            s.free = [m]
        b = K.bank()
        for j in range(16):
            m = K.PE.run(nc.tensor.matmul, b[:, j:j + 1], acc[:, j * P:(j + 1) * P], K.c("ones")[:, 0:1],
                         start=True, stop=True, after=[m, b.free if j == 0 else ()], counted=j == 15) or m
        acc_slot.free = [m]
        a = K.cols["b_ada"][0]
        m = K.DVE.run(nc.vector.tensor_tensor, K.mod[:, ds(g * 16, 16)], b[:, 0:16],
                      K.columns[:, ds(a + g * 16, 16)], ALU.add, after=m)
        b.free = [m]

    prog.loop(3, group)


def modulated_norm(K, gain, shift_at, scale_at, out):
    nc = K.nc
    g = K.stat[:, 0:KD]
    m = K.rms([K.h[:, k, :] for k in range(KD)], D, 1e-6, after=K.DVE.count.mark())
    K.DVE.run(nc.vector.tensor_scalar, g, K.mod[:, scale_at:scale_at + KD], 1.0, None, ALU.add)
    K.DVE.run(nc.vector.tensor_tensor, g, g, K.col(gain), ALU.mult)
    return K.scaled(out, [K.h[:, k, :] for k in range(KD)], g, K.mod[:, shift_at:shift_at + KD])


def ssd_decays(K, w_in, dt_bias, A_log, cs_dram, cd_dram):
    nc, V, S = K.nc, K.DVE, K.ACT
    H = 32
    K.headq = K.carve(4, NT, H)
    K.cdb = K.carve(NT, H)
    K.kept_ssd = K.big_at
    sc = K.carve(12, T)
    K.fetch("scan128")
    q = lambda n: sc[0:H, n, :]
    s, w, m = K.weights(w_in.rearrange("(k p) n -> p k n", p=P)[:, :, 6144:6144 + H], None)
    small = K.stat[0:H, 16:20]
    io = K.prog.arrivals("head_vectors")
    m1 = K.ACT.dma(io, small[:, 0:1], dt_bias.rearrange("(h a) -> h a", a=1))
    m1 = K.ACT.dma(io, small[:, 1:2], A_log.rearrange("(h a) -> h a", a=1))
    b = K.bank()
    m = K.matmuls(b[0:H, :], [(w[:, k, :], K.u[:, k, :]) for k in range(KD)], after=[m, b.free, V.count.mark()])
    s.free = [m]
    x, ax, e, z, z2, acc, dt, cs, e1, dd, tmp = (q(n) for n in range(11))
    ts, tt, stt = nc.vector.tensor_scalar, nc.vector.tensor_tensor, nc.vector.scalar_tensor_tensor
    m = V.run(ts, x, b[0:H, :], small[:, 0:1], None, ALU.add, after=[m, m1])
    b.free = [m]
    V.run(ts, tmp, x, -1.0, None, ALU.mult)
    m = V.run(tt, ax, x, tmp, ALU.min)
    m = S.run(nc.scalar.activation, e, ax, ACT.Exp, after=m)
    V.run(ts, z, e, 2.0, None, ALU.add, after=m)
    V.run(nc.vector.reciprocal, z, z)
    V.run(tt, z, z, e, ALU.mult)
    V.run(tt, z2, z, z, ALU.mult)
    V.run(ts, acc, z2, 1.0 / 17, 1.0 / 15, ALU.mult, ALU.add)
    for d in (13, 11, 9, 7, 5, 3, 1):
        V.run(tt, acc, acc, z2, ALU.mult)
        V.run(ts, acc, acc, 1.0 / d, None, ALU.add)
    V.run(tt, acc, acc, z, ALU.mult)
    V.run(ts, tmp, x, 0.0, None, ALU.max)
    m = V.run(stt, dt, acc, 2.0, tmp, ALU.mult, ALU.add)
    m = S.run(nc.scalar.activation, small[:, 2:3], small[:, 1:2], ACT.Exp, after=m)
    m = V.run(ts, small[:, 2:3], small[:, 2:3], -1.0, None, ALU.mult, after=m)
    V.run(ts, tmp, dt, small[:, 2:3], None, ALU.mult)
    m = V.run(nc.vector.tensor_tensor_scan, cs, K.c("scan128")[0:H, :], tmp, 0.0, ALU.mult, ALU.add)
    m_cs = K.ACT.dma(K.prog.arrivals("cs_out"), cs_dram, cs, after=m)
    m = S.run(nc.scalar.activation, e1, cs, ACT.Exp, after=m)
    for c in range(NT):
        end = cs[:, (c + 1) * P - 1:(c + 1) * P]
        m = V.run(ts, dd[:, c * P:(c + 1) * P], cs[:, c * P:(c + 1) * P], -1.0, end, ALU.mult, ALU.add)
    m = S.run(nc.scalar.activation, dd, dd, ACT.Exp, after=m)
    m = V.run(tt, dd, dd, dt, ALU.mult, after=m)
    diag = sc[0:H, 11, 0:P].rearrange("h (c g) -> h c g", g=H)
    for c in range(NT):
        m = V.run(ts, diag[:, c, :], K.c("ident")[0:H, 0:H], e1[:, (c + 1) * P - 1:(c + 1) * P], None, ALU.mult)
    b = K.bank()
    m = K.matmuls(b[:, 0:P], [(K.c("ones")[0:H, :], sc[0:H, 11, 0:P])], after=[m, b.free])
    m = V.run(nc.vector.tensor_copy, K.cdb, b[:, 0:P].rearrange("p (c g) -> p c g", g=H), after=m)
    b.free = [m]
    b = K.bank()
    m = K.transposes([(b[:, (i * NT + c) * H:(i * NT + c + 1) * H], src[:, c * P:(c + 1) * P])
                      for i, src in enumerate((dt, cs, e1, dd)) for c in range(NT)], b, after=m)
    m = V.run(nc.vector.tensor_copy, K.headq.rearrange("p a c h -> p (a c h)"), b[:, :], after=m)
    b.free = [m]
    K.m_cs = m_cs


def ssd_groups(K, w_in, cs_dram, D_skip, y):
    nc, V, S, prog = K.nc, K.DVE, K.ACT, K.prog
    ts, tt, stt = nc.vector.tensor_scalar, nc.vector.tensor_tensor, nc.vector.scalar_tensor_tensor
    act = nc.scalar.activation
    pre = [Slot(prog, K.carve(T + 3)) for _ in range(2)]
    pre_ring = Ring(prog, pre)
    post = K.carve(4, T)
    xs_tok, xdt, xdec = K.carve(NT, 256), K.carve(NT, 256), K.carve(NT, 256)
    B_tok = K.carve(NT, P)
    CB = K.carve(NT, P)
    prev = K.carve(NT, 256)
    zs = K.carve(NT, 256)
    cs_all = Slot(prog, K.carve(4, T), "cs_all_in")
    W = K.carve(4, NT, P)
    ytok, t1 = K.carve(NT, 256), K.carve(NT, 256)
    gcol = K.carve(64)
    hq = K.carve(4 * NT, 4)
    cd = K.carve(NT, 4)
    Dsk = K.carve(32)
    Dg, ss, nss = K.carve(4), K.carve(4), K.carve(4)
    m_D = K.ACT.dma(K.prog.arrivals("D_skip"), Dsk, D_skip.partition_broadcast(P))
    for p_ in pre:
        V.run(nc.vector.memset, p_[:, 0:3], 0.0)
    V.run(nc.vector.memset, prev[:, 0, :], 0.0)
    V.wait(m_D)
    wv = w_in.rearrange("(k p) n -> p k n", p=P)
    cwa, cba, nga = K.cols["conv_w"][0], K.cols["conv_b"][0], K.cols["ssd_norm_g"][0]
    cw = K.columns[:, cwa:cwa + 128].rearrange("p (i c) -> p i c", i=4)
    gw = gcol[:, 0:16].rearrange("p (i c) -> p i c", i=4)

    def group(g):
        prog.join(V, S)
        cp = nc.vector.tensor_copy
        V.run(cp, gw[:, :, 0:2], cw[:, :, ds(2 * g, 2)])
        V.run(cp, gw[:, :, 2:3], cw[:, :, ds(16 + g, 1)])
        V.run(cp, gw[:, :, 3:4], cw[:, :, ds(24 + g, 1)])
        V.run(cp, gcol[:, 16:18], K.columns[:, ds(cba + 2 * g, 2)])
        V.run(cp, gcol[:, 18:19], K.columns[:, ds(cba + 16 + g, 1)])
        V.run(cp, gcol[:, 19:20], K.columns[:, ds(cba + 24 + g, 1)])
        V.run(cp, gcol[:, 20:22], K.columns[:, ds(nga + 2 * g, 2)])
        V.run(cp, Dg, Dsk[:, ds(4 * g, 4)])
        V.run(cp, cd, K.cdb[:, :, ds(4 * g, 4)])
        V.run(cp, hq, K.headq.rearrange("p a c h -> p (a c) h")[:, :, ds(4 * g, 4)])
        m_csb = K.ACT.dma(cs_all, cs_all.t, cs_dram[ds(4 * g, 4), :].partition_broadcast(P), after=cs_all.free)
        sx, wx, mx = K.weights(wv[:, :, ds(2048 + 256 * g, 256)], None)
        sbc = K.wring.take()
        wbc = sbc[:, :].rearrange("p (a k n) -> p a k n", a=2, k=KD)
        K.SP.dma(sbc, wbc[:, 0], wv[:, :, ds(4096 + 128 * g, 128)], after=sbc.free)
        mbc = K.SP.dma(sbc, wbc[:, 1], wv[:, :, ds(5120 + 128 * g, 128)])
        sz, wz, mz = K.weights(wv[:, :, ds(256 * g, 256)], None)
        for j in range(4):
            w, i, m_w = (wx, j, mx) if j < 2 else (wbc[:, j - 2], 0, mbc)
            b, m = K.project(w, i, K.u, m_in=m_w)
            if j == 1:
                sx.free = [m]
            if j == 3:
                sbc.free = [m]
            p_ = pre_ring.take()
            m = S.run(act, p_[:, 3:3 + T], b[:, :], ACT.Copy, after=[m, p_.free])
            b.free = [m]
            m = V.run(ts, post[:, j, :], p_[:, 0:T], gw[:, 0, j:j + 1], gcol[:, 16 + j:17 + j], ALU.mult, ALU.add,
                      after=[m, post_free[0]])
            for i in range(1, 4):
                m = V.run(stt, post[:, j, :], p_[:, i:i + T], gw[:, i, j:j + 1], post[:, j, :], ALU.mult, ALU.add)
            p_.free = [m]
            m_post = S.run(act, post[:, j, :], post[:, j, :], ACT.Silu, after=m)
        zb = K.bank(2)
        for c in range(NT):
            b = zb[c // 2]
            m = K.matmuls(b[:, c % 2 * 256:c % 2 * 256 + 256],
                          [(K.u[:, k, c * P:(c + 1) * P], wz[:, k, :]) for k in range(KD)],
                          after=[mz, b.free if c % 2 == 0 else ()])
        sz.free = [m]
        for i, b in enumerate(zb):
            m = S.run(act, zs[:, 2 * i:2 * i + 2, :].rearrange("p a b -> p (a b)"), b[:, :], ACT.Silu, after=m)
            b.free = [m]
        m_z = m
        xb = K.bank(2)
        for i, b in enumerate(xb):
            m = K.transposes([(b[:, (c * 2 + j) * P:(c * 2 + j + 1) * P], post[:, j, (2 * i + c) * P:(2 * i + c + 1) * P])
                              for c in range(2) for j in range(2)], b, after=m_post)
            m = S.run(act, xs_tok[:, 2 * i:2 * i + 2, :].rearrange("p a b -> p (a b)"), b[:, :], ACT.Copy, after=m)
            b.free = [m]
        bb = K.bank()
        m1 = K.transposes([(bb[:, c * P:(c + 1) * P], post[:, 2, c * P:(c + 1) * P]) for c in range(NT)], bb)
        m1 = S.run(act, B_tok.rearrange("p a b -> p (a b)"), bb[:, :], ACT.Copy, after=m1)
        bb.free = [m1]
        xh = xs_tok.rearrange("p c (h d) -> p (c h) d", d=64)
        per_head = lambda a: hq[:, 4 * a:4 * a + 4, :].rearrange("p c h -> p (c h)").unsqueeze(2).to_broadcast([P, 16, 64])
        V.run(tt, xdt.rearrange("p c (h d) -> p (c h) d", d=64), xh, per_head(0), ALU.mult, after=m)
        m_x = V.run(tt, xdec.rearrange("p c (h d) -> p (c h) d", d=64), xh, per_head(3), ALU.mult)
        cb = K.bank()
        for c in range(NT):
            m = K.matmuls(cb[:, c * P:(c + 1) * P], [(post[:, 2, c * P:(c + 1) * P], post[:, 3, c * P:(c + 1) * P])],
                          after=cb.free if c == 0 else ())
        m = V.run(tt, CB, cb[:, :].rearrange("p (c l) -> p c l", l=P),
                  K.c("upper").unsqueeze(1).to_broadcast([P, NT, P]), ALU.mult, after=m)
        cb.free = [m]
        for r in range(4):
            V.run(tt, W[:, r], cs_all.t[:, r, :].rearrange("p (c l) -> p c l", l=P),
                  hq[:, 4:8, r].unsqueeze(2).to_broadcast([P, NT, P]), ALU.subtract, after=m_csb)
        Wf = W.rearrange("p r c l -> p (r c l)")
        m = V.run(ts, Wf, Wf, 0.0, None, ALU.min)
        cs_all.free = [m]
        m = S.run(act, Wf, Wf, ACT.Exp, after=m)
        for r in range(4):
            m = V.run(tt, W[:, r], W[:, r], CB, ALU.mult, after=m)
        m_W = m
        sbk = K.bank(2)
        for c in range(3):
            b = sbk[c // 2]
            m = K.matmuls(b[:, c % 2 * 256:c % 2 * 256 + 256], [(B_tok[:, c, :], xdec[:, c, :])],
                          after=[m1, m_x, b.free if c % 2 == 0 else ()])
        for c in range(3):
            b = sbk[c // 2]
            add = b[:, c % 2 * 256:c % 2 * 256 + 256]
            if c == 0:
                m = V.run(cp, prev[:, 1, :], add, after=[m, prev_free[0]])
            else:
                V.run(tt, prev[:, c + 1, :].rearrange("p (h d) -> p h d", d=64),
                      prev[:, c, :].rearrange("p (h d) -> p h d", d=64),
                      cd[:, c, :].unsqueeze(2).to_broadcast([P, 4, 64]), ALU.mult)
                m = V.run(tt, prev[:, c + 1, :], prev[:, c + 1, :], add, ALU.add)
            b.free = [m]
        yd, yo = K.bank(2), K.bank(2)
        for c in range(NT):
            b, o = yo[c // 2], c % 2 * 256
            m = K.matmuls(b[:, o:o + 256], [(post[:, 3, c * P:(c + 1) * P], prev[:, c, :])],
                          after=[m, b.free if c % 2 == 0 else ()])
            b = yd[c // 2]
            for r in range(4):
                m = K.matmuls(b[:, o + 64 * r:o + 64 * r + 64], [(W[:, r, c, :], xdt[:, c, 64 * r:64 * r + 64])],
                              after=[m_W, b.free if c % 2 == 0 and r == 0 else ()])
        post_free[0] = prev_free[0] = None
        for i in range(2):
            o = yo[i]
            h4 = lambda a: a.rearrange("p (x d) -> p x d", d=64)
            m2 = V.run(tt, t1[:, 2 * i:2 * i + 2, :].rearrange("p c (h d) -> p (c h) d", d=64), h4(o[:, :]),
                       hq[:, 8 + 2 * i:10 + 2 * i, :].rearrange("p c h -> p (c h)").unsqueeze(2).to_broadcast([P, 8, 64]),
                       ALU.mult, after=m)
            o.free = [m2]
            f = lambda a: a[:, 2 * i:2 * i + 2, :].rearrange("p a b -> p (a b)")
            m2 = V.run(tt, f(t1), f(t1), yd[i][:, :], ALU.add)
            yd[i].free = [m2]
        for c in range(NT):
            V.run(tt, ytok[:, c, :].rearrange("p (h d) -> p h d", d=64), xs_tok[:, c, :].rearrange("p (h d) -> p h d", d=64),
                  Dg.unsqueeze(2).to_broadcast([P, 4, 64]), ALU.mult)
        V.run(tt, ytok, ytok, t1, ALU.add)
        V.run(tt, ytok, ytok, zs, ALU.mult, after=m_z)
        V.run(tt, t1, ytok, ytok, ALU.mult)
        V.run(nc.vector.tensor_reduce, ss, t1, AX.X, ALU.add)
        m = V.run(ts, ss, ss, 1.0 / 256, 1e-6, ALU.mult, ALU.add)
        m = S.run(act, nss, ss, ACT.Sqrt, after=m)
        V.run(nc.vector.reciprocal, nss, nss, after=m)
        m = V.run(tt, ytok, ytok, nss.unsqueeze(2).to_broadcast([P, NT, 256]), ALU.mult)
        for j in range(2):
            b = K.bank()
            m = K.transposes([(b[:, c * P:(c + 1) * P], ytok[:, c, j * P:(j + 1) * P]) for c in range(NT)], b, after=m)
            m = S.run(act, y[:, ds(2 * g + j, 1), :], b[:, :].unsqueeze(1), ACT.Copy, scale=gcol[:, 20 + j:21 + j], after=m)
            b.free = [m]

    post_free, prev_free = [None], [None]
    prog.loop(8, group)


def pool_branch(K, w_in, pool_w, mixed):
    nc, V, S, prog = K.nc, K.DVE, K.ACT, K.prog
    tt, stt = nc.vector.tensor_tensor, nc.vector.scalar_tensor_tensor
    PADW = 16
    xp = [Slot(prog, K.carve(PADW + T)) for _ in range(2)]
    sums = [K.carve(PADW + T) for _ in range(2)]
    pooled = Slot(prog, K.carve(2, T))
    for a in [x.t for x in xp] + sums:
        V.run(nc.vector.memset, a[:, 0:PADW], 0.0)
    wv = w_in.rearrange("(k p) n -> p k n", p=P)
    for gi, win in enumerate((2, 4, 8, 16)):
        s, w, m_w = K.weights(wv[:, :, 6176 + 256 * gi:6176 + 256 * gi + 256], None)
        sp, wp, m_p = K.weights(pool_w[gi].rearrange("(k p) n -> p k n", p=P), None, rows=2)
        pf = pooled.free
        for j in range(2):
            b, m = K.project(w, j, K.u, m_in=m_w)
            s.free = [m]
            x = xp[j]
            m = S.run(nc.scalar.activation, x[:, PADW:], b[:, :], ACT.Copy, after=[m, x.free])
            b.free = [m]
            cur, step, n = x.t, 1, 0
            while step < win:
                nxt = sums[n % 2]
                V.run(tt, nxt[:, PADW:], cur[:, PADW:], cur[:, PADW - step:PADW - step + T], ALU.add, after=m)
                cur, step, n = nxt, 2 * step, n + 1
            other = sums[n % 2]
            V.run(tt, other[:, PADW:], cur[:, PADW:], K.c(f"inv{win}"), ALU.mult)
            m = V.run(tt, pooled[:, j, :], other[:, PADW:], x[:, PADW:], ALU.subtract, after=pf)
            x.free = [m]
        for j in range(2):
            b, m1 = K.project(wp, j, pooled.t, k=2, m_in=[m_p, m])
            sp.free = pooled.free = [m1]
            m1 = S.run(nc.scalar.activation, mixed[:, 2 * gi + j, :], b[:, :], ACT.Copy,
                      scale=K.col("pool_scale", 2 * gi + j), after=m1)
            b.free = [m1]


def combine(K, w_in, w_br_ssd, w_br_pool, w_out, y, pooled, merged):
    nc, V, S, prog = K.nc, K.DVE, K.ACT, K.prog
    tt, stt = nc.vector.tensor_tensor, nc.vector.scalar_tensor_tensor
    wv = w_in.rearrange("(k p) n -> p k n", p=P)
    wsv = w_br_ssd.rearrange("(k p) n -> p k n", p=P)
    wpv = w_br_pool.rearrange("(k p) n -> p k n", p=P)
    gate = [Slot(prog, K.carve(T)) for _ in range(2)]

    def column(j):
        ss, ws, m_s = K.weights(wsv[:, :, ds(j * P, P)], None, rows=16)
        sp, wp, m_p = K.weights(wpv[:, :, ds(j * P, P)], None)
        sg = K.wring.take()
        wg = sg[:, :].rearrange("p (a k n) -> p a k n", a=2, k=KD)
        K.SP.dma(sg, wg[:, 0], wv[:, :, ds(7200 + j * P, P)], after=sg.free)
        m_g = K.SP.dma(sg, wg[:, 1], wv[:, :, ds(8224 + j * P, P)])
        for i in range(2):
            b, m = K.project(wg[:, i], 0, K.u, m_in=m_g)
            sg.free = [m]
            m = S.run(nc.scalar.activation, gate[i][:, :], b[:, :], ACT.Sigmoid, after=[m, gate[i].free])
            b.free = [m]
        b1, m1 = K.project(ws, 0, y, k=16, m_in=m_s)
        ss.free = [m1]
        b2, m2 = K.project(wp, 0, pooled, m_in=m_p)
        sp.free = [m2]
        V.run(tt, gate[0][:, :], gate[0][:, :], b1[:, :], ALU.mult, after=[m, m1])
        b1.free = [V.count.mark()]
        V.run(tt, gate[1][:, :], gate[1][:, :], b2[:, :], ALU.mult, after=m2)
        b2.free = [V.count.mark()]
        m = V.run(tt, merged[:, ds(j, 1), :], gate[0][:, :].unsqueeze(1), gate[1][:, :].unsqueeze(1), ALU.add)
        gate[0].free = gate[1].free = [m]

    prog.loop(KD // 2, lambda i: [column(2 * i + n) for n in range(2)])
    residual_product(K, w_out, merged, 16)


def residual_product(K, w, src, gate_at):
    nc, V = K.nc, K.DVE
    wv = w.rearrange("(k p) n -> p k n", p=P)
    K.PE.wait(K.DVE.count.mark(), K.ACT.count.mark())

    for j2 in range(KD // 2):
        s, w_, m_w = K.weights(wv[:, :, ds(j2 * 256, 256)], None)
        for j in range(2):
            b, m = K.project(w_, j, src, m_in=m_w)
            s.free = [m]
            hj = K.h[:, ds(2 * j2 + j, 1), :]
            m = V.run(nc.vector.scalar_tensor_tensor, hj, b[:, :].unsqueeze(1), K.mod[:, ds(gate_at + 2 * j2 + j, 1)],
                      hj, ALU.mult, ALU.add, after=m)
            b.free = [m]
E_ALL, TOP, F_E = 64, 8, 256


def router(K, w_router, router_bias, score, rep):
    nc, V, S = K.nc, K.DVE, K.ACT
    ts, tt = nc.vector.tensor_scalar, nc.vector.tensor_tensor
    G = 8
    choice, masked = K.carve(NT, E_ALL), K.carve(NT, E_ALL)
    top = K.carve(NT * G, 8)
    gs, gm, pen = K.carve(NT, G), K.carve(NT, G), K.carve(NT, G)
    cmp1, cmp2 = K.carve(NT, G, G), K.carve(NT, G, G)
    bias, total = K.carve(E_ALL), K.carve(NT)
    K.fetch("before8")
    m_b = K.ACT.dma(K.prog.arrivals("router_bias"), bias, router_bias.partition_broadcast(P))
    s, w, m = K.weights(w_router.rearrange("(k p) n -> p k n", p=P), None)
    b = K.bank()
    for t in range(NT):
        m = K.matmuls(b[:, t * E_ALL:(t + 1) * E_ALL], [(K.u[:, k, t * P:(t + 1) * P], w[:, k, :]) for k in range(KD)],
                      after=[m, V.count.mark(), b.free if t == 0 else ()])
    s.free = [m]
    merge = lambda a: a.rearrange("p a b -> p (a b)")
    m = S.run(nc.scalar.activation, merge(score), b[:, 0:NT * E_ALL], ACT.Sigmoid, after=m)
    b.free = [m]
    V.run(tt, choice, score, bias.unsqueeze(1).to_broadcast([P, NT, E_ALL]), ALU.add, after=[m, m_b])
    for t in range(NT):
        for g in range(G):
            V.run(nc.vector.max, top[:, t * G + g, :], choice[:, t, g * 8:(g + 1) * 8])
    V.run(tt, merge(gs), top[:, :, 0], top[:, :, 1], ALU.add)
    other = gs.unsqueeze(2).to_broadcast([P, NT, G, G])
    this = gs.unsqueeze(3).to_broadcast([P, NT, G, G])
    for t in range(NT):
        V.run(tt, cmp1[:, t], other[:, t], this[:, t], ALU.is_gt)
        V.run(tt, cmp2[:, t], other[:, t], this[:, t], ALU.is_equal)
        V.run(tt, cmp2[:, t], cmp2[:, t], K.c("before8").rearrange("p (j i) -> p j i", i=G), ALU.mult)
    V.run(tt, cmp1, cmp1, cmp2, ALU.add)
    V.run(nc.vector.tensor_reduce, gs, cmp1, AX.X, ALU.add)
    V.run(ts, gm, gs, 4.0, None, ALU.is_lt)
    V.run(ts, pen, gm, 1.0, 1e30, ALU.subtract, ALU.mult)
    e8 = lambda a: a.rearrange("p t (g e) -> p (t g) e", e=8)
    wide = lambda a: merge(a).unsqueeze(2).to_broadcast([P, NT * G, 8])
    V.run(tt, e8(masked), e8(choice), wide(gm), ALU.mult)
    V.run(tt, e8(masked), e8(masked), wide(pen), ALU.add)
    for t in range(NT):
        V.run(nc.vector.max, top[:, t, :], masked[:, t, :])
        V.run(nc.vector.match_replace, rep[:, t, :], top[:, t, :], masked[:, t, :], -3e30)
    V.run(tt, rep, rep, masked, ALU.not_equal)
    V.run(tt, score, score, rep, ALU.mult)
    V.run(nc.vector.tensor_reduce, total, score, AX.X, ALU.add)
    V.run(nc.vector.reciprocal, total, total)
    V.run(ts, total, total, ROUTED_SCALE, None, ALU.mult)
    V.run(tt, score, score, total.unsqueeze(2).to_broadcast([P, NT, E_ALL]), ALU.mult)


EXTRA = 31
I32 = mybir.dt.int32
TURN = 8
AHEAD = 4


class Experts:

    def __init__(self, K, u_rows, total_rows):
        self.K, prog = K, K.prog
        self.u_rows, self.total_rows = u_rows, total_rows
        slot = lambda name=None, *shape: Slot(prog, K.carve(*shape), name)
        self.sel = [slot(None, NT, P) for _ in range(2)]
        self.rhs = [slot(None, NT, 3) for _ in range(2)]
        self.lists = [Slot(prog, (K.carve(4), K.sb(f"rows{n}", [P, 2], I32))) for n in range(TURN)]
        self.x_rows = [Slot(prog, K.carve(D), f"x_rows{n}_in", 0) for n in range(AHEAD)]
        self.added = Slot(prog, None, "rows_added", 0)
        self.xT = [slot(None, KD, P) for _ in range(2)]
        self.act = slot(None, F_E)
        self.hid = [slot(None, F_E) for _ in range(2)]
        self.hidT = slot(None, 2, P)
        self.y = [slot(None, D) for n in range(2)]
        for s in self.x_rows:
            K.DVE.run(K.nc.vector.memset, s.t, 0.0)

    def select(self, n, positions, weights, after=()):
        nc, V, K, sel, rhs = self.K.nc, self.K.DVE, self.K, self.sel[n % 2], self.rhs[n % 2]
        V.run(nc.vector.tensor_tensor, sel.t, K.c("slot_row").unsqueeze(1).to_broadcast([P, NT, P]),
              positions.to_broadcast([P, NT, P]), ALU.is_equal, after=[sel.free, after])
        return V.run(nc.vector.tensor_copy, rhs[:, :, 2:3], weights, after=rhs.free)

    def list_tokens(self, n, m):
        K, nc, V = self.K, self.K.nc, self.K.DVE
        sel, rhs, lst = self.sel[n % 2], self.rhs[n % 2], self.lists[n % TURN]
        info, rows = lst.t
        b = K.bank()
        m = K.matmuls(b[:, 0:3], [(sel[:, t, :], rhs[:, t, :]) for t in range(NT)], after=[m, b.free])
        sel.free = rhs.free = [m]
        m = V.run(nc.vector.tensor_copy, info[:, 0:3], b[:, 0:3], after=[m, lst.free])
        b.free = [m]
        V.run(nc.vector.tensor_copy, rows[:, 0:1], info[:, 0:1])
        V.run(nc.vector.scalar_tensor_tensor, info[:, 3:4], info[:, 1:2], self.minus_spare, info[:, 0:1],
              ALU.mult, ALU.add)
        m = V.run(nc.vector.tensor_tensor, rows[:, 1:2], info[:, 3:4], K.c("spare_row")[:, 0:1], ALU.add)
        x = self.x_rows[n % AHEAD]
        K.POOL.wait(m, x.free, K.POOL.count.mark())
        m = K.POOL.indirect(x, K.nc.gpsimd.indirect_dma_start, x.t, None, self.u_rows,
                            bass.IndirectOffsetOnAxis(ap=rows[:, 0:1], axis=0))
        return m

    def turn(self, n, m_rows):
        K, x, xT = self.K, self.x_rows[n % AHEAD], self.xT[n % 2]
        for half in range(2):
            b = K.bank()
            m1 = K.transposes([(b[:, j * P:(j + 1) * P], x[:, (4 * half + j) * P:(4 * half + j + 1) * P])
                               for j in range(4)], b, after=m_rows)
            m = K.ACT.run(K.nc.scalar.activation, xT[:, 4 * half:4 * half + 4, :].rearrange("p a b -> p (a b)"),
                          b[:, :], ACT.Copy, after=[m1, xT.free])
            b.free = [m]
        x.free = [m1]
        return m

    def load(self, n, wg, wu, wd):
        K, slots = self.K, self.K.wslots[3 * (n % 2):3 * (n % 2) + 3]
        return [K.weights(w.rearrange("(k p) n -> p k n", p=P), None, rows=rows, slot=s)
                for w, rows, s in zip((wg, wu, wd), (KD, KD, 2), slots)]

    def gate_up(self, n, xT, w, weight, after=()):
        K, nc, hid = self.K, self.K.nc, self.hid[n % 2]
        (sg, g, mg), (su, u, mu), _ = w
        b = K.bank()
        m = K.matmuls(b[:, 0:F_E], [(xT(k), g[:, k, :]) for k in range(KD)], after=[after, mg, b.free])
        sg.free = [m]
        m1 = K.matmuls(b[:, F_E:2 * F_E], [(xT(k), u[:, k, :]) for k in range(KD)], after=mu)
        su.free = [m1]
        m = K.ACT.run(nc.scalar.activation, self.act.t, b[:, 0:F_E], ACT.Silu, after=[m1, self.act.free])
        if weight is None:
            m = K.DVE.run(nc.vector.tensor_tensor, hid.t, b[:, F_E:2 * F_E], self.act.t, ALU.mult,
                          after=[m, hid.free])
        else:
            m = K.DVE.run(nc.vector.scalar_tensor_tensor, hid.t, b[:, F_E:2 * F_E], weight, self.act.t,
                          ALU.mult, ALU.mult, after=[m, hid.free])
        b.free = self.act.free = [m]
        return m, m1

    def turn_hid(self, n, m_hid):
        K, nc, hid = self.K, self.K.nc, self.hid[n % 2]
        b = K.bank()
        m = K.transposes([(b[:, j * P:(j + 1) * P], hid.t[:, j * P:(j + 1) * P]) for j in range(2)], b, after=m_hid)
        hid.free = [m]
        m = K.DVE.run(nc.vector.tensor_copy, self.hidT.t.rearrange("p a b -> p (a b)"), b[:, 0:F_E],
                      after=[m, self.hidT.free])
        b.free = [m]
        return m

    def down(self, n, w_down, m):
        K, nc, y = self.K, self.K.nc, self.y[n % 2]
        sd, d, md = w_down
        out = []
        for half in range(2):
            b = K.bank()
            m1 = K.matmuls(b[:, :], [(self.hidT.t[:, j, :], d[:, j, half * 512:half * 512 + 512]) for j in range(2)],
                           after=[m, md, b.free])
            dst = y[:, half * 512:half * 512 + 512]
            if half == 0:
                m2 = K.ACT.run(nc.scalar.activation, dst, b[:, :], ACT.Copy, after=[m1, y.free])
            else:
                m2 = K.DVE.run(nc.vector.tensor_copy, dst, b[:, :], after=[m1, y.free])
            b.free = [m2]
            out.append(m2)
        sd.free = self.hidT.free = [m1]
        return out

    def add_rows(self, n, m_y):
        K, y, lst = self.K, self.y[n % 2], self.lists[n % TURN]
        K.POOL.wait(m_y, self.added.free, K.POOL.count.mark())
        m = K.POOL.indirect(self.added, K.nc.gpsimd.indirect_dma_start, self.total_rows,
                            bass.IndirectOffsetOnAxis(ap=lst.t[1][:, 1:2], axis=0), y.t, None, compute_op=ALU.add)
        y.free = lst.free = self.added.free = [m]
        return m


def experts(K, A, score, chosen, u_rows, total_rows):
    nc, V, S, prog = K.nc, K.DVE, K.ACT, K.prog
    ts, tt, stt = nc.vector.tensor_scalar, nc.vector.tensor_tensor, nc.vector.scalar_tensor_tensor
    X = Experts(K, u_rows, total_rows)
    K.fetch("before", "slot_row", "expert_row", "token_and_one", "spare_row")
    pos, far = K.carve(NT, E_ALL), K.carve(NT, E_ALL)
    count, extra, upto, base, hot, hot2 = (K.carve(E_ALL) for _ in range(6))
    one, minus, num, gx, wx = K.carve(E_ALL), K.carve(1), K.carve(8), K.carve(NT), K.carve(NT)
    tmp4 = K.carve(NT, E_ALL)
    number = K.sb("numbers", [P, 2], I32)
    b = K.bank()
    for t in range(NT):
        m = K.matmuls(b[:, t * E_ALL:(t + 1) * E_ALL], [(K.c("before"), chosen[:, t, :])]
                      + [(K.c("ones"), chosen[:, i, :]) for i in range(t)], after=[b.free, V.count.mark()])
    m = K.matmuls(b[:, 256:256 + E_ALL], [(K.c("ones"), chosen[:, i, :]) for i in range(NT)])
    V.run(ts, pos, b[:, 0:256].rearrange("p (t e) -> p t e", e=E_ALL), 1.0, None, ALU.add, after=m)
    m = V.run(nc.vector.tensor_copy, count, b[:, 256:256 + E_ALL])
    b.free = [m]
    V.run(tt, pos, pos, chosen, ALU.mult)
    V.run(ts, pos, pos, 1.0, None, ALU.subtract)
    V.run(ts, extra, count, 128.0, None, ALU.is_gt)
    for more in (256.0, 384.0):
        V.run(ts, base, count, more, None, ALU.is_gt)
        V.run(tt, extra, extra, base, ALU.add)
    V.run(nc.vector.memset, one, 1.0)
    V.run(nc.vector.tensor_tensor_scan, upto, one, extra, 0.0, ALU.mult, ALU.add)
    V.run(tt, extra, upto, extra, ALU.subtract)
    V.run(ts, base, extra, 128.0, 127.0, ALU.mult, ALU.subtract)
    V.run(tt, far, pos, base.unsqueeze(1).to_broadcast([P, NT, E_ALL]), ALU.add)
    V.run(ts, tmp4, pos, 128.0, None, ALU.is_ge)
    V.run(tt, far, far, tmp4, ALU.mult)
    V.run(nc.vector.memset, num, 0.0)
    V.run(nc.vector.tensor_copy, number[:, 0:1], upto[:, E_ALL - 1:E_ALL])
    V.run(ts, minus, K.c("spare_row")[:, 0:1], -1.0, None, ALU.mult)
    X.minus_spare = minus
    for r in X.rhs:
        m_t = V.run(nc.vector.tensor_copy, r[:, :, 0:2], K.c("token_and_one").rearrange("p (t a) -> p t a", a=2))

    rows_in = [Slot(prog, None) for _ in range(AHEAD)]

    select = lambda e, n: X.select(n, pos[:, :, ds(e, 1)], score[:, :, ds(e, 1)])

    def list_tokens(n, m):
        rows_in[n % AHEAD].free = [X.list_tokens(n, m)]

    for n in range(AHEAD):
        list_tokens(n, select(n, n))
    w = X.load(1, A["ws_gate"][0], A["ws_up"][0], A["ws_down"][0])
    turned, hid_ready, w_down = ([Slot(prog, None) for _ in range(2)] for _ in range(3))
    for t in range(NT):
        m, _ = X.gate_up(t, lambda k: K.u[:, k, t * P:(t + 1) * P], w, None)
        m = X.down(t, w[2], X.turn_hid(t, m))
        y = X.y[t % 2]
        m = K.POOL.dma(X.added, total_rows[t * P:(t + 1) * P, :], y.t, after=[m, X.added.free])
        y.free = X.added.free = [m]
    wg, wu, wd = (A[n][0].rearrange("e k n -> (e k) n") for n in ("we_gate", "we_up", "we_down"))
    weights_of = lambda e: (wg[ds(e * D, D), :], wu[ds(e * D, D), :], wd[ds(e * F_E, F_E), :])
    down_view = lambda n: K.wslots[3 * (n % 2) + 2][:, :].rearrange("p (k n) -> p k n", n=D)

    def open_block(e, n):
        w, xT = X.load(n, *weights_of(e)), X.xT[n % 2]
        w_down[n % 2].free = [w[2][2]]
        m_hid, m_read = X.gate_up(n, lambda k: xT[:, k, :], w, X.lists[n % TURN].t[0][:, 2:3], after=turned[n % 2].free)
        hid_ready[n % 2].free, xT.free = [m_hid], [m_read]

    def turn(n):
        turned[n % 2].free = [X.turn(n, rows_in[n % AHEAD].free)]

    def block(e, n, left=E_ALL):
        if left > AHEAD:
            m_sel = select(e + AHEAD, n + AHEAD)
        if left > 1:
            open_block(e + 1, n + 1)
        m = X.turn_hid(n, hid_ready[n % 2].free)
        if left > 2:
            turn(n + 2)
        m = X.down(n, (K.wslots[3 * (n % 2) + 2], down_view(n), w_down[n % 2].free), m)
        if left > AHEAD:
            list_tokens(n + AHEAD, m_sel)
        X.add_rows(n, m)

    turn(0)
    open_block(0, 0)
    turn(1)
    prog.loop(E_ALL // TURN - 1, lambda i: [block(TURN * i + n, n) for n in range(TURN)])
    for n in range(TURN):
        block(E_ALL - TURN + n, n, TURN - n)

    prog.phase(X.added.free)
    limit = nc.values_load(number[0:1, 0:1], min_val=0, max_val=EXTRA)

    def extra_block(i):
        for s in X.x_rows[:1] + X.y[:1] + X.lists[:1] + [X.added]:
            s.free = [V.count.mark()]
        V.run(ts, hot, extra, num[:, 0:1], None, ALU.is_le)
        V.run(ts, hot2, upto, num[:, 0:1], None, ALU.is_gt)
        V.run(tt, hot, hot, hot2, ALU.mult)
        V.run(tt, hot2, hot, K.c("expert_row"), ALU.mult)
        V.run(nc.vector.tensor_reduce, num[:, 1:2], hot2, AX.X, ALU.add)
        m_e = V.run(nc.vector.tensor_copy, number[:, 1:2], num[:, 1:2])
        V.run(tt, tmp4, far, hot.unsqueeze(1).to_broadcast([P, NT, E_ALL]), ALU.mult)
        V.run(nc.vector.tensor_reduce, gx, tmp4, AX.X, ALU.add)
        V.run(tt, tmp4, score, hot.unsqueeze(1).to_broadcast([P, NT, E_ALL]), ALU.mult)
        V.run(nc.vector.tensor_reduce, wx, tmp4, AX.X, ALU.add)
        V.run(ts, gx, gx, num[:, 2:3], None, ALU.subtract)
        m = X.list_tokens(0, X.select(0, gx.unsqueeze(2), wx.unsqueeze(2)))
        K.SP.wait(m_e)
        e = nc.sync.value_load(number[0:1, 1:2], min_val=0, max_val=E_ALL - 1) if not prog.dry else 0
        w = X.load(0, *weights_of(e))
        m = X.turn(0, m)
        m, m_read = X.gate_up(0, lambda k: X.xT[0][:, k, :], w, X.lists[0].t[0][:, 2:3], after=m)
        X.xT[0].free = [m_read]
        m = X.add_rows(0, X.down(0, w[2], X.turn_hid(0, m)))
        V.run(ts, num[:, 0:1], num[:, 0:1], 1.0, None, ALU.add, after=m)
        V.run(ts, num[:, 2:3], num[:, 2:3], 128.0, None, ALU.add)

    V.run(nc.vector.memset, num[:, 2:3], 1.0)
    prog.loop_while(EXTRA, limit, extra_block)


def moe(K, A):
    nc, V = K.nc, K.DVE
    modulated_norm(K, "norm_ffn_g", 24, 32, K.u)
    K.new_phase()
    score, chosen = K.carve(NT, E_ALL), K.carve(NT, E_ALL)
    kept = K.big_at
    stored = K.store_rows(K.u, K.u_rows)
    router(K, A["w_router"][0], A["router_bias"][0], score, chosen)
    K.new_phase(kept, stored)
    experts(K, A, score, chosen, K.u_rows, K.total_rows)
    for t in range(NT):
        s = K.wring.take()
        m = K.SP.dma(s, s[:, 0:D], K.total_rows[t * P:(t + 1) * P, :], after=s.free)
        for half in range(2):
            b = K.bank()
            m1 = K.transposes([(b[:, j * P:(j + 1) * P], s[:, (4 * half + j) * P:(4 * half + j + 1) * P])
                               for j in range(4)], b, after=m)
            b4 = b[:, :].rearrange("p (a b) -> p a b", b=P)
            sq = K.sq_ring.take()
            sq4 = sq[:, :].rearrange("p (a b) -> p a b", b=P)
            hh = K.h[:, 4 * half:4 * half + 4, t * P:(t + 1) * P]
            m2 = V.run(nc.vector.tensor_tensor, sq4, b4,
                       K.mod[:, 40 + 4 * half:44 + 4 * half].unsqueeze(2).to_broadcast([P, 4, P]), ALU.mult, after=[m1, sq.free])
            b.free = [m2]
            m2 = V.run(nc.vector.tensor_tensor, hh, hh, sq4, ALU.add)
            sq.free = [m2]
        s.free = [m1]
    K.new_phase()
    K.rms([K.h[:, k, :] for k in range(KD)], D, 1e-6, after=V.count.mark())
    K.scaled(K.h, [K.h[:, k, :] for k in range(KD)], K.col("final_norm_g"))
    K.new_phase()
HEAD = 64
R_, K_, V_, G_, W_, A_ = range(6)


def rwkv_inputs(K, A, scratch):
    nc, V, S, prog = K.nc, K.DVE, K.ACT, K.prog
    m = K.rms([K.h[:, k, :] for k in range(KD)], D, 1e-6, after=V.count.mark())
    K.scaled(K.u, [K.h[:, k, :] for k in range(KD)], K.columns[:, K.cols["norm_pre"][0]:K.cols["norm_pre"][0] + KD])
    dx = K.carve(KD, T)
    V.run(nc.vector.tensor_tensor, dx[:, :, 1:T], K.u[:, :, 0:T - 1], K.u[:, :, 1:T], ALU.subtract)
    V.run(nc.vector.tensor_scalar, dx[:, :, 0:1], K.u[:, :, 0:1], -1.0, None, ALU.mult)
    mix = [Slot(prog, K.carve(KD, T)) for _ in range(2)]
    out = Ring(prog, [Slot(prog, K.carve(T), f"rwkv_out{n}") for n in range(4)])
    small = Slot(prog, K.carve(T))
    mu = K.cols["a_mu"][0]

    def mixed(slot, c):
        for k in range(KD):
            m = V.run(nc.vector.scalar_tensor_tensor, slot[:, k, :], dx[:, k, :], K.columns[:, ds(mu + c * KD + k, 1)],
                      K.u[:, k, :], ALU.mult, ALU.add, after=slot.free)
        return m

    def two(i):
        for n in range(2):
            c, x = 2 * i + n, mix[n]
            m_x = mixed(x, c)
            wv = A["a_w_in_2"][0].rearrange("c k n -> (c k) n")[ds(c * D, D), :].rearrange("(k p) n -> p k n", p=P)
            for q in range(4):
                s, w, m_w = K.weights(wv[:, :, q * 256:(q + 1) * 256], None)
                for j in range(2):
                    b, m = K.project(w, j, x.t, m_in=[m_w, m_x])
                    s.free = x.free = [m]
                    o = out.take()
                    m = S.run(nc.scalar.activation, o[:, :], b[:, :], ACT.Copy, after=[m, o.free])
                    b.free = [m]
                    o.free = [S.dma(o, scratch[2 * q + j].rearrange("p w t -> w p t")[ds(c, 1)]
                                       .rearrange("w p t -> (w p) t"), o.t, after=m)]

    prog.loop(2, two)
    for which, w1, w2, bias, func in ((W_, "a_w1_2", "a_w2_2", "w0", ACT.Tanh), (A_, "a_a1_2", "a_a2_2", "a0", ACT.Copy)):
        x = mix[which % 2]
        m_x = mixed(x, which)
        s, w, m_w = K.weights(A[w1][0].rearrange("(k p) n -> p k n", p=P), None)
        b = K.bank()
        m = K.matmuls(b[0:HEAD, :], [(w[:, k, :], x[:, k, :]) for k in range(KD)], after=[m_w, m_x, b.free])
        s.free = x.free = [m]
        m_s = S.run(nc.scalar.activation, small[0:HEAD, :], b[0:HEAD, :], func, after=[m, small.free])
        b.free = [m_s]
        s = K.wring.take()
        m_w = K.SP.dma(s, s[0:HEAD, 0:D], A[w2][0], after=s.free)
        for j in range(KD):
            b = K.bank()
            m = K.matmuls(b[:, :], [(s[0:HEAD, j * P:(j + 1) * P], small[0:HEAD, :])], after=[m_w, m_s, b.free])
            s.free = small.free = [m]
            o = out.take()
            m = S.run(nc.scalar.activation, o[:, :], b[:, :], ACT.Sigmoid, bias=K.col(bias, j), after=[m, o.free])
            b.free = [m]
            o.free = [S.dma(o, scratch[j, :, which, :], o.t, after=m)]
    return [o.count.mark() for o in out.slots]


def rwkv_pairs(K, scratch, y_out):
    nc, V, S, prog = K.nc, K.DVE, K.ACT, K.prog
    ts, tt, stt = nc.vector.tensor_scalar, nc.vector.tensor_tensor, nc.vector.scalar_tensor_tensor
    act, cp = nc.scalar.activation, nc.vector.tensor_copy
    K.fetch("same_head", "neg_up16", "neg_low16", "neg_off16", "neg_off32", "up64", "upeq64", "scan64", "head_cols")
    ins = Ring(prog, [Slot(prog, K.carve(6, T), f"pair{n}_in") for n in range(2)])
    names = "L Em Ep En kk k2 al0 al1 be ka rh rh0 rh1 rkr vt kat bet al0t al1t TaT X2 Wv nU yt yf dv lw gs"
    buf = {n: K.carve(T) for n in names.split()}
    St, SP_, St2 = K.carve(P), K.carve(P), K.carve(P)
    pcol = K.carve(16)
    spare = [K.wslots[n][:, T * q:T * (q + 1)] for n in range(6) for q in range(4)]
    mats = {}
    for h in range(2):
        for n in "M MT N NT X O16 O32 ak qb qk G".split():
            mats[n, h] = spare.pop()
    tile = lambda a, t: a[:, t * P:(t + 1) * P]
    tiles = lambda a: a.rearrange("p (t n) -> p t n", n=P)
    wide = lambda name: K.c(name).unsqueeze(1).to_broadcast([P, NT, P])
    col = lambda name, p: K.columns[:, ds(K.cols[name][0] + p, 1)]
    B = buf

    def mm_tiles(pairs, after):
        b = K.bank()
        for t in range(NT):
            m = K.PE.run(nc.tensor.matmul, b[:, t * P:(t + 1) * P], tile(pairs[0], t), tile(pairs[1], t), start=True,
                         stop=True, after=[after, b.free] if t == 0 else (), counted=t == NT - 1)
        b.free = []
        return b, m

    def body(i):
        for n in range(2):
            pair(2 * i + n)

    def pair(p):
        prog.join(V, S)
        x = ins.take()
        m_in = K.SP.dma(x, x.t.rearrange("p w t -> p (w t)"), scratch.rearrange("c p w t -> (c p) (w t)")[ds(p * P, P), :],
                        after=x.free)
        r, k, v, g, sg, a = (x[:, n, :] for n in range(6))
        for n, name in enumerate(("k_k", "k_a", "r_k", "lnx_g", "lnx_b")):
            V.run(cp, pcol[:, n:n + 1], col(name, p))
        V.run(ts, pcol[:, 5:6], pcol[:, 1:2], -1.0, 1.0, ALU.mult, ALU.add)
        V.run(ts, B["lw"], sg, -float(np.exp(-0.5)), None, ALU.mult, after=m_in)
        m = V.run(nc.vector.tensor_tensor_scan, B["L"], K.c("scan64"), B["lw"], 0.0, ALU.mult, ALU.add)
        m1 = V.run(tt, B["Em"], B["L"], B["lw"], ALU.subtract)
        S.run(act, B["Ep"], B["L"], ACT.Exp, after=m)
        S.run(act, B["En"], B["L"], ACT.Exp, scale=-1.0)
        m_e = S.run(act, B["Em"], B["Em"], ACT.Exp, after=m1)
        m = V.run(ts, B["kk"], k, pcol[:, 0:1], None, ALU.mult)
        m = V.run(tt, B["dv"], B["kk"], B["kk"], ALU.mult)
        b = K.bank()
        m = K.matmuls(b[:, :], [(K.c("same_head"), B["dv"])], after=[m, b.free])
        m = S.run(act, B["gs"], b[:, :], ACT.Sqrt, after=m)
        b.free = [m]
        V.run(ts, B["gs"], B["gs"], 1e-12, None, ALU.max, after=m)
        V.run(nc.vector.reciprocal, B["gs"], B["gs"])
        V.run(tt, B["kk"], B["kk"], B["gs"], ALU.mult)
        V.run(ts, B["k2"], a, pcol[:, 1:2], pcol[:, 5:6], ALU.mult, ALU.add)
        V.run(tt, B["k2"], B["k2"], k, ALU.mult)
        V.run(tt, B["be"], B["kk"], a, ALU.mult, after=m_e)
        V.run(tt, B["be"], B["be"], B["En"], ALU.mult)
        V.run(tt, B["ka"], B["k2"], B["En"], ALU.mult)
        V.run(tt, B["rh"], r, B["Ep"], ALU.mult)
        for h in range(2):
            hc = K.c("head_cols")[:, h:h + 1]
            V.run(stt, B[f"al{h}"], B["kk"], hc, B["Em"], ALU.mult, ALU.mult)
            V.run(ts, B[f"rh{h}"], B["rh"], hc, None, ALU.mult)
        m = V.run(stt, B["rkr"], r, pcol[:, 2:3], B["k2"], ALU.mult, ALU.mult)
        b = K.bank()
        m1 = K.matmuls(b[:, :], [(K.c("same_head"), B["rkr"])], after=[m, b.free])
        m1 = V.run(tt, B["rkr"], b[:, :], v, ALU.mult, after=m1)
        b.free = [m1]
        for src, dst in ((v, "vt"), (B["ka"], "kat"), (B["be"], "bet"), (B["al0"], "al0t"), (B["al1"], "al1t")):
            b = K.bank()
            m1 = K.transposes([(b[:, t * P:(t + 1) * P], tile(src, t)) for t in range(NT)], b, after=m)
            m_t = S.run(act, B[dst], b[:, :], ACT.Copy, after=m1)
            b.free = [m_t]
        for h in range(2):
            al, rh = B[f"al{h}"], B[f"rh{h}"]
            for lhs, rhs, outs in ((B["be"], al, [("M", "neg_up16")]),
                                   (al, B["be"], [("MT", "neg_low16"), ("O16", "neg_off16"), ("O32", "neg_off32")]),
                                   (B["ka"], al, [("ak", "up64")]),
                                   (B["be"], rh, [("qb", "upeq64")]), (B["ka"], rh, [("qk", "upeq64")])):
                b, m1 = mm_tiles((lhs, rhs), m)
                for n, mask in outs:
                    m2 = V.run(tt, tiles(mats[n, h]), tiles(b[:, :]), wide(mask), ALU.mult, after=m1)
                b.free = [m2]
            m_A = V.run(tt, tiles(mats["X", h]), tiles(mats["M", h]), wide("ident"), ALU.add)

        def copy_out(dst, pairs, after):
            b, m1 = mm_tiles(pairs, after)
            m2 = S.run(act, dst, b[:, :], ACT.Copy, after=m1)
            b.free = [m2]
            return m2

        def add_to_X(h, pairs, after):
            b, m1 = mm_tiles(pairs, after)
            m2 = V.run(tt, mats["X", h], mats["X", h], b[:, :], ALU.add, after=m1)
            b.free = [m2]
            return m2

        m_sq, m_X = [m_A, m_A], [m_A, m_A]
        for step in range(3):
            src, dst = (("M", "MT"), ("N", "NT")) if step % 2 == 0 else (("N", "NT"), ("M", "MT"))
            for h in range(2):
                M, MT = mats[src[0], h], mats[src[1], h]
                if step < 2:
                    copy_out(mats[dst[0], h], (MT, M), [m_sq[h], m_X[h]])
                m_sq[h] = copy_out(mats[dst[1], h], (M, MT), [m_sq[h], m_X[h]])
            for h in range(2):
                m_X[h] = add_to_X(h, (mats[dst[1], h], mats["X", h]), [m_sq[h], m_X[h]])
        for off in ("O16", "O32"):
            m_G = [None, None]
            for h in range(2):
                b = K.bank()
                m1 = K.transposes([(b[:, t * P:(t + 1) * P], tile(mats["X", h], t)) for t in range(NT)], b, after=m_X[h])
                m1 = S.run(act, mats["N", h], b[:, :], ACT.Copy, after=m1)
                b.free = [m1]
                m_G[h] = copy_out(mats["G", h], (mats[off, h], mats["X", h]), m_X[h])
            for h in range(2):
                m_X[h] = add_to_X(h, (mats["N", h], mats["G", h]), m_G[h])
        hs = lambda arr, t, h: arr[:, t * P + h * HEAD:t * P + (h + 1) * HEAD]

        def by_head(dst, mat, rhs, after, engine):
            b = K.bank()
            for t in range(NT):
                for h in range(2):
                    m1 = K.PE.run(nc.tensor.matmul, hs(b, t, h), tile(mats[mat, h], t), hs(rhs, t, h), start=True,
                                  stop=True, after=[after, b.free] if t + h == 0 else (), counted=t == NT - 1 and h == 1)
            m2 = S.run(act, dst, b[:, :], ACT.Copy, after=m1)
            b.free = [m2]
            return m2

        m1 = by_head(B["X2"], "ak", B["vt"], [m_t, m_A], S)
        m_W = by_head(B["Wv"], "X", B["X2"], [m1, m_X], S)
        b = K.bank()
        for t in range(NT):
            m1 = K.matmuls(b[:, t * P:(t + 1) * P], [(tile(B[f"al{h}t"], t), tile(mats["X", h], t)) for h in range(2)],
                           after=[m_t, m_X, b.free if t == 0 else ()])
        m1 = S.run(act, B["TaT"], b[:, :], ACT.Copy, after=m1)
        b.free = [m1]
        m_S = V.run(nc.vector.memset, St, 0.0)
        for c in range(T // HEAD):
            t, q = c // 2, c % 2
            rows = slice(HEAD * q, HEAD * q + HEAD)
            b = K.bank()
            K.PE.run(nc.tensor.matmul, b[:, 0:P], tile(B["TaT"], t), St, start=True, stop=True,
                     after=[m1, m_S, b.free], counted=False)
            m2 = K.PE.run(nc.tensor.matmul, b[:, P:2 * P], tile(B["rh"], t), St, start=True, stop=True)
            m_U = V.run(stt, tile(B["nU"], t)[rows], b[rows, 0:P], -1.0, tile(B["Wv"], t)[rows], ALU.mult, ALU.subtract,
                        after=[m2, m_W])
            m3 = V.run(cp, tile(B["yt"], t)[rows], b[rows, P:2 * P])
            b.free = [m3]
            if c == T // HEAD - 1:
                break
            end = B["Ep"][:, HEAD * c + HEAD - 1:HEAD * c + HEAD]
            V.run(ts, SP_, St, end, None, ALU.mult)
            b = K.bank()
            m2 = K.matmuls(b[:, 0:P], [(tile(B["bet"], t)[rows], tile(B["nU"], t)[rows]),
                                       (tile(B["kat"], t)[rows], tile(B["vt"], t)[rows])], after=[m_U, b.free])
            m3 = V.run(stt, St2, b[:, 0:P], end, K.c("same_head"), ALU.mult, ALU.mult, after=m2)
            b.free = [m3]
            m_S = V.run(tt, St, St2, SP_, ALU.add)
        b = K.bank()
        for t in range(NT):
            for h in range(2):
                m2 = K.matmuls(hs(b, t, h), [(tile(mats["qb", h], t), hs(B["nU"], t, h)),
                                             (tile(mats["qk", h], t), hs(B["vt"], t, h))],
                               after=[m_U, b.free if t + h == 0 else ()])
        m2 = V.run(tt, B["yt"], B["yt"], b[:, :], ALU.add, after=m2)
        b.free = [m2]
        b = K.bank()
        m2 = K.transposes([(b[:, t * P:(t + 1) * P], tile(B["yt"], t)) for t in range(NT)], b, after=m2)
        m2 = V.run(cp, B["yf"], b[:, :], after=m2)
        b.free = [m2]
        b = K.bank()
        m2 = K.matmuls(b[:, :], [(K.c("same_head"), B["yf"])], after=[m2, b.free])
        m2 = V.run(stt, B["dv"], b[:, :], -1.0 / HEAD, B["yf"], ALU.mult, ALU.add, after=m2)
        b.free = [m2]
        m2 = S.run(act, B["yf"], B["dv"], ACT.Square, after=m2)
        b = K.bank()
        m2 = K.matmuls(b[:, :], [(K.c("same_head"), B["yf"])], after=[m2, b.free])
        m2 = V.run(ts, B["gs"], b[:, :], 1.0 / HEAD, 64e-5, ALU.mult, ALU.add, after=m2)
        b.free = [m2]
        m2 = S.run(act, B["gs"], B["gs"], ACT.Sqrt, after=m2)
        m3 = S.run(act, B["yf"], g, ACT.Silu)
        V.run(nc.vector.reciprocal, B["gs"], B["gs"], after=m2)
        V.run(tt, B["dv"], B["dv"], B["gs"], ALU.mult)
        V.run(ts, B["dv"], B["dv"], pcol[:, 3:4], pcol[:, 4:5], ALU.mult, ALU.add)
        V.run(tt, B["dv"], B["dv"], B["rkr"], ALU.add)
        m2 = V.run(tt, y_out[:, ds(p, 1), :], B["dv"].unsqueeze(1), B["yf"].unsqueeze(1), ALU.mult, after=m3)
        x.free = [m2]

    prog.loop(KD // 2, body)


def columns_of(K, name, n):
    a = K.cols[name][0] + n * KD
    return K.columns[:, a:a + KD]


def post_and_ple(K, A, n, w_out, src):
    nc, V, S, prog = K.nc, K.DVE, K.ACT, K.prog
    stt, tt = nc.vector.scalar_tensor_tensor, nc.vector.tensor_tensor
    out = K.carve(KD, T)
    pT = K.carve(2, T)
    sig = Ring(prog, [Slot(prog, K.carve(T)) for _ in range(2)])
    p_in = A["p_2"][n, 0]
    s = K.wring.take()
    m = K.SP.dma(s, s[:, 0:4 * 256].rearrange("p (t d) -> p t d", d=256), p_in.rearrange("(t p) d -> p t d", p=P),
                 after=s.free)
    for j in range(2):
        b = K.bank()
        m1 = K.transposes([(b[:, t * P:(t + 1) * P], s[:, t * 256 + j * P:t * 256 + (j + 1) * P]) for t in range(NT)], b,
                          after=m)
        m1 = V.run(nc.vector.tensor_copy, pT[:, j, :], b[:, :], after=m1)
        b.free = [m1]
    s.free = [m1]
    wv = w_out.rearrange("(k p) n -> p k n", p=P)

    def add_normed(gains):
        K.rms([out[:, k, :] for k in range(KD)], D, 1e-6, after=[V.count.mark(), S.count.mark()])
        for k in range(KD):
            V.run(tt, out[:, k, :], out[:, k, :], K.rstd[:, :], ALU.mult)
            V.run(stt, K.h[:, k, :], out[:, k, :], gains[:, k:k + 1], K.h[:, k, :], ALU.mult, ALU.add)

    prog.phase()

    for i in range(KD // 2):
        s, w, m_w = K.weights(wv[:, :, ds(i * 256, 256)], None)
        for j in range(2):
            b, m = K.project(w, j, src, m_in=m_w)
            s.free = [m]
            m = S.run(nc.scalar.activation, out[:, ds(2 * i + j, 1), :], b[:, :].unsqueeze(1), ACT.Copy, after=m)
            b.free = [m]

    add_normed(columns_of(K, "norm_post", n))
    prog.phase()
    pgv = A["ple_gate_2"][n].rearrange("(k p) n -> p k n", p=P)
    pwv = A["ple_w_2"][n].rearrange("(k p) n -> p k n", p=P)

    s2, w2, m_w2 = K.weights(pwv, None, rows=2)
    for i in range(KD // 2):
        s, w, m_w = K.weights(pgv[:, :, ds(i * 256, 256)], None)
        for j in range(2):
            b, m = K.project(w, j, K.h, m_in=m_w)
            b2, m2 = K.project(w2, 2 * i + j, pT, k=2, m_in=m_w2)
            s.free, s2.free = [m], [m2]
            a = sig.take()
            m = S.run(nc.scalar.activation, a[:, :], b[:, :], ACT.Sigmoid, after=[m, a.free])
            b.free = [m]
            m = V.run(tt, out[:, ds(2 * i + j, 1), :], a[:, :].unsqueeze(1), b2[:, :].unsqueeze(1), ALU.mult, after=[m, m2])
            b2.free = a.free = [m]

    add_normed(columns_of(K, "ple_norm", n))
    K.new_phase()


LAM_INIT = 0.8 - 0.6 * float(np.exp(-0.3))


def attention(K, A, o_out):
    nc, V, S, prog = K.nc, K.DVE, K.ACT, K.prog
    ts, tt, stt = nc.vector.tensor_scalar, nc.vector.tensor_tensor, nc.vector.scalar_tensor_tensor
    act, cp = nc.scalar.activation, nc.vector.tensor_copy
    K.fetch("cos", "sin", "turn", "future")
    hk = K.carve(KD, T)
    chunks = [K.h[:, k, :] for k in range(KD)]
    K.rms(chunks, D, 1e-6, after=V.count.mark())
    K.scaled(K.u, chunks, columns_of(K, "norm_pre", 1))
    K.scaled(hk, chunks, columns_of(K, "kv_norm", 0))
    lq = K.carve(4, HEAD)
    lam = K.carve(8)
    m = S.dma(prog.arrivals("lambda"), lq.rearrange("p a d -> p (a d)"),
                 A["b_lambda_2"][0].rearrange("a d -> (a d)").partition_broadcast(P))
    V.run(tt, lq[:, 0:2, :], lq[:, 0:4:2, :], lq[:, 1:4:2, :], ALU.mult, after=m)
    m = V.run(nc.vector.tensor_reduce, lam[:, 0:2], lq[:, 0:2, :], AX.X, ALU.add)
    m = S.run(act, lam[:, 0:2], lam[:, 0:2], ACT.Exp, after=m)
    V.run(tt, lam[:, 2:3], lam[:, 1:2], lam[:, 0:1], ALU.subtract, after=m)
    V.run(ts, lam[:, 2:3], lam[:, 2:3], LAM_INIT, None, ALU.subtract)
    V.run(ts, lam[:, 3:4], K.col("subln"), 1.0 - LAM_INIT, None, ALU.mult)
    q, k, qr = K.carve(T), K.carve(T), K.carve(T)
    vtok, gate, of = K.carve(T), K.carve(T), K.carve(T)
    probs = [Slot(prog, K.carve(T)) for _ in range(4)]
    pT = [Slot(prog, K.carve(T)) for _ in range(2)]
    st = K.carve(4, 2, 4)
    prog.phase()
    qv = A["b_w_in_2"][0].rearrange("(k p) n -> p k n", p=P)
    kv = A["kv_w_2"].rearrange("(k p) n -> p k n", p=P)

    def head(h):
        prog.join(V, S)
        slots = [K.wring.take(), K.wring.take()]
        w, m_w = [], []
        for s, v in zip(slots, (qv, kv)):
            w.append(s[:, :].rearrange("p (a k n) -> p a k n", a=2, k=KD))
            K.SP.dma(s, w[-1][:, 0], v[:, :, ds(h * P, P)], after=s.free)
            m_w.append(K.SP.dma(s, w[-1][:, 1], v[:, :, ds(D + h * P, P)]))
        for dst, wi, src, scale in ((q, w[0], K.u, HEAD ** -0.5), (k, w[1], hk, 1.0)):
            b, m = K.project(wi[:, 0], 0, src, m_in=m_w)
            m = S.run(act, dst, b[:, :], ACT.Copy, scale=scale, after=m)
            b.free = [m]
            b = K.bank()
            m = K.matmuls(b[:, :], [(K.c("turn"), dst)], after=[m, b.free])
            V.run(tt, qr, b[:, :], K.c("sin"), ALU.mult, after=m)
            b.free = [V.count.mark()]
            V.run(tt, dst, dst, K.c("cos"), ALU.mult)
            m_qk = V.run(tt, dst, dst, qr, ALU.add)
        b, m = K.project(w[0][:, 1], 0, K.u)
        slots[0].free = [m]
        m_g = S.run(act, gate, b[:, :], ACT.Silu, after=m)
        b.free = [m_g]
        b = K.bank()
        for t in range(NT):
            m = K.matmuls(b[:, t * P:(t + 1) * P], [(hk[:, i, t * P:(t + 1) * P], w[1][:, 1, i, :]) for i in range(KD)],
                          after=b.free if t == 0 else ())
        slots[1].free = [m]
        m_v = S.run(act, vtok, b[:, :], ACT.Copy, after=m)
        b.free = [m_v]
        ob = K.bank()
        for qb in range(NT):
            n = (qb + 1) * P
            pr = probs[2 * (qb % 2):2 * (qb % 2) + 2]
            for c in range(2):
                rows = slice(HEAD * c, HEAD * c + HEAD)
                b = K.bank()
                if b is ob:
                    b = K.bank()
                m = K.matmuls(b[:, 0:n], [(q[rows, qb * P:n], k[rows, 0:n])], after=[m_qk, b.free])
                m = V.run(tt, b[:, qb * P:n], b[:, qb * P:n], K.c("future"), ALU.add, after=m)
                m = V.run(nc.vector.tensor_reduce, st[:, qb, c, 0:1], b[:, 0:n], AX.X, ALU.max, negate=True)
                m = S.run(act, pr[c][:, 0:n], b[:, 0:n], ACT.Exp, bias=st[:, qb, c, 0:1], accum_out=st[:, qb, c, 1:2],
                          after=[m, pr[c].free])
                b.free = [m]
            V.run(nc.vector.reciprocal, st[:, qb, :, 2:3], st[:, qb, :, 1:2], after=m)
            V.run(tt, st[:, qb, 1, 3:4], st[:, qb, 1, 2:3], lam[:, 2:3], ALU.mult)
            V.run(ts, pr[0][:, 0:n], pr[0][:, 0:n], st[:, qb, 0, 2:3], None, ALU.mult)
            m = V.run(stt, pr[0][:, 0:n], pr[1][:, 0:n], st[:, qb, 1, 3:4], pr[0][:, 0:n], ALU.mult, ALU.add)
            b = K.bank()
            if b is ob:
                b = K.bank()
            m = K.transposes([(b[:, kb * P:(kb + 1) * P], pr[0][:, kb * P:(kb + 1) * P]) for kb in range(qb + 1)], b,
                             after=m)
            pr[0].free = pr[1].free = [m]
            pt = pT[qb % 2]
            m = S.run(act, pt[:, 0:n], b[:, 0:n], ACT.Copy, after=[m, pt.free])
            b.free = [m]
            m = K.matmuls(ob[:, qb * P:n], [(vtok[:, kb * P:(kb + 1) * P], pt[:, kb * P:(kb + 1) * P])
                                            for kb in range(qb + 1)], after=[m, m_v, ob.free if qb == 0 else ()])
            pt.free = [m]
        m = V.run(cp, of, ob[:, :], after=m)
        ob.free = [m]
        m = S.run(act, qr, of, ACT.Square, after=m)
        b = K.bank()
        m = K.matmuls(b[:, :], [(K.c("ones"), qr)], after=[m, b.free])
        m = V.run(ts, qr, b[:, :], 1.0 / P, 1e-5, ALU.mult, ALU.add, after=m)
        b.free = [m]
        m = S.run(act, qr, qr, ACT.Sqrt, after=m)
        V.run(nc.vector.reciprocal, qr, qr, after=m)
        V.run(tt, of, of, qr, ALU.mult)
        V.run(stt, o_out[:, ds(h, 1), :], of.unsqueeze(1), lam[:, 3:4], gate.unsqueeze(1), ALU.mult, ALU.mult, after=m_g)

    prog.loop(KD, head)
    K.prog.phase()


def block2(K, A, scratch):
    inputs_stored = rwkv_inputs(K, A, scratch)
    K.new_phase()
    K.prog.join(K.SP)
    K.SP.wait(inputs_stored)
    rwkv_pairs(K, scratch, K.u)
    K.new_phase()
    for s in K.wslots:
        s.free = [e.count.mark() for e in (K.PE, K.ACT, K.DVE)]
    post_and_ple(K, A, 0, A["a_w_out_2"][0], K.u)
    o_out = K.carve(KD, T)
    attention(K, A, o_out)
    K.big_at = KD * T
    post_and_ple(K, A, 1, A["b_w_out_2"][0], o_out)
def block1_mixer(K, A):
    r = lambda a: a.rearrange("(k p) -> k p", p=P)
    adaln(K, A["w_ada"][0])
    K.new_phase()
    modulated_norm(K, "norm_mix_g", 0, 8, K.u)
    K.new_phase()
    w_in = A["w_in"][0]
    K.fetch("upper")
    K.big_const = K.big_at
    y = K.carve(16, T)
    K.y_ssd = y
    keep_y = K.big_at
    ssd_decays(K, w_in, A["dt_bias"][0], A["A_log"][0], K.cs_dram, None)
    K.new_phase(K.kept_ssd, K.m_cs)
    ssd_groups(K, w_in, K.cs_dram, A["D_skip"][0], y)
    K.new_phase(keep_y)
    K.fetch("inv2", "inv4", "inv8", "inv16")
    used = K.big_at
    pooled = K.carve(KD, T)
    merged = K.carve(KD, T)
    pool_branch(K, w_in, A["pool_w"][0], pooled)
    K.prog.phase()
    K.big_at = used + 16 * T
    combine(K, w_in, A["w_br_ssd"][0], A["w_br_pool"][0], A["w_out"][0], y, pooled, merged)
    K.new_phase()


def vector_list(A):
    f = lambda a: a.rearrange("(k p) -> k p", p=P)
    f2 = lambda a: a.rearrange("i (k p) -> (i k) p", p=P)
    names = [("conv_w", f2(A["conv_w"][0])), ("conv_b", f(A["conv_b"][0])), ("ssd_norm_g", f(A["ssd_norm_g"][0])),
             ("b_ada", f(A["b_ada"][0])), ("c", f2(A["c"])), ("norm_mix_g", f(A["norm_mix_g"][0])),
             ("norm_ffn_g", f(A["norm_ffn_g"][0])), ("final_norm_g", f(A["final_norm_g"])),
             ("pool_scale", f(A["pool_scale"][0]))]
    names += [("a_mu", A["a_mu_2"][0].rearrange("i (k p) -> (i k) p", p=P)),
              ("norm_pre", f2(A["norm_pre_2"])), ("norm_post", f2(A["norm_post_2"])), ("ple_norm", f2(A["ple_norm_2"])),
              ("kv_norm", f(A["kv_norm_2"])), ("subln", f2(A["b_subln_2"]))]
    names += [(n, f(A[f"a_{n}_2"][0])) for n in ("w0", "a0", "k_k", "k_a", "lnx_g", "lnx_b")]
    names += [("r_k", A["a_r_k_2"][0].rearrange("(k a) n -> k (a n)", a=2))]
    return names


def build_program(nc, A, consts, out):
    K = Kernel(nc, consts)
    K.cs_dram = nc.dram_tensor("ssd_sums", [32, T], F32, kind="Internal").ap()
    K.u_rows = nc.dram_tensor("u_rows", [T, D], F32, kind="Internal").ap()
    K.total_rows = nc.dram_tensor("total_rows", [T + P, D], F32, kind="Internal").ap()
    rwkv_dram = nc.dram_tensor("rwkv_inputs", [KD, P, 6, T], F32, kind="Internal").ap()
    K.prog.start()
    K.fetch("ident", "ones")
    K.load_columns(vector_list(A))
    K.load_x(A["x"][0])
    K.prog.phase()
    block1_mixer(K, A)
    moe(K, A)
    block2(K, A, rwkv_dram)
    K.SP.wait(K.store_rows(K.h, out[0]))


def kernel(**inputs):
    import concourse.bacc as bacc
    from concourse.bass_utils import run_bass_kernel_spmd

    nc = bacc.Bacc("TRN2", target_bir_lowering=False, num_devices=1)
    arrays, A = {}, {}
    for name, value in inputs.items():
        arrays[f"in_{name}"] = np.ascontiguousarray(value)
        A[name] = nc.dram_tensor(f"in_{name}", arrays[f"in_{name}"].shape, F32, kind="ExternalInput").ap()
    arrays["shape_consts"] = const_table()
    consts = nc.dram_tensor("shape_consts", arrays["shape_consts"].shape, F32, kind="ExternalInput").ap()
    out = nc.dram_tensor("out_h", (1, T, D), F32, kind="ExternalOutput").ap()
    build_program(nc, A, consts, out)
    r = run_bass_kernel_spmd(nc, [arrays], core_ids=[0])
    return r.results[0]["out_h"]
```

```python
import numpy as np
import concourse.bass as bass
from concourse import mybir

F32 = mybir.dt.float32
ALU = mybir.AluOpType
ACT = mybir.ActivationFunctionType
AX = mybir.AxisListType
ds = bass.ds

P = 128
FIRST = 4096


class Mark:

    def __init__(self, count, n, loop=None, shift=0):
        self.count, self.n, self.loop, self.shift = count, n, loop, shift


class Count:

    def __init__(self, prog, name, first=FIRST):
        self.prog, self.sem, self.first = prog, prog.nc.alloc_semaphore(name), first
        self.n, self.start, self.per = 0, first, 0
        if prog.begun and first:
            prog.nc.sync.sem_inc(self.sem, first)
        prog.counts.append(self)

    def add(self, ins, by):
        self.n += by
        if ins is not None:
            ins.then_inc(self.sem, by)
        return self.mark()

    def mark(self):
        if self.prog.in_loop is None:
            return Mark(self, self.start + self.n)
        return Mark(self, self.n, self.prog.in_loop)

    def used(self):
        return self.start + self.n > self.first or self.prog.in_loop is not None

    def value(self, mark):
        if mark.loop is None:
            return mark.n
        assert mark.loop == self.prog.in_loop
        return (self.start - mark.shift * self.per + mark.n) + self.prog.iteration * self.per


def flat(marks):
    for m in marks:
        if isinstance(m, (list, tuple)):
            yield from flat(m)
        elif m is not None:
            yield m


class Lane:

    def __init__(self, prog, eng, name):
        self.prog, self.eng, self.count = prog, eng, Count(prog, f"{name}_done")
        prog.lanes.append(self)

    def wait(self, *marks):
        last = {}
        for m in flat(marks):
            place = (m.count, m.loop is not None)
            if place not in last or (-m.shift, m.n) > (-last[place].shift, last[place].n):
                last[place] = m
        for m in last.values():
            if not self.prog.dry:
                self.eng.wait_ge(m.count.sem, m.count.value(m))
                if self in (self.prog.sp, self.prog.pool) and m.loop is not None:
                    self.eng.sem_inc(self.prog.waits_alone, 1)

    def run(self, fn, *args, after=(), counted=True, **kw):
        self.wait(after, self.count.mark() if self is not self.prog.pe and self.count.used() else ())
        if self.prog.dry:
            return self.count.add(None, 1) if counted else None
        ins = fn(*args, **kw)
        return self.count.add(ins, 1) if counted else None

    def dma(self, slot, out, in_, after=()):
        self.wait(after)
        if not self.prog.dry:
            return slot.count.add(self.eng.dma_start(out, in_), 16)
        return slot.count.add(None, 16)


    def indirect(self, slot, fn, *args, **kw):
        return slot.count.add(None if self.prog.dry else fn(*args, **kw), 16)


class Slot:

    def __init__(self, prog, tensor, name=None, first=FIRST):
        self.t, self.free = tensor, []
        self.count = Count(prog, name, first) if name else None
        prog.slots.append(self)

    def __getitem__(self, key):
        return self.t[key]


class Ring:
    def __init__(self, prog, slots):
        self.slots, self.at = slots, 0
        prog.rings.append(self)

    def take(self, n=1):
        if self.at + n > len(self.slots):
            self.at = 0
        got = self.slots[self.at:self.at + n]
        self.at += n
        return got[0] if n == 1 else got


class Program:
    def __init__(self, nc):
        self.nc = nc
        self.counts, self.slots, self.rings, self.lanes = [], [], [], []
        self.in_loop, self.iteration, self.dry, self.loops = None, None, False, 0
        self.begun = False
        self.turn_sems, self.over = [], 0
        self.turns_over = nc.alloc_semaphore("turns_over")
        self.waits_alone = nc.alloc_semaphore("waits_alone")
        self.pe = None
        self.pe = Lane(self, nc.tensor, "pe")
        self.act = Lane(self, nc.scalar, "act")
        self.dve = Lane(self, nc.vector, "dve")
        self.pool = Lane(self, nc.gpsimd, "pool")
        self.sp = Lane(self, nc.sync, "sp")

    def arrivals(self, name):
        return Slot(self, None, f"{name}_{len(self.counts)}")

    def start(self):
        self.begun = True
        for c in self.counts:
            self.nc.sync.sem_inc(c.sem, FIRST)

    def fresh(self):
        for r in self.rings:
            r.at = 0

    def loop(self, times, body):
        self.fresh()
        for c in self.counts:
            c.start, c.n = c.start + c.n, 0
        before = [list(s.free) for s in self.slots]
        self.loops += 1
        self.in_loop, self.dry = self.loops, True
        body(0)
        self.dry = False
        for c in self.counts:
            c.per, c.n = c.n, 0
        for s, b in zip(self.slots, before):
            s.free = b + [Mark(m.count, m.n, m.loop, 1) for m in s.free if m.loop is not None]
        self.fresh()
        with self.nc.Fori(0, times) as i:
            self.iteration = i
            body(i)
        self.in_loop = self.iteration = None
        for c in self.counts:
            c.start += (times - 1) * c.per
        for s in self.slots:
            s.free = [m if m.loop is None else Mark(m.count, m.count.start + m.n)
                      for m in s.free if not m.shift]
        for c in self.counts:
            c.start, c.n, c.per = c.start + c.n, 0, 0
        self.fresh()

    def loop_while(self, times, limit, body):
        self.phase()
        self.join(self.sp)
        for s in self.slots:
            s.free = []
        kept = [(c, c.sem, c.start + c.n) for c in self.counts]
        self.loops += 1
        self.in_loop, self.dry = self.loops, True
        for c in self.counts:
            c.start, c.n = c.first, 0
        self.fresh()
        body(0)
        self.dry = False
        for c in self.counts:
            c.per, c.n = c.n, 0
            if c.per:
                c.sem = self.nc.alloc_semaphore(f"turns_{len(self.turn_sems)}")
                self.turn_sems.append(c.sem)
                if c.first:
                    self.nc.sync.sem_inc(c.sem, c.first)
        for s in self.slots:
            s.free = [Mark(m.count, m.n, m.loop, 1) for m in s.free]
        self.fresh()
        with self.nc.Fori(0, times) as i:
            with self.nc.If(i < limit):
                self.iteration = i
                body(i)
        self.in_loop = self.iteration = None
        for c, sem, start in kept:
            c.sem, c.start, c.n, c.per = sem, start, 0, 0
        for s in self.slots:
            s.free = []
        self.fresh()
        for lane in self.lanes:
            lane.eng.drain().then_inc(self.turns_over, 1)
        self.over += len(self.lanes)
        for lane in self.lanes:
            lane.eng.wait_ge(self.turns_over, self.over)

    def join(self, *lanes):
        marks = [e.count.mark() for e in (self.pe, self.act, self.dve, self.pool) if e.count.used()]
        for lane in lanes:
            lane.wait(marks)

    def phase(self, *stores):
        marks = [e.count.mark() for e in (self.pe, self.act, self.dve, self.pool) if e.count.used()]
        for lane in self.lanes:
            if lane is not self.sp:
                lane.wait(marks, stores)
T = 512
D = 1024
KD = D // P
NT = T // P
ROUTED_SCALE = 2.5

BIG = 28160

CONST_COLS = {}


def const_table():
    parts = []

    def put(name, a):
        a = np.asarray(a, np.float32)
        start = sum(x.shape[1] for x in parts)
        CONST_COLS[name] = (start, a.shape[1])
        parts.append(a)

    r, c = np.arange(P)[:, None], np.arange(P)[None, :]
    t = np.arange(T)
    wide = np.ones((P, 1))
    put("ident", r == c)
    put("ones", np.ones((P, P)))
    put("upper", r <= c)
    put("same_head", r // 64 == c // 64)
    put("neg_up16", -1.0 * ((r < c) & (r // 16 == c // 16)))
    put("neg_low16", -1.0 * ((r > c) & (r // 16 == c // 16)))
    for b in (16, 32):
        put(f"neg_off{b}", -1.0 * ((r // (2 * b) == c // (2 * b)) & (r // b > c // b)))
    put("up64", (r < c) & (r // 64 == c // 64))
    put("upeq64", (r <= c) & (r // 64 == c // 64))
    put("future", np.where(c > r, -1e30, 0.0))
    g = np.arange(8)
    put("before8", wide * (g[None, :] < g[:, None]).reshape(1, 64))
    put("before", r < c)
    put("slot_row", np.broadcast_to(c, (P, P)))
    put("expert_row", wide * np.arange(64)[None, :])
    put("token_and_one", np.stack([r[:, 0] + P * (i // 2) if i % 2 == 0 else r[:, 0] * 0 + 1 for i in range(8)], 1))
    put("spare_row", T + r + 0 * c[:, 0:2])
    put("scan128", wide * (t % 128 != 0)[None, :])
    put("scan64", wide * (t % 64 != 0)[None, :])
    for w in (2, 4, 8, 16):
        put(f"inv{w}", wide * (1.0 / np.minimum(t + 1, w))[None, :])
    inv = np.float32(500000.0) ** (-np.arange(0, 16, 2, dtype=np.float32) / np.float32(16))
    ang = t.astype(np.float32)[:, None] * inv[None, :]
    cos, sin, turn = np.ones((P, T)), np.zeros((P, T)), np.zeros((P, P))
    for comp in (0, 64):
        for j in range(8):
            for half in (0, 8):
                cos[comp + half + j] = np.cos(ang[:, j])
                sin[comp + half + j] = np.sin(ang[:, j])
            turn[comp + 8 + j, comp + j] = -1.0
            turn[comp + j, comp + 8 + j] = 1.0
    put("cos", cos)
    put("sin", sin)
    put("turn", turn)
    put("head_cols", np.stack([np.arange(P) < 64, np.arange(P) >= 64], 1))
    return np.concatenate(parts, axis=1)


class Kernel:

    def __init__(self, nc, consts):
        self.nc = nc
        self.prog = p = Program(nc)
        self.PE, self.ACT, self.DVE, self.POOL, self.SP = p.pe, p.act, p.dve, p.pool, p.sp
        self.sbuf_names = 0
        self.psum = nc.alloc_psum_tensor("psum_all", [P, 8, 512], F32)
        self.banks = [Slot(p, self.psum[:, b, :]) for b in range(8)]
        self.bank_ring = self.all_banks = Ring(p, self.banks)
        self.seven_banks = Ring(p, self.banks[:7])
        self.front_banks, self.back_banks = Ring(p, self.banks[:4]), Ring(p, self.banks[4:])
        self.wslots = [Slot(p, self.sb(f"weights{n}", [P, 2048]), f"weights{n}_in") for n in range(6)]
        self.wring = Ring(p, self.wslots)
        self.consts = consts
        self.const = self.sb("const_sb", [P, 2 * P])
        self.at_hand = {"ident": self.const[:, 0:P], "ones": self.const[:, P:2 * P]}
        self.h = self.sb("h", [P, KD, T])
        self.u = self.sb("u", [P, KD, T])
        self.big = self.sb("big", [P, BIG])
        self.sq = [Slot(p, self.sb(f"sq{n}", [P, T])) for n in range(2)]
        self.rstd = self.sb("rstd", [P, T])
        self.sq_ring = Ring(p, self.sq)
        self.stat = self.sb("stat", [P, 64])
        self.big_at = 0

    def sb(self, name, shape, dt=F32):
        return self.nc.alloc_sbuf_tensor(name, shape, dt)

    def c(self, name):
        return self.at_hand[name]

    def fetch(self, *names):
        arrive = self.prog.arrivals("const")
        for name in names:
            a, n = CONST_COLS[name]
            where = self.const[:, (0 if name == "ident" else P):(P if name == "ident" else 2 * P)] \
                if name in ("ident", "ones") else self.carve(n)
            self.at_hand[name] = where
            m = self.ACT.dma(arrive, where, self.consts[:, a:a + n])
        for lane in (self.PE, self.DVE, self.ACT):
            lane.wait(m)
        self.in_const = m

    def carve(self, *shape):
        n = int(np.prod(shape))
        a = self.big[:, self.big_at:self.big_at + n]
        self.big_at += n
        assert self.big_at <= BIG, self.big_at
        if len(shape) == 2:
            return a.rearrange("p (a b) -> p a b", b=shape[1])
        if len(shape) == 3:
            return a.rearrange("p (a b c) -> p a b c", b=shape[1], c=shape[2])
        return a

    def new_phase(self, keep=0, stores=()):
        self.prog.phase(stores)
        self.big_at = keep

    def bank(self, n=1):
        return self.bank_ring.take(n)

    def braid(self, back, front):
        streams = [(front, self.front_banks), (back, self.back_banks)]
        while streams:
            for s in list(streams):
                self.bank_ring = s[1]
                if s[0] is None or next(s[0], "over") == "over":
                    streams.remove(s)
        self.bank_ring = self.all_banks

    def pipeline(self, times, front, back, before=None):
        def step(g, n, more=True, ahead=True):
            start = self.step_start()
            self.braid(back(g, n, start, ahead), front(g + 1, 1 - n, start) if more else None)

        self.prog.fresh()
        self.braid(before, front(0, 0, self.step_start()))
        self.prog.loop(times // 2 - 1, lambda i: [step(2 * i + n, n) for n in range(2)])
        step(times - 2, 0, ahead=False)
        step(times - 1, 1, more=False, ahead=False)

    def step_start(self):
        self.prog.join(self.DVE, self.ACT)
        return [self.DVE.count.mark(), self.ACT.count.mark()]

    def weights(self, view, cols, rows=KD, slot=None, lane=None):
        slot = slot or self.wring.take()
        n = view.shape[-1]
        dst = slot[:, 0:rows * n].rearrange("p (k n) -> p k n", n=n)
        m = (lane or self.SP).dma(slot, dst, view, after=slot.free)
        slot.free = []
        return slot, dst, m

    def matmuls(self, out, terms, after=(), each=None):
        for n, (lhsT, rhs) in enumerate(terms):
            last = n == len(terms) - 1
            m = self.PE.run(self.nc.tensor.matmul, out, lhsT, rhs, start=n == 0, stop=last,
                            after=[after, each[n] if each else ()], counted=last)
            after = ()
        return m

    def project(self, w, j, src, k=KD, m_in=(), each=None):
        b = self.bank()
        m = self.matmuls(b[:, :], [(w[:, i, j * P:(j + 1) * P], src[:, i, :]) for i in range(k)],
                         after=[m_in, b.free], each=each)
        b.free = []
        return b, m

    def project_in_two(self, w, j, src, m_in=()):
        b = self.bank()
        for half in range(2):
            for i in range(4 * half, 4 * half + 4):
                m = self.PE.run(self.nc.tensor.matmul, b[:, :], w[:, i, j * P:(j + 1) * P], src[:, i, :],
                                start=i == 0, stop=i == KD - 1, after=[m_in, b.free] if i == 0 else (),
                                counted=i == KD - 1)
            yield
        b.free = []
        return b, m

    def transposes(self, out_in, bank, after=()):
        after = [after, bank.free]
        for n, (o, i) in enumerate(out_in):
            k = i.shape[0]
            m = self.PE.run(self.nc.tensor.transpose, o, i, self.c("ident")[0:k, 0:k], after=after,
                            counted=n == len(out_in) - 1)
            after = ()
        bank.free = []
        return m

    def rms(self, chunks, eps=1e-6, after=()):
        sums = Squares(self)
        for ch in chunks:
            sums.square(ch, after)
        return sums.rstd(eps)

    def scaled(self, out, chunks, gains, shifts=None, after=()):
        nc, marks = self.nc, []
        for k, ch in enumerate(chunks):
            m = self.DVE.run(nc.vector.scalar_tensor_tensor, out[:, k, :], ch, gains[:, k:k + 1], self.rstd[:, :],
                             ALU.mult, ALU.mult, after=after)
            if shifts is not None:
                m = self.ACT.run(nc.scalar.activation, out[:, k, :], out[:, k, :], ACT.Identity,
                                 bias=shifts[:, k:k + 1], after=m)
            marks.append(m)
        return marks

    def load_columns(self, vectors):
        nc = self.nc
        self.cols = {}
        total = sum(a.shape[0] for _, a in vectors)
        tiles = -(-total // P) + 1
        self.columns = self.sb("columns", [P, tiles * P])
        rows = self.big[:, 0:tiles * P]
        m0 = self.DVE.run(nc.vector.memset, rows, 0.0)
        at = 0
        arrive = self.prog.arrivals("vectors")
        for name, a in vectors:
            n = a.shape[0]
            if at % P + n > P:
                at += P - at % P
            self.cols[name] = (at, n)
            t, r = at // P, at % P
            m = self.SP.dma(arrive, rows[r:r + n, t * P:(t + 1) * P], a, after=m0)
            at += n
        assert at <= tiles * P
        for t in range(tiles):
            b = self.bank()
            m1 = self.transposes([(b[:, 0:P], rows[:, t * P:(t + 1) * P])], b, after=[m, self.in_const])
            m1 = self.DVE.run(nc.vector.tensor_copy, self.columns[:, t * P:(t + 1) * P], b[:, 0:P], after=m1)
            b.free = [m1]
        return m1

    def col(self, name, k=None):
        a, n = self.cols[name]
        return self.columns[:, a:a + n] if k is None else self.columns[:, a + k:a + k + 1]

    def load_x(self, x):
        nc = self.nc
        for t in range(NT):
            s = self.wring.take()
            m = self.SP.dma(s, s[:, 0:D], x[t * P:(t + 1) * P, :], after=s.free)
            for half in range(2):
                b = self.bank()
                m1 = self.transposes([(b[:, j * P:(j + 1) * P], s[:, (4 * half + j) * P:(4 * half + j + 1) * P])
                                      for j in range(4)], b, after=[m, self.in_const])
                m2 = self.DVE.run(nc.vector.tensor_copy, self.h[:, 4 * half:4 * half + 4, t * P:(t + 1) * P],
                                  b[:, :].rearrange("p (a b) -> p a b", b=P), after=m1)
                b.free = [m2]
            s.free = [m1]
        return m2

    def store_rows(self, src, out):
        nc, stores = self.nc, []
        for t in range(NT):
            s = self.wring.take()
            for half in range(2):
                b = self.bank()
                m1 = self.transposes([(b[:, j * P:(j + 1) * P], src[:, 4 * half + j, t * P:(t + 1) * P])
                                      for j in range(4)], b, after=self.DVE.count.mark())
                m2 = self.DVE.run(nc.vector.tensor_copy, s[:, 512 * half:512 * half + 512], b[:, :],
                                  after=[m1, s.free])
                b.free = [m2]
            m = self.SP.dma(s, out[t * P:(t + 1) * P, :], s[:, 0:D], after=m2)
            s.free = [m]
            stores.append(m)
        return stores


class Squares:

    def __init__(self, K):
        self.K, self.n, self.made, self.b = K, 0, None, K.banks[7]
        K.bank_ring = K.seven_banks

    def add(self):
        if self.made:
            K, (s, m) = self.K, self.made
            self.m = K.PE.run(K.nc.tensor.matmul, self.b[:, :], K.c("ones"), s[:, :], start=self.n == 1,
                              stop=self.n == KD, after=[m, self.b.free if self.n == 1 else ()])
            s.free = [self.m]

    def square(self, chunk, after=()):
        K = self.K
        self.add()
        s = K.sq_ring.take()
        self.made = s, K.ACT.run(K.nc.scalar.activation, s[:, :], chunk, ACT.Square, after=[after, s.free])
        self.n += 1

    def rstd(self, eps=1e-6):
        K, nc = self.K, self.K.nc
        self.add()
        m = K.DVE.run(nc.vector.tensor_scalar, K.rstd[:, :], self.b[:, :], 1.0 / D, eps, ALU.mult, ALU.add, after=self.m)
        self.b.free = [m]
        m = K.ACT.run(nc.scalar.activation, K.rstd[:, :], K.rstd[:, :], ACT.Sqrt, after=m)
        K.bank_ring = K.all_banks
        return K.DVE.run(nc.vector.reciprocal, K.rstd[:, :], K.rstd[:, :], after=m)
def adaln_start(K, w_ada):
    nc = K.nc
    K.mod = K.sb("mod", [P, 48])
    K.c_act = K.sb("c_act", [P, KD])
    K.w_ada = w_ada.rearrange("(k p) n -> p k n", p=P)
    K.ACT.run(nc.scalar.activation, K.c_act[:, :], K.col("c"), ACT.Silu, after=K.DVE.count.mark())
    K.POOL.wait(K.ACT.count.mark())
    K.ada_sums = Ring(K.prog, [Slot(K.prog, K.sb(f"ada_sums{n}", [P, 256])) for n in range(2)])
    K.DVE.wait(K.ACT.count.mark())

    def four(i):
        for q in range(4):
            adaln_columns(K, 4 * i + q, adaln_sums(K, 4 * i + q, K.wring.take(), K.DVE, nc.vector))

    K.prog.loop(2, four)


def adaln_sums(K, q, slot, lane, engine):
    acc = K.ada_sums.take()
    _, w, m_w = K.weights(K.w_ada[:, :, ds(q * 256, 256)], None, slot=slot)
    run, tt = lane.run, engine.tensor_tensor
    run(tt, w, w, K.c_act[:, :].unsqueeze(2).to_broadcast([P, KD, 256]), ALU.mult, after=m_w)
    run(tt, w[:, 0:4, :], w[:, 0:4, :], w[:, 4:8, :], ALU.add)
    run(tt, w[:, 0:2, :], w[:, 0:2, :], w[:, 2:4, :], ALU.add)
    m = run(tt, acc[:, :], w[:, 0, :], w[:, 1, :], ALU.add, after=acc.free)
    slot.free = [m]
    return acc, m


def adaln_columns(K, q, sums):
    nc, b, (acc, m) = K.nc, K.bank(), sums
    for j in range(2):
        m = K.matmuls(b[:, j:j + 1], [(acc[:, j * P:(j + 1) * P], K.c("ones")[:, 0:1])],
                      after=[m, b.free if j == 0 else ()])
    acc.free = [m]
    m = K.DVE.run(nc.vector.tensor_tensor, K.mod[:, ds(q * 2, 2)], b[:, 0:2],
                  K.columns[:, ds(K.cols["b_ada"][0] + q * 2, 2)], ALU.add, after=m)
    b.free = [m]


def modulated_norm(K, gain, shift_at, scale_at, out):
    nc = K.nc
    g = K.stat[:, 0:KD]
    K.DVE.run(nc.vector.tensor_scalar, g, K.mod[:, scale_at:scale_at + KD], 1.0, None, ALU.add)
    K.DVE.run(nc.vector.tensor_tensor, g, g, K.col(gain), ALU.mult)
    return K.scaled(out, [K.h[:, k, :] for k in range(KD)], g, K.mod[:, shift_at:shift_at + KD])


def ssd_decays(K, w_in, dt_bias, A_log, cs_dram, cd_dram):
    nc, V, S = K.nc, K.DVE, K.ACT
    H = 32
    K.headq = K.carve(4, NT, H)
    K.cdb = K.carve(NT, H)
    K.kept_ssd = K.big_at
    sc = K.carve(12, T)
    K.fetch("scan128")
    q = lambda n: sc[0:H, n, :]
    s, w, m = K.weights(w_in.rearrange("(k p) n -> p k n", p=P)[:, :, 6144:6144 + H], None)
    small = K.stat[0:H, 16:20]
    io = K.prog.arrivals("head_vectors")
    m1 = K.ACT.dma(io, small[:, 0:1], dt_bias.rearrange("(h a) -> h a", a=1))
    m1 = K.ACT.dma(io, small[:, 1:2], A_log.rearrange("(h a) -> h a", a=1))
    b = K.bank()
    m = K.matmuls(b[0:H, :], [(w[:, k, :], K.u[:, k, :]) for k in range(KD)], after=[m, b.free, V.count.mark()])
    s.free = [m]
    x, ax, e, z, z2, acc, dt, cs, e1, dd, tmp = (q(n) for n in range(11))
    ts, tt, stt = nc.vector.tensor_scalar, nc.vector.tensor_tensor, nc.vector.scalar_tensor_tensor
    m = V.run(ts, x, b[0:H, :], small[:, 0:1], None, ALU.add, after=[m, m1])
    b.free = [m]
    V.run(ts, tmp, x, -1.0, None, ALU.mult)
    m = V.run(tt, ax, x, tmp, ALU.min)
    m = S.run(nc.scalar.activation, e, ax, ACT.Exp, after=m)
    V.run(ts, z, e, 2.0, None, ALU.add, after=m)
    V.run(nc.vector.reciprocal, z, z)
    V.run(tt, z, z, e, ALU.mult)
    V.run(tt, z2, z, z, ALU.mult)
    V.run(ts, acc, z2, 1.0 / 17, 1.0 / 15, ALU.mult, ALU.add)
    for d in (13, 11, 9, 7, 5, 3, 1):
        V.run(tt, acc, acc, z2, ALU.mult)
        V.run(ts, acc, acc, 1.0 / d, None, ALU.add)
    V.run(tt, acc, acc, z, ALU.mult)
    V.run(ts, tmp, x, 0.0, None, ALU.max)
    m = V.run(stt, dt, acc, 2.0, tmp, ALU.mult, ALU.add)
    m = S.run(nc.scalar.activation, small[:, 2:3], small[:, 1:2], ACT.Exp, after=m)
    m = V.run(ts, small[:, 2:3], small[:, 2:3], -1.0, None, ALU.mult, after=m)
    V.run(ts, tmp, dt, small[:, 2:3], None, ALU.mult)
    m = V.run(nc.vector.tensor_tensor_scan, cs, K.c("scan128")[0:H, :], tmp, 0.0, ALU.mult, ALU.add)
    m_cs = K.ACT.dma(K.prog.arrivals("cs_out"), cs_dram, cs, after=m)
    m = S.run(nc.scalar.activation, e1, cs, ACT.Exp, after=m)
    for c in range(NT):
        end = cs[:, (c + 1) * P - 1:(c + 1) * P]
        m = V.run(ts, dd[:, c * P:(c + 1) * P], cs[:, c * P:(c + 1) * P], -1.0, end, ALU.mult, ALU.add)
    m = S.run(nc.scalar.activation, dd, dd, ACT.Exp, after=m)
    m = V.run(tt, dd, dd, dt, ALU.mult, after=m)
    diag = sc[0:H, 11, 0:P].rearrange("h (c g) -> h c g", g=H)
    for c in range(NT):
        m = V.run(ts, diag[:, c, :], K.c("ident")[0:H, 0:H], e1[:, (c + 1) * P - 1:(c + 1) * P], None, ALU.mult)
    b = K.bank()
    m = K.matmuls(b[:, 0:P], [(K.c("ones")[0:H, :], sc[0:H, 11, 0:P])], after=[m, b.free])
    m = V.run(nc.vector.tensor_copy, K.cdb, b[:, 0:P].rearrange("p (c g) -> p c g", g=H), after=m)
    b.free = [m]
    b = K.bank()
    m = K.transposes([(b[:, (i * NT + c) * H:(i * NT + c + 1) * H], src[:, c * P:(c + 1) * P])
                      for i, src in enumerate((dt, cs, e1, dd)) for c in range(NT)], b, after=m)
    m = V.run(nc.vector.tensor_copy, K.headq.rearrange("p a c h -> p (a c h)"), b[:, :], after=m)
    b.free = [m]
    K.m_cs = m_cs


def ssd_groups(K, w_in, cs_dram, D_skip, y):
    nc, V, S, prog = K.nc, K.DVE, K.ACT, K.prog
    ts, tt, stt = nc.vector.tensor_scalar, nc.vector.tensor_tensor, nc.vector.scalar_tensor_tensor
    act = nc.scalar.activation
    pre = [Slot(prog, K.carve(T + 3)) for _ in range(2)]
    pre_ring = Ring(prog, pre)
    posts = [K.carve(4, T) for _ in range(2)]
    xs_tok, xdt, xdec = K.carve(NT, 256), K.carve(NT, 256), K.carve(NT, 256)
    B_tok = K.carve(NT, P)
    CB = K.carve(NT, P)
    prev = K.carve(NT, 256)
    zss = [K.carve(NT, 256) for _ in range(2)]
    cs_all = Slot(prog, K.carve(4, T), "cs_all_in")
    W = K.carve(4, NT, P)
    ytok, t1 = K.carve(NT, 256), K.carve(NT, 256)
    gcols = [K.carve(24) for _ in range(2)]
    hqs = [K.carve(4 * NT, 4) for _ in range(2)]
    cds = [K.carve(NT, 4) for _ in range(2)]
    Dsk = K.carve(32)
    Dgs, ss, nss = [K.carve(4) for _ in range(2)], K.carve(4), K.carve(4)
    m_D = K.ACT.dma(K.prog.arrivals("D_skip"), Dsk, D_skip.partition_broadcast(P))
    for p_ in pre:
        V.run(nc.vector.memset, p_[:, 0:3], 0.0)
    V.run(nc.vector.memset, prev[:, 0, :], 0.0)
    V.wait(m_D)
    wv = w_in.rearrange("(k p) n -> p k n", p=P)
    cwa, cba, nga = K.cols["conv_w"][0], K.cols["conv_b"][0], K.cols["ssd_norm_g"][0]
    cw = K.columns[:, cwa:cwa + 128].rearrange("p (i c) -> p i c", i=4)

    cp = nc.vector.tensor_copy

    def front(g, n, start):
        post, zs, gcol, hq, cd, Dg = posts[n], zss[n], gcols[n], hqs[n], cds[n], Dgs[n]
        gw = gcol[:, 0:16].rearrange("p (i c) -> p i c", i=4)
        V.run(cp, gw[:, :, 0:2], cw[:, :, ds(2 * g, 2)])
        V.run(cp, gw[:, :, 2:3], cw[:, :, ds(16 + g, 1)])
        V.run(cp, gw[:, :, 3:4], cw[:, :, ds(24 + g, 1)])
        V.run(cp, gcol[:, 16:18], K.columns[:, ds(cba + 2 * g, 2)])
        V.run(cp, gcol[:, 18:19], K.columns[:, ds(cba + 16 + g, 1)])
        V.run(cp, gcol[:, 19:20], K.columns[:, ds(cba + 24 + g, 1)])
        V.run(cp, gcol[:, 20:22], K.columns[:, ds(nga + 2 * g, 2)])
        V.run(cp, Dg, Dsk[:, ds(4 * g, 4)])
        V.run(cp, cd, K.cdb[:, :, ds(4 * g, 4)])
        V.run(cp, hq, K.headq.rearrange("p a c h -> p (a c) h")[:, :, ds(4 * g, 4)])
        sx, wx, mx = K.weights(wv[:, :, ds(2048 + 256 * g, 256)], None, slot=K.wslots[5 * n])
        sbc = K.wslots[1]
        wbc = sbc[:, :].rearrange("p (a k n) -> p a k n", a=2, k=KD)
        K.SP.dma(sbc, wbc[:, 0], wv[:, :, ds(4096 + 128 * g, 128)], after=sbc.free)
        mbc = K.SP.dma(sbc, wbc[:, 1], wv[:, :, ds(5120 + 128 * g, 128)])
        sums = []
        for j in range(4):
            w, i, m_w = (wx, j, mx) if j < 2 else (wbc[:, j - 2], 0, mbc)
            b, m = K.project(w, i, K.u, m_in=m_w)
            if j == 1:
                sx.free = [m]
            if j == 3:
                sbc.free = [m]
            yield
            p_ = pre_ring.take()
            m = S.run(act, p_[:, 3:3 + T], b[:, :], ACT.Copy, after=[m, p_.free])
            b.free = [m]
            m = V.run(ts, post[:, j, :], p_[:, 0:T], gw[:, 0, j:j + 1], gcol[:, 16 + j:17 + j], ALU.mult, ALU.add,
                      after=m)
            for i in range(1, 4):
                m = V.run(stt, post[:, j, :], p_[:, i:i + T], gw[:, i, j:j + 1], post[:, j, :], ALU.mult, ALU.add)
            p_.free = [m]
            S.run(act, post[:, j, :], post[:, j, :], ACT.Silu, after=m)
            if j % 2:
                sums.append(adaln_sums(K, 8 + 2 * g + len(sums), K.wslots[3 + j // 2], K.POOL, nc.gpsimd))
        sz, wz, mz = K.weights(wv[:, :, ds(256 * g, 256)], None, slot=K.wslots[2])
        zb = K.bank(2)
        for c in range(NT):
            b = zb[c // 2]
            m = K.matmuls(b[:, c % 2 * 256:c % 2 * 256 + 256],
                          [(K.u[:, k, c * P:(c + 1) * P], wz[:, k, :]) for k in range(KD)],
                          after=[mz, b.free if c % 2 == 0 else ()])
            yield
        sz.free = [m]
        for i, b in enumerate(zb):
            m = S.run(act, zs[:, 2 * i:2 * i + 2, :].rearrange("p a b -> p (a b)"), b[:, :], ACT.Silu, after=m)
            b.free = [m]
        for r in range(2):
            adaln_columns(K, 8 + 2 * g + r, sums[r])

    def back(g, n, start, ahead):
        post, zs, gcol, hq, cd, Dg = posts[n], zss[n], gcols[n], hqs[n], cds[n], Dgs[n]
        m_csb = K.ACT.dma(cs_all, cs_all.t, cs_dram[ds(4 * g, 4), :].partition_broadcast(P), after=cs_all.free)
        xb = K.bank(2)
        for i, b in enumerate(xb):
            m = K.transposes([(b[:, (c * 2 + j) * P:(c * 2 + j + 1) * P], post[:, j, (2 * i + c) * P:(2 * i + c + 1) * P])
                              for c in range(2) for j in range(2)], b, after=start)
            m = S.run(act, xs_tok[:, 2 * i:2 * i + 2, :].rearrange("p a b -> p (a b)"), b[:, :], ACT.Copy, after=m)
            b.free = [m]
        bb = K.bank()
        m1 = K.transposes([(bb[:, c * P:(c + 1) * P], post[:, 2, c * P:(c + 1) * P]) for c in range(NT)], bb)
        m1 = S.run(act, B_tok.rearrange("p a b -> p (a b)"), bb[:, :], ACT.Copy, after=m1)
        bb.free = [m1]
        xh = xs_tok.rearrange("p c (h d) -> p (c h) d", d=64)
        per_head = lambda a: hq[:, 4 * a:4 * a + 4, :].rearrange("p c h -> p (c h)").unsqueeze(2).to_broadcast([P, 16, 64])
        V.run(tt, xdt.rearrange("p c (h d) -> p (c h) d", d=64), xh, per_head(0), ALU.mult, after=m)
        m_x = V.run(tt, xdec.rearrange("p c (h d) -> p (c h) d", d=64), xh, per_head(3), ALU.mult)
        cb = K.bank()
        for c in range(NT):
            m = K.matmuls(cb[:, c * P:(c + 1) * P], [(post[:, 2, c * P:(c + 1) * P], post[:, 3, c * P:(c + 1) * P])],
                          after=cb.free if c == 0 else ())
        yield
        m = V.run(tt, CB, cb[:, :].rearrange("p (c l) -> p c l", l=P),
                  K.c("upper").unsqueeze(1).to_broadcast([P, NT, P]), ALU.mult, after=m)
        cb.free = [m]
        for r in range(4):
            V.run(tt, W[:, r], cs_all.t[:, r, :].rearrange("p (c l) -> p c l", l=P),
                  hq[:, 4:8, r].unsqueeze(2).to_broadcast([P, NT, P]), ALU.subtract, after=m_csb)
        Wf = W.rearrange("p r c l -> p (r c l)")
        m = V.run(ts, Wf, Wf, 0.0, None, ALU.min)
        cs_all.free = [m]
        m = S.run(act, Wf, Wf, ACT.Exp, after=m)
        for r in range(4):
            m = V.run(tt, W[:, r], W[:, r], CB, ALU.mult, after=m)
        m_W = m
        sbk = K.bank(2)
        for c in range(3):
            b = sbk[c // 2]
            m = K.matmuls(b[:, c % 2 * 256:c % 2 * 256 + 256], [(B_tok[:, c, :], xdec[:, c, :])],
                          after=[m1, m_x, b.free if c % 2 == 0 else ()])
        yield
        for c in range(3):
            b = sbk[c // 2]
            add = b[:, c % 2 * 256:c % 2 * 256 + 256]
            if c == 0:
                m = V.run(cp, prev[:, 1, :], add, after=m)
            else:
                V.run(tt, prev[:, c + 1, :].rearrange("p (h d) -> p h d", d=64),
                      prev[:, c, :].rearrange("p (h d) -> p h d", d=64),
                      cd[:, c, :].unsqueeze(2).to_broadcast([P, 4, 64]), ALU.mult)
                m = V.run(tt, prev[:, c + 1, :], prev[:, c + 1, :], add, ALU.add)
            b.free = [m]
        yield
        yield
        yd, yo = K.bank(2), K.bank(2)
        for c in range(NT):
            b, o = yo[c // 2], c % 2 * 256
            m = K.matmuls(b[:, o:o + 256], [(post[:, 3, c * P:(c + 1) * P], prev[:, c, :])],
                          after=[m, b.free if c % 2 == 0 else ()])
            b = yd[c // 2]
            for r in range(4):
                m = K.matmuls(b[:, o + 64 * r:o + 64 * r + 64], [(W[:, r, c, :], xdt[:, c, 64 * r:64 * r + 64])],
                              after=[m_W, b.free if c % 2 == 0 and r == 0 else ()])
        yield
        for i in range(2):
            o = yo[i]
            h4 = lambda a: a.rearrange("p (x d) -> p x d", d=64)
            m2 = V.run(tt, t1[:, 2 * i:2 * i + 2, :].rearrange("p c (h d) -> p (c h) d", d=64), h4(o[:, :]),
                       hq[:, 8 + 2 * i:10 + 2 * i, :].rearrange("p c h -> p (c h)").unsqueeze(2).to_broadcast([P, 8, 64]),
                       ALU.mult, after=m)
            o.free = [m2]
            f = lambda a: a[:, 2 * i:2 * i + 2, :].rearrange("p a b -> p (a b)")
            m2 = V.run(tt, f(t1), f(t1), yd[i][:, :], ALU.add)
            yd[i].free = [m2]
        for c in range(NT):
            V.run(tt, ytok[:, c, :].rearrange("p (h d) -> p h d", d=64), xs_tok[:, c, :].rearrange("p (h d) -> p h d", d=64),
                  Dg.unsqueeze(2).to_broadcast([P, 4, 64]), ALU.mult)
        V.run(tt, ytok, ytok, t1, ALU.add)
        V.run(tt, ytok, ytok, zs, ALU.mult)
        V.run(tt, t1, ytok, ytok, ALU.mult)
        V.run(nc.vector.tensor_reduce, ss, t1, AX.X, ALU.add)
        m = V.run(ts, ss, ss, 1.0 / 256, 1e-6, ALU.mult, ALU.add)
        m = S.run(act, nss, ss, ACT.Sqrt, after=m)
        V.run(nc.vector.reciprocal, nss, nss, after=m)
        m = V.run(tt, ytok, ytok, nss.unsqueeze(2).to_broadcast([P, NT, 256]), ALU.mult)
        for _ in range(3):
            yield
        for j in range(2):
            b = K.bank()
            m = K.transposes([(b[:, c * P:(c + 1) * P], ytok[:, c, j * P:(j + 1) * P]) for c in range(NT)], b, after=m)
            m = S.run(act, y[:, ds(2 * g + j, 1), :], b[:, :].unsqueeze(1), ACT.Copy, scale=gcol[:, 20 + j:21 + j], after=m)
            b.free = [m]

    K.pipeline(8, front, back)


def pool_branch(K, w_in, pool_w, mixed):
    nc, V, S, prog = K.nc, K.DVE, K.ACT, K.prog
    tt, stt = nc.vector.tensor_tensor, nc.vector.scalar_tensor_tensor
    PADW = 16
    xp = [Slot(prog, K.carve(PADW + T)) for _ in range(2)]
    sums = [K.carve(PADW + T) for _ in range(2)]
    pooled = Slot(prog, K.carve(2, T))
    for a in [x.t for x in xp] + sums:
        V.run(nc.vector.memset, a[:, 0:PADW], 0.0)
    wv = w_in.rearrange("(k p) n -> p k n", p=P)
    for gi, win in enumerate((2, 4, 8, 16)):
        s, w, m_w = K.weights(wv[:, :, 6176 + 256 * gi:6176 + 256 * gi + 256], None)
        sp, wp, m_p = K.weights(pool_w[gi].rearrange("(k p) n -> p k n", p=P), None, rows=2)
        pf = pooled.free
        for j in range(2):
            b, m = K.project(w, j, K.u, m_in=m_w)
            s.free = [m]
            x = xp[j]
            m = S.run(nc.scalar.activation, x[:, PADW:], b[:, :], ACT.Copy, after=[m, x.free])
            b.free = [m]
            cur, step, n = x.t, 1, 0
            while step < win:
                nxt = sums[n % 2]
                V.run(tt, nxt[:, PADW:], cur[:, PADW:], cur[:, PADW - step:PADW - step + T], ALU.add, after=m)
                cur, step, n = nxt, 2 * step, n + 1
            other = sums[n % 2]
            V.run(tt, other[:, PADW:], cur[:, PADW:], K.c(f"inv{win}"), ALU.mult)
            m = V.run(tt, pooled[:, j, :], other[:, PADW:], x[:, PADW:], ALU.subtract, after=pf)
            x.free = [m]
        for j in range(2):
            b, m1 = K.project(wp, j, pooled.t, k=2, m_in=[m_p, m])
            sp.free = pooled.free = [m1]
            m1 = S.run(nc.scalar.activation, mixed[:, 2 * gi + j, :], b[:, :], ACT.Copy,
                      scale=K.col("pool_scale", 2 * gi + j), after=m1)
            b.free = [m1]


def combine(K, w_in, w_br_ssd, w_br_pool, w_out, y, pooled, merged):
    nc, V, S, prog = K.nc, K.DVE, K.ACT, K.prog
    tt, stt = nc.vector.tensor_tensor, nc.vector.scalar_tensor_tensor
    wv = w_in.rearrange("(k p) n -> p k n", p=P)
    wsv = w_br_ssd.rearrange("(k p) n -> p k n", p=P)
    wpv = w_br_pool.rearrange("(k p) n -> p k n", p=P)
    gate = [Slot(prog, K.carve(T)) for _ in range(2)]

    def column(j):
        ss, ws, m_s = K.weights(wsv[:, :, ds(j * P, P)], None, rows=16)
        sp, wp, m_p = K.weights(wpv[:, :, ds(j * P, P)], None)
        sg = K.wring.take()
        wg = sg[:, :].rearrange("p (a k n) -> p a k n", a=2, k=KD)
        K.SP.dma(sg, wg[:, 0], wv[:, :, ds(7200 + j * P, P)], after=sg.free)
        m_g = K.SP.dma(sg, wg[:, 1], wv[:, :, ds(8224 + j * P, P)])
        for i in range(2):
            b, m = K.project(wg[:, i], 0, K.u, m_in=m_g)
            sg.free = [m]
            m = S.run(nc.scalar.activation, gate[i][:, :], b[:, :], ACT.Sigmoid, after=[m, gate[i].free])
            b.free = [m]
        b1, m1 = K.project(ws, 0, y, k=16, m_in=m_s)
        ss.free = [m1]
        b2, m2 = K.project(wp, 0, pooled, m_in=m_p)
        sp.free = [m2]
        V.run(tt, gate[0][:, :], gate[0][:, :], b1[:, :], ALU.mult, after=[m, m1])
        b1.free = [V.count.mark()]
        V.run(tt, gate[1][:, :], gate[1][:, :], b2[:, :], ALU.mult, after=m2)
        b2.free = [V.count.mark()]
        m = V.run(tt, merged[:, ds(j, 1), :], gate[0][:, :].unsqueeze(1), gate[1][:, :].unsqueeze(1), ALU.add)
        gate[0].free = gate[1].free = [m]

    prog.loop(KD // 2, lambda i: [column(2 * i + n) for n in range(2)])
    residual_product(K, w_out, merged, 16)


def residual_product(K, w, src, gate_at):
    nc, V = K.nc, K.DVE
    wv = w.rearrange("(k p) n -> p k n", p=P)
    K.PE.wait(K.DVE.count.mark(), K.ACT.count.mark())
    sums = Squares(K)
    for j2 in range(KD // 2):
        s, w_, m_w = K.weights(wv[:, :, ds(j2 * 256, 256)], None)
        for j in range(2):
            b, m = K.project(w_, j, src, m_in=m_w)
            s.free = [m]
            hj = K.h[:, ds(2 * j2 + j, 1), :]
            m = V.run(nc.vector.scalar_tensor_tensor, hj, b[:, :].unsqueeze(1), K.mod[:, ds(gate_at + 2 * j2 + j, 1)],
                      hj, ALU.mult, ALU.add, after=m)
            b.free = [m]
            sums.square(K.h[:, 2 * j2 + j, :], m)
    sums.rstd()
E_ALL, TOP, F_E = 64, 8, 256


def router(K, w_router, router_bias, score, rep):
    nc, V, S = K.nc, K.DVE, K.ACT
    ts, tt = nc.vector.tensor_scalar, nc.vector.tensor_tensor
    G = 8
    choice, masked = K.carve(NT, E_ALL), K.carve(NT, E_ALL)
    top = K.carve(NT * G, 8)
    gs, gm, pen = K.carve(NT, G), K.carve(NT, G), K.carve(NT, G)
    cmp1, cmp2 = K.carve(NT, G, G), K.carve(NT, G, G)
    bias, total = K.carve(E_ALL), K.carve(NT)
    K.fetch("before8")
    m_b = K.ACT.dma(K.prog.arrivals("router_bias"), bias, router_bias.partition_broadcast(P))
    s, w, m = K.weights(w_router.rearrange("(k p) n -> p k n", p=P), None)
    b = K.bank()
    for t in range(NT):
        m = K.matmuls(b[:, t * E_ALL:(t + 1) * E_ALL], [(K.u[:, k, t * P:(t + 1) * P], w[:, k, :]) for k in range(KD)],
                      after=[m, V.count.mark(), b.free if t == 0 else ()])
    s.free = [m]
    merge = lambda a: a.rearrange("p a b -> p (a b)")
    m = S.run(nc.scalar.activation, merge(score), b[:, 0:NT * E_ALL], ACT.Sigmoid, after=m)
    b.free = [m]
    V.run(tt, choice, score, bias.unsqueeze(1).to_broadcast([P, NT, E_ALL]), ALU.add, after=[m, m_b])
    for t in range(NT):
        for g in range(G):
            V.run(nc.vector.max, top[:, t * G + g, :], choice[:, t, g * 8:(g + 1) * 8])
    V.run(tt, merge(gs), top[:, :, 0], top[:, :, 1], ALU.add)
    other = gs.unsqueeze(2).to_broadcast([P, NT, G, G])
    this = gs.unsqueeze(3).to_broadcast([P, NT, G, G])
    for t in range(NT):
        V.run(tt, cmp1[:, t], other[:, t], this[:, t], ALU.is_gt)
        V.run(tt, cmp2[:, t], other[:, t], this[:, t], ALU.is_equal)
        V.run(tt, cmp2[:, t], cmp2[:, t], K.c("before8").rearrange("p (j i) -> p j i", i=G), ALU.mult)
    V.run(tt, cmp1, cmp1, cmp2, ALU.add)
    V.run(nc.vector.tensor_reduce, gs, cmp1, AX.X, ALU.add)
    V.run(ts, gm, gs, 4.0, None, ALU.is_lt)
    V.run(ts, pen, gm, 1.0, 1e30, ALU.subtract, ALU.mult)
    e8 = lambda a: a.rearrange("p t (g e) -> p (t g) e", e=8)
    wide = lambda a: merge(a).unsqueeze(2).to_broadcast([P, NT * G, 8])
    V.run(tt, e8(masked), e8(choice), wide(gm), ALU.mult)
    V.run(tt, e8(masked), e8(masked), wide(pen), ALU.add)
    for t in range(NT):
        V.run(nc.vector.max, top[:, t, :], masked[:, t, :])
        V.run(nc.vector.match_replace, rep[:, t, :], top[:, t, :], masked[:, t, :], -3e30)
    V.run(tt, rep, rep, masked, ALU.not_equal)
    V.run(tt, score, score, rep, ALU.mult)
    V.run(nc.vector.tensor_reduce, total, score, AX.X, ALU.add)
    V.run(nc.vector.reciprocal, total, total)
    V.run(ts, total, total, ROUTED_SCALE, None, ALU.mult)
    V.run(tt, score, score, total.unsqueeze(2).to_broadcast([P, NT, E_ALL]), ALU.mult)


EXTRA = 31
I32 = mybir.dt.int32
TURN = 8
AHEAD = 4


class Experts:

    def __init__(self, K, u_rows, total_rows):
        self.K, prog = K, K.prog
        self.u_rows, self.total_rows = u_rows, total_rows
        slot = lambda name=None, *shape: Slot(prog, K.carve(*shape), name)
        self.sel = [slot(None, NT, P) for _ in range(2)]
        self.rhs = [slot(None, NT, 3) for _ in range(2)]
        self.lists = [Slot(prog, (K.carve(4), K.sb(f"rows{n}", [P, 2], I32))) for n in range(TURN)]
        self.x_rows = [Slot(prog, K.carve(D), f"x_rows{n}_in", 0) for n in range(AHEAD)]
        self.added = Slot(prog, None, "rows_added", 0)
        self.xT = [slot(None, KD, P) for _ in range(2)]
        self.act = slot(None, F_E)
        self.hid = [slot(None, F_E) for _ in range(2)]
        self.hidT = slot(None, 2, P)
        self.y = [slot(None, D) for n in range(2)]
        for s in self.x_rows:
            K.DVE.run(K.nc.vector.memset, s.t, 0.0)

    def select(self, n, positions, weights, after=()):
        nc, V, K, sel, rhs = self.K.nc, self.K.DVE, self.K, self.sel[n % 2], self.rhs[n % 2]
        V.run(nc.vector.tensor_tensor, sel.t, K.c("slot_row").unsqueeze(1).to_broadcast([P, NT, P]),
              positions.to_broadcast([P, NT, P]), ALU.is_equal, after=[sel.free, after])
        return V.run(nc.vector.tensor_copy, rhs[:, :, 2:3], weights, after=rhs.free)

    def list_tokens(self, n, m):
        K, nc, V = self.K, self.K.nc, self.K.DVE
        sel, rhs, lst = self.sel[n % 2], self.rhs[n % 2], self.lists[n % TURN]
        info, rows = lst.t
        b = K.bank()
        m = K.matmuls(b[:, 0:3], [(sel[:, t, :], rhs[:, t, :]) for t in range(NT)], after=[m, b.free])
        sel.free = rhs.free = [m]
        m = V.run(nc.vector.tensor_copy, info[:, 0:3], b[:, 0:3], after=[m, lst.free])
        b.free = [m]
        V.run(nc.vector.tensor_copy, rows[:, 0:1], info[:, 0:1])
        V.run(nc.vector.scalar_tensor_tensor, info[:, 3:4], info[:, 1:2], self.minus_spare, info[:, 0:1],
              ALU.mult, ALU.add)
        m = V.run(nc.vector.tensor_tensor, rows[:, 1:2], info[:, 3:4], K.c("spare_row")[:, 0:1], ALU.add)
        x = self.x_rows[n % AHEAD]
        K.POOL.wait(m, x.free, K.POOL.count.mark())
        m = K.POOL.indirect(x, K.nc.gpsimd.indirect_dma_start, x.t, None, self.u_rows,
                            bass.IndirectOffsetOnAxis(ap=rows[:, 0:1], axis=0))
        return m

    def turn(self, n, m_rows):
        K, x, xT = self.K, self.x_rows[n % AHEAD], self.xT[n % 2]
        for half in range(2):
            b = K.bank()
            m1 = K.transposes([(b[:, j * P:(j + 1) * P], x[:, (4 * half + j) * P:(4 * half + j + 1) * P])
                               for j in range(4)], b, after=m_rows)
            m = K.ACT.run(K.nc.scalar.activation, xT[:, 4 * half:4 * half + 4, :].rearrange("p a b -> p (a b)"),
                          b[:, :], ACT.Copy, after=[m1, xT.free])
            b.free = [m]
        x.free = [m1]
        return m

    def load(self, n, wg, wu, wd):
        K, slots = self.K, self.K.wslots[3 * (n % 2):3 * (n % 2) + 3]
        return [K.weights(w.rearrange("(k p) n -> p k n", p=P), None, rows=rows, slot=s)
                for w, rows, s in zip((wg, wu, wd), (KD, KD, 2), slots)]

    def gate_up(self, n, xT, w, weight, after=()):
        K, nc, hid = self.K, self.K.nc, self.hid[n % 2]
        (sg, g, mg), (su, u, mu), _ = w
        b = K.bank()
        m = K.matmuls(b[:, 0:F_E], [(xT(k), g[:, k, :]) for k in range(KD)], after=[after, mg, b.free])
        sg.free = [m]
        m1 = K.matmuls(b[:, F_E:2 * F_E], [(xT(k), u[:, k, :]) for k in range(KD)], after=mu)
        su.free = [m1]
        m = K.ACT.run(nc.scalar.activation, self.act.t, b[:, 0:F_E], ACT.Silu, after=[m1, self.act.free])
        if weight is None:
            m = K.DVE.run(nc.vector.tensor_tensor, hid.t, b[:, F_E:2 * F_E], self.act.t, ALU.mult,
                          after=[m, hid.free])
        else:
            m = K.DVE.run(nc.vector.scalar_tensor_tensor, hid.t, b[:, F_E:2 * F_E], weight, self.act.t,
                          ALU.mult, ALU.mult, after=[m, hid.free])
        b.free = self.act.free = [m]
        return m, m1

    def turn_hid(self, n, m_hid):
        K, nc, hid = self.K, self.K.nc, self.hid[n % 2]
        b = K.bank()
        m = K.transposes([(b[:, j * P:(j + 1) * P], hid.t[:, j * P:(j + 1) * P]) for j in range(2)], b, after=m_hid)
        hid.free = [m]
        m = K.DVE.run(nc.vector.tensor_copy, self.hidT.t.rearrange("p a b -> p (a b)"), b[:, 0:F_E],
                      after=[m, self.hidT.free])
        b.free = [m]
        return m

    def down(self, n, w_down, m):
        K, nc, y = self.K, self.K.nc, self.y[n % 2]
        sd, d, md = w_down
        out = []
        for half in range(2):
            b = K.bank()
            m1 = K.matmuls(b[:, :], [(self.hidT.t[:, j, :], d[:, j, half * 512:half * 512 + 512]) for j in range(2)],
                           after=[m, md, b.free])
            dst = y[:, half * 512:half * 512 + 512]
            if half == 0:
                m2 = K.ACT.run(nc.scalar.activation, dst, b[:, :], ACT.Copy, after=[m1, y.free])
            else:
                m2 = K.DVE.run(nc.vector.tensor_copy, dst, b[:, :], after=[m1, y.free])
            b.free = [m2]
            out.append(m2)
        sd.free = self.hidT.free = [m1]
        return out

    def add_rows(self, n, m_y):
        K, y, lst = self.K, self.y[n % 2], self.lists[n % TURN]
        K.POOL.wait(m_y, self.added.free, K.POOL.count.mark())
        m = K.POOL.indirect(self.added, K.nc.gpsimd.indirect_dma_start, self.total_rows,
                            bass.IndirectOffsetOnAxis(ap=lst.t[1][:, 1:2], axis=0), y.t, None, compute_op=ALU.add)
        y.free = lst.free = self.added.free = [m]
        return m


def experts(K, A, score, chosen, u_rows, total_rows):
    nc, V, S, prog = K.nc, K.DVE, K.ACT, K.prog
    ts, tt, stt = nc.vector.tensor_scalar, nc.vector.tensor_tensor, nc.vector.scalar_tensor_tensor
    X = Experts(K, u_rows, total_rows)
    K.fetch("before", "slot_row", "expert_row", "token_and_one", "spare_row")
    pos, far = K.carve(NT, E_ALL), K.carve(NT, E_ALL)
    count, extra, upto, base, hot, hot2 = (K.carve(E_ALL) for _ in range(6))
    one, minus, num, gx, wx = K.carve(E_ALL), K.carve(1), K.carve(8), K.carve(NT), K.carve(NT)
    tmp4 = K.carve(NT, E_ALL)
    number = K.sb("numbers", [P, 2], I32)
    b = K.bank()
    for t in range(NT):
        m = K.matmuls(b[:, t * E_ALL:(t + 1) * E_ALL], [(K.c("before"), chosen[:, t, :])]
                      + [(K.c("ones"), chosen[:, i, :]) for i in range(t)], after=[b.free, V.count.mark()])
    m = K.matmuls(b[:, 256:256 + E_ALL], [(K.c("ones"), chosen[:, i, :]) for i in range(NT)])
    V.run(ts, pos, b[:, 0:256].rearrange("p (t e) -> p t e", e=E_ALL), 1.0, None, ALU.add, after=m)
    m = V.run(nc.vector.tensor_copy, count, b[:, 256:256 + E_ALL])
    b.free = [m]
    V.run(tt, pos, pos, chosen, ALU.mult)
    V.run(ts, pos, pos, 1.0, None, ALU.subtract)
    V.run(ts, extra, count, 128.0, None, ALU.is_gt)
    for more in (256.0, 384.0):
        V.run(ts, base, count, more, None, ALU.is_gt)
        V.run(tt, extra, extra, base, ALU.add)
    V.run(nc.vector.memset, one, 1.0)
    V.run(nc.vector.tensor_tensor_scan, upto, one, extra, 0.0, ALU.mult, ALU.add)
    V.run(tt, extra, upto, extra, ALU.subtract)
    V.run(ts, base, extra, 128.0, 127.0, ALU.mult, ALU.subtract)
    V.run(tt, far, pos, base.unsqueeze(1).to_broadcast([P, NT, E_ALL]), ALU.add)
    V.run(ts, tmp4, pos, 128.0, None, ALU.is_ge)
    V.run(tt, far, far, tmp4, ALU.mult)
    V.run(nc.vector.memset, num, 0.0)
    V.run(nc.vector.tensor_copy, number[:, 0:1], upto[:, E_ALL - 1:E_ALL])
    V.run(ts, minus, K.c("spare_row")[:, 0:1], -1.0, None, ALU.mult)
    X.minus_spare = minus
    for r in X.rhs:
        m_t = V.run(nc.vector.tensor_copy, r[:, :, 0:2], K.c("token_and_one").rearrange("p (t a) -> p t a", a=2))

    rows_in = [Slot(prog, None) for _ in range(AHEAD)]

    select = lambda e, n: X.select(n, pos[:, :, ds(e, 1)], score[:, :, ds(e, 1)])

    def list_tokens(n, m):
        rows_in[n % AHEAD].free = [X.list_tokens(n, m)]

    for n in range(AHEAD):
        list_tokens(n, select(n, n))
    w = X.load(1, A["ws_gate"][0], A["ws_up"][0], A["ws_down"][0])
    turned, hid_ready, w_down = ([Slot(prog, None) for _ in range(2)] for _ in range(3))
    for t in range(NT):
        m, _ = X.gate_up(t, lambda k: K.u[:, k, t * P:(t + 1) * P], w, None)
        m = X.down(t, w[2], X.turn_hid(t, m))
        y = X.y[t % 2]
        m = K.POOL.dma(X.added, total_rows[t * P:(t + 1) * P, :], y.t, after=[m, X.added.free])
        y.free = X.added.free = [m]
    wg, wu, wd = (A[n][0].rearrange("e k n -> (e k) n") for n in ("we_gate", "we_up", "we_down"))
    weights_of = lambda e: (wg[ds(e * D, D), :], wu[ds(e * D, D), :], wd[ds(e * F_E, F_E), :])
    down_view = lambda n: K.wslots[3 * (n % 2) + 2][:, :].rearrange("p (k n) -> p k n", n=D)

    def open_block(e, n):
        w, xT = X.load(n, *weights_of(e)), X.xT[n % 2]
        w_down[n % 2].free = [w[2][2]]
        m_hid, m_read = X.gate_up(n, lambda k: xT[:, k, :], w, X.lists[n % TURN].t[0][:, 2:3], after=turned[n % 2].free)
        hid_ready[n % 2].free, xT.free = [m_hid], [m_read]

    def turn(n):
        turned[n % 2].free = [X.turn(n, rows_in[n % AHEAD].free)]

    def block(e, n, left=E_ALL):
        if left > AHEAD:
            m_sel = select(e + AHEAD, n + AHEAD)
        if left > 1:
            open_block(e + 1, n + 1)
        m = X.turn_hid(n, hid_ready[n % 2].free)
        if left > 2:
            turn(n + 2)
        m = X.down(n, (K.wslots[3 * (n % 2) + 2], down_view(n), w_down[n % 2].free), m)
        if left > AHEAD:
            list_tokens(n + AHEAD, m_sel)
        X.add_rows(n, m)

    turn(0)
    open_block(0, 0)
    turn(1)
    prog.loop(E_ALL // TURN - 1, lambda i: [block(TURN * i + n, n) for n in range(TURN)])
    for n in range(TURN):
        block(E_ALL - TURN + n, n, TURN - n)

    prog.phase(X.added.free)
    limit = nc.values_load(number[0:1, 0:1], min_val=0, max_val=EXTRA)

    def extra_block(i):
        for s in X.x_rows[:1] + X.y[:1] + X.lists[:1] + [X.added]:
            s.free = [V.count.mark()]
        V.run(ts, hot, extra, num[:, 0:1], None, ALU.is_le)
        V.run(ts, hot2, upto, num[:, 0:1], None, ALU.is_gt)
        V.run(tt, hot, hot, hot2, ALU.mult)
        V.run(tt, hot2, hot, K.c("expert_row"), ALU.mult)
        V.run(nc.vector.tensor_reduce, num[:, 1:2], hot2, AX.X, ALU.add)
        m_e = V.run(nc.vector.tensor_copy, number[:, 1:2], num[:, 1:2])
        V.run(tt, tmp4, far, hot.unsqueeze(1).to_broadcast([P, NT, E_ALL]), ALU.mult)
        V.run(nc.vector.tensor_reduce, gx, tmp4, AX.X, ALU.add)
        V.run(tt, tmp4, score, hot.unsqueeze(1).to_broadcast([P, NT, E_ALL]), ALU.mult)
        V.run(nc.vector.tensor_reduce, wx, tmp4, AX.X, ALU.add)
        V.run(ts, gx, gx, num[:, 2:3], None, ALU.subtract)
        m = X.list_tokens(0, X.select(0, gx.unsqueeze(2), wx.unsqueeze(2)))
        K.SP.wait(m_e)
        e = nc.sync.value_load(number[0:1, 1:2], min_val=0, max_val=E_ALL - 1) if not prog.dry else 0
        w = X.load(0, *weights_of(e))
        m = X.turn(0, m)
        m, m_read = X.gate_up(0, lambda k: X.xT[0][:, k, :], w, X.lists[0].t[0][:, 2:3], after=m)
        X.xT[0].free = [m_read]
        m = X.add_rows(0, X.down(0, w[2], X.turn_hid(0, m)))
        V.run(ts, num[:, 0:1], num[:, 0:1], 1.0, None, ALU.add, after=m)
        V.run(ts, num[:, 2:3], num[:, 2:3], 128.0, None, ALU.add)

    V.run(nc.vector.memset, num[:, 2:3], 1.0)
    prog.loop_while(EXTRA, limit, extra_block)


def moe(K, A):
    nc, V = K.nc, K.DVE
    modulated_norm(K, "norm_ffn_g", 24, 32, K.u)
    K.new_phase()
    score, chosen = K.carve(NT, E_ALL), K.carve(NT, E_ALL)
    kept = K.big_at
    stored = K.store_rows(K.u, K.u_rows)
    router(K, A["w_router"][0], A["router_bias"][0], score, chosen)
    K.new_phase(kept, stored)
    experts(K, A, score, chosen, K.u_rows, K.total_rows)
    for t in range(NT):
        s = K.wring.take()
        m = K.SP.dma(s, s[:, 0:D], K.total_rows[t * P:(t + 1) * P, :], after=s.free)
        for half in range(2):
            b = K.bank()
            m1 = K.transposes([(b[:, j * P:(j + 1) * P], s[:, (4 * half + j) * P:(4 * half + j + 1) * P])
                               for j in range(4)], b, after=m)
            b4 = b[:, :].rearrange("p (a b) -> p a b", b=P)
            sq = K.sq_ring.take()
            sq4 = sq[:, :].rearrange("p (a b) -> p a b", b=P)
            hh = K.h[:, 4 * half:4 * half + 4, t * P:(t + 1) * P]
            m2 = V.run(nc.vector.tensor_tensor, sq4, b4,
                       K.mod[:, 40 + 4 * half:44 + 4 * half].unsqueeze(2).to_broadcast([P, 4, P]), ALU.mult, after=[m1, sq.free])
            b.free = [m2]
            m2 = V.run(nc.vector.tensor_tensor, hh, hh, sq4, ALU.add)
            sq.free = [m2]
        s.free = [m1]
    K.new_phase()
    K.rms([K.h[:, k, :] for k in range(KD)], after=V.count.mark())
    marks = K.scaled(K.h, [K.h[:, k, :] for k in range(KD)], K.col("final_norm_g"))
    K.rms([K.h[:, k, :] for k in range(KD)], after=marks)
    K.new_phase()
HEAD = 64
R_, K_, V_, G_, W_, A_ = range(6)


def rwkv_inputs(K, A, scratch):
    nc, V, S, prog = K.nc, K.DVE, K.ACT, K.prog
    K.scaled(K.u, [K.h[:, k, :] for k in range(KD)], K.columns[:, K.cols["norm_pre"][0]:K.cols["norm_pre"][0] + KD])
    dx = K.carve(KD, T)
    V.run(nc.vector.tensor_tensor, dx[:, :, 1:T], K.u[:, :, 0:T - 1], K.u[:, :, 1:T], ALU.subtract)
    V.run(nc.vector.tensor_scalar, dx[:, :, 0:1], K.u[:, :, 0:1], -1.0, None, ALU.mult)
    mix = [Slot(prog, K.carve(KD, T)) for _ in range(2)]
    out = Ring(prog, [Slot(prog, K.carve(T), f"rwkv_out{n}") for n in range(4)])
    small = Slot(prog, K.carve(T))
    mu = K.cols["a_mu"][0]

    def mixed(slot, c):
        for k in range(KD):
            m = V.run(nc.vector.scalar_tensor_tensor, slot[:, k, :], dx[:, k, :], K.columns[:, ds(mu + c * KD + k, 1)],
                      K.u[:, k, :], ALU.mult, ALU.add, after=slot.free)
        return m

    def two(i):
        for n in range(2):
            c, x = 2 * i + n, mix[n]
            m_x = mixed(x, c)
            wv = A["a_w_in_2"][0].rearrange("c k n -> (c k) n")[ds(c * D, D), :].rearrange("(k p) n -> p k n", p=P)
            for q in range(4):
                s, w, m_w = K.weights(wv[:, :, q * 256:(q + 1) * 256], None)
                for j in range(2):
                    b, m = K.project(w, j, x.t, m_in=[m_w, m_x])
                    s.free = x.free = [m]
                    o = out.take()
                    m = S.run(nc.scalar.activation, o[:, :], b[:, :], ACT.Copy, after=[m, o.free])
                    b.free = [m]
                    o.free = [S.dma(o, scratch[2 * q + j].rearrange("p w t -> w p t")[ds(c, 1)]
                                       .rearrange("w p t -> (w p) t"), o.t, after=m)]

    prog.loop(2, two)
    for which, w1, w2, bias, func in ((W_, "a_w1_2", "a_w2_2", "w0", ACT.Tanh), (A_, "a_a1_2", "a_a2_2", "a0", ACT.Copy)):
        x = mix[which % 2]
        m_x = mixed(x, which)
        s, w, m_w = K.weights(A[w1][0].rearrange("(k p) n -> p k n", p=P), None)
        b = K.bank()
        m = K.matmuls(b[0:HEAD, :], [(w[:, k, :], x[:, k, :]) for k in range(KD)], after=[m_w, m_x, b.free])
        s.free = x.free = [m]
        m_s = S.run(nc.scalar.activation, small[0:HEAD, :], b[0:HEAD, :], func, after=[m, small.free])
        b.free = [m_s]
        s = K.wring.take()
        m_w = K.SP.dma(s, s[0:HEAD, 0:D], A[w2][0], after=s.free)
        for j in range(KD):
            b = K.bank()
            m = K.matmuls(b[:, :], [(s[0:HEAD, j * P:(j + 1) * P], small[0:HEAD, :])], after=[m_w, m_s, b.free])
            s.free = small.free = [m]
            o = out.take()
            m = S.run(nc.scalar.activation, o[:, :], b[:, :], ACT.Sigmoid, bias=K.col(bias, j), after=[m, o.free])
            b.free = [m]
            o.free = [S.dma(o, scratch[j, :, which, :], o.t, after=m)]
    return [o.count.mark() for o in out.slots]


def rwkv_pairs(K, scratch, y_out):
    nc, V, S, prog = K.nc, K.DVE, K.ACT, K.prog
    ts, tt, stt = nc.vector.tensor_scalar, nc.vector.tensor_tensor, nc.vector.scalar_tensor_tensor
    act, cp = nc.scalar.activation, nc.vector.tensor_copy
    K.fetch("same_head", "neg_up16", "neg_low16", "neg_off16", "neg_off32", "up64", "upeq64", "scan64", "head_cols")
    ins = [Slot(prog, K.carve(6, T), f"pair{n}_in") for n in range(2)]
    shared = {n: K.carve(T) for n in "L Em Ep En kk k2 lw al0t al1t X2 gate".split()}
    shared.update({name: shared[n] for name, n in zip("nU yt yf dv gs".split(), "En kk k2 lw L".split())})
    left = [{n: K.carve(T) for n in "al0 al1 be ka rh rkr vt kat bet TaT Wv".split()} for _ in range(2)]
    St, SP_, St2 = K.carve(P), K.carve(P), K.carve(P)
    pcols, all_ends = [K.carve(8) for _ in range(2)], [K.carve(T // HEAD) for _ in range(2)]
    spare = [K.wslots[n][:, T * q:T * (q + 1)] for n in range(6) for q in range(4)]
    mats = {(n, h): spare.pop() for h in range(2) for n in "M MT N NT X O16 O32 ak".split()}
    for n in range(2):
        left[n].update({(name, h): spare.pop() for h in range(2) for name in ("qb", "qk")})
    tile = lambda a, t: a[:, t * P:(t + 1) * P]
    tiles = lambda a: a.rearrange("p (t n) -> p t n", n=P)
    wide = lambda name: K.c(name).unsqueeze(1).to_broadcast([P, NT, P])
    col = lambda name, p: K.columns[:, ds(K.cols[name][0] + p, 1)]
    def mm_tiles(pairs, after):
        b = K.bank()
        for t in range(NT):
            m = K.PE.run(nc.tensor.matmul, b[:, t * P:(t + 1) * P], tile(pairs[0], t), tile(pairs[1], t), start=True,
                         stop=True, after=[after, b.free] if t == 0 else (), counted=t == NT - 1)
        b.free = []
        return b, m

    def copy_out(dst, pairs, after):
        b, m1 = mm_tiles(pairs, after)
        m2 = S.run(act, dst, b[:, :], ACT.Copy, after=m1)
        b.free = [m2]
        return m2

    def add_to_X(h, pairs, after):
        b, m1 = mm_tiles(pairs, after)
        m2 = V.run(tt, mats["X", h], mats["X", h], b[:, :], ALU.add, after=m1)
        b.free = [m2]
        return m2

    hs = lambda arr, t, h: arr[:, t * P + h * HEAD:t * P + (h + 1) * HEAD]

    def by_head(dst, mat, rhs, after):
        b = K.bank()
        for t in range(NT):
            for h in range(2):
                m1 = K.PE.run(nc.tensor.matmul, hs(b, t, h), tile(mats[mat, h], t), hs(rhs, t, h), start=True,
                              stop=True, after=[after, b.free] if t + h == 0 else (), counted=t == NT - 1 and h == 1)
        m2 = S.run(act, dst, b[:, :], ACT.Copy, after=m1)
        b.free = [m2]
        return m2

    def load(p, n):
        x = ins[n]
        return K.SP.dma(x, x.t.rearrange("p w t -> p (w t)"),
                        scratch.rearrange("c p w t -> (c p) (w t)")[ds(p * P, P), :], after=x.free)

    def prepare(p, n, m_in):
        B, pcol, x = {**shared, **left[n]}, pcols[n], ins[n]
        r, k, v, _, sg, a = (x[:, q, :] for q in range(6))
        for q, name in enumerate(("k_k", "k_a", "r_k", "lnx_g", "lnx_b")):
            V.run(cp, pcol[:, q:q + 1], col(name, p))
        V.run(ts, pcol[:, 5:6], pcol[:, 1:2], -1.0, 1.0, ALU.mult, ALU.add)
        yield
        V.run(ts, B["lw"], sg, -float(np.exp(-0.5)), None, ALU.mult, after=m_in)
        m = V.run(nc.vector.tensor_tensor_scan, B["L"], K.c("scan64"), B["lw"], 0.0, ALU.mult, ALU.add)
        m1 = V.run(tt, B["Em"], B["L"], B["lw"], ALU.subtract)
        yield
        S.run(act, B["Ep"], B["L"], ACT.Exp, after=m)
        S.run(act, B["En"], B["L"], ACT.Exp, scale=-1.0)
        m_e = S.run(act, B["Em"], B["Em"], ACT.Exp, after=m1)
        m = V.run(ts, B["kk"], k, pcol[:, 0:1], None, ALU.mult)
        m = V.run(tt, B["lw"], B["kk"], B["kk"], ALU.mult)
        b = K.bank()
        m = K.matmuls(b[:, :], [(K.c("same_head"), B["lw"])], after=[m, b.free])
        yield
        m = S.run(act, B["L"], b[:, :], ACT.Sqrt, after=m)
        b.free = [m]
        V.run(ts, B["L"], B["L"], 1e-12, None, ALU.max, after=m)
        V.run(nc.vector.reciprocal, B["L"], B["L"])
        yield
        V.run(tt, B["kk"], B["kk"], B["L"], ALU.mult)
        V.run(cp, all_ends[n], B["Ep"][:, HEAD - 1:T:HEAD], after=m_e)
        yield
        V.run(ts, B["k2"], a, pcol[:, 1:2], pcol[:, 5:6], ALU.mult, ALU.add)
        yield
        V.run(tt, B["k2"], B["k2"], k, ALU.mult)
        V.run(tt, B["be"], B["kk"], a, ALU.mult, after=m_e)
        yield
        V.run(tt, B["be"], B["be"], B["En"], ALU.mult)
        V.run(tt, B["ka"], B["k2"], B["En"], ALU.mult)
        yield
        V.run(tt, B["rh"], r, B["Ep"], ALU.mult)
        for h in range(2):
            hc = K.c("head_cols")[:, h:h + 1]
            V.run(stt, B[f"al{h}"], B["kk"], hc, B["Em"], ALU.mult, ALU.mult)
            yield
        yield
        m = V.run(stt, B["rkr"], r, pcol[:, 2:3], B["k2"], ALU.mult, ALU.mult)
        b = K.bank()
        m1 = K.matmuls(b[:, :], [(K.c("same_head"), B["rkr"])], after=[m, b.free])
        m1 = V.run(tt, B["rkr"], b[:, :], v, ALU.mult, after=m1)
        b.free = [m1]
        x.free = [m1]

    def front(p, n, start):
        B, x, m, v = {**shared, **left[n]}, ins[n], start, ins[n][:, V_, :]
        for src, dst in ((v, "vt"), (B["ka"], "kat"), (B["be"], "bet"), (B["al0"], "al0t"), (B["al1"], "al1t")):
            b = K.bank()
            m1 = K.transposes([(b[:, t * P:(t + 1) * P], tile(src, t)) for t in range(NT)], b, after=m)
            m_t = S.run(act, B[dst], b[:, :], ACT.Copy, after=m1)
            b.free = [m_t]
            if src is v:
                x.free = x.free + [m1]
            if dst in ("kat", "al0t"):
                yield
        made = []

        def mask_made():
            for b, m1, h, outs in made:
                for name, mask in outs:
                    dst = B[name, h] if (name, h) in B else mats[name, h]
                    m2 = V.run(tt, tiles(dst), tiles(b[:, :]), wide(mask), ALU.mult, after=m1)
                b.free = [m2]
            made.clear()

        for h in range(2):
            al, rows = B[f"al{h}"], slice(HEAD * h, HEAD * h + HEAD)
            for lhs, rhs, outs in ((B["be"], al, [("M", "neg_up16")]),
                                   (al, B["be"], [("MT", "neg_low16"), ("O16", "neg_off16"), ("O32", "neg_off32")]),
                                   (B["ka"], al, [("ak", "up64")]),
                                   (B["be"][rows], B["rh"][rows], [("qb", "upeq64")]),
                                   (B["ka"][rows], B["rh"][rows], [("qk", "upeq64")])):
                made.append((*mm_tiles((lhs, rhs), m), h, outs))
                if len(made) == 2:
                    yield
                    mask_made()
        for h in range(2):
            m_A = V.run(tt, tiles(mats["X", h]), tiles(mats["M", h]), wide("ident"), ALU.add)

        m_sq, m_X = [m_A, m_A], [m_A, m_A]
        for step in range(3):
            src, dst = (("M", "MT"), ("N", "NT")) if step % 2 == 0 else (("N", "NT"), ("M", "MT"))
            for h in range(2):
                M, MT = mats[src[0], h], mats[src[1], h]
                if step < 2:
                    copy_out(mats[dst[0], h], (MT, M), [m_sq[h], m_X[h]])
                    yield
                m_sq[h] = copy_out(mats[dst[1], h], (M, MT), [m_sq[h], m_X[h]])
                yield
            for h in range(2):
                m_X[h] = add_to_X(h, (mats[dst[1], h], mats["X", h]), [m_sq[h], m_X[h]])
            yield
        for off in ("O16", "O32"):
            m_G = [None, None]
            for h in range(2):
                b = K.bank()
                m1 = K.transposes([(b[:, t * P:(t + 1) * P], tile(mats["X", h], t)) for t in range(NT)], b, after=m_X[h])
                m1 = S.run(act, mats["N", h], b[:, :], ACT.Copy, after=m1)
                b.free = [m1]
                yield
                m_G[h] = copy_out(mats["M", h], (mats[off, h], mats["X", h]), m_X[h])
                yield
            for h in range(2):
                m_X[h] = add_to_X(h, (mats["N", h], mats["M", h]), m_G[h])
            yield
        m1 = by_head(B["X2"], "ak", B["vt"], [m_t, m_A])
        yield
        by_head(B["Wv"], "X", B["X2"], [m1, m_X])
        b = K.bank()
        for t in range(NT):
            m1 = K.matmuls(b[:, t * P:(t + 1) * P], [(tile(B[f"al{h}t"], t), tile(mats["X", h], t)) for h in range(2)],
                           after=[m_t, m_X, b.free if t == 0 else ()])
        m1 = S.run(act, B["TaT"], b[:, :], ACT.Copy, after=m1)
        b.free = [m1]

    def back(p, n, start, ahead):
        B, pcol, ends, x = {**shared, **left[n]}, pcols[n], all_ends[n], ins[n]
        m_gate = S.run(act, B["gate"], x[:, G_, :], ACT.Silu)
        x.free = x.free + [m_gate]
        if ahead:
            m_in = load(p + 2, n)
        m_S = V.run(nc.vector.memset, St, 0.0)
        for c in range(T // HEAD):
            t, q = c // 2, c % 2
            rows = slice(HEAD * q, HEAD * q + HEAD)
            b = K.bank()
            K.PE.run(nc.tensor.matmul, b[:, 0:P], tile(B["TaT"], t), St, start=True, stop=True,
                     after=[start, m_S, b.free], counted=False)
            m2 = K.PE.run(nc.tensor.matmul, b[:, P:2 * P], tile(B["rh"], t), St, start=True, stop=True)
            yield
            m_U = V.run(stt, tile(B["nU"], t)[rows], b[rows, 0:P], -1.0, tile(B["Wv"], t)[rows], ALU.mult, ALU.subtract,
                        after=m2)
            m3 = V.run(cp, tile(B["yt"], t)[rows], b[rows, P:2 * P])
            b.free = [m3]
            if c == T // HEAD - 1:
                break
            end = ends[:, c:c + 1]
            V.run(ts, SP_, St, end, None, ALU.mult)
            b = K.bank()
            m2 = K.matmuls(b[:, 0:P], [(tile(B["bet"], t)[rows], tile(B["nU"], t)[rows]),
                                       (tile(B["kat"], t)[rows], tile(B["vt"], t)[rows])], after=[m_U, b.free])
            yield
            m3 = V.run(stt, St2, b[:, 0:P], end, K.c("same_head"), ALU.mult, ALU.mult, after=m2)
            b.free = [m3]
            m_S = V.run(tt, St, St2, SP_, ALU.add)
        b = K.bank()
        for t in range(NT):
            for h in range(2):
                m2 = K.matmuls(hs(b, t, h), [(tile(B["qb", h], t), hs(B["nU"], t, h)),
                                             (tile(B["qk", h], t), hs(B["vt"], t, h))],
                               after=[m_U, b.free if t + h == 0 else ()])
        yield
        m2 = V.run(tt, B["yt"], B["yt"], b[:, :], ALU.add, after=m2)
        b.free = [m2]
        yield
        b = K.bank()
        m2 = K.transposes([(b[:, t * P:(t + 1) * P], tile(B["yt"], t)) for t in range(NT)], b, after=m2)
        m2 = V.run(cp, B["yf"], b[:, :], after=m2)
        b.free = [m2]
        yield
        b = K.bank()
        m2 = K.matmuls(b[:, :], [(K.c("same_head"), B["yf"])], after=[m2, b.free])
        m2 = V.run(stt, B["dv"], b[:, :], -1.0 / HEAD, B["yf"], ALU.mult, ALU.add, after=m2)
        b.free = [m2]
        m2 = S.run(act, B["yf"], B["dv"], ACT.Square, after=m2)
        yield
        b = K.bank()
        m2 = K.matmuls(b[:, :], [(K.c("same_head"), B["yf"])], after=[m2, b.free])
        m2 = V.run(ts, B["gs"], b[:, :], 1.0 / HEAD, 64e-5, ALU.mult, ALU.add, after=m2)
        b.free = [m2]
        m2 = S.run(act, B["gs"], B["gs"], ACT.Sqrt, after=m2)
        V.run(nc.vector.reciprocal, B["gs"], B["gs"], after=m2)
        V.run(tt, B["dv"], B["dv"], B["gs"], ALU.mult)
        V.run(ts, B["dv"], B["dv"], pcol[:, 3:4], pcol[:, 4:5], ALU.mult, ALU.add)
        V.run(tt, B["dv"], B["dv"], B["rkr"], ALU.add)
        V.run(tt, y_out[:, ds(p, 1), :], B["dv"].unsqueeze(1), B["gate"].unsqueeze(1), ALU.mult)
        if ahead:
            yield from prepare(p + 2, n, m_in)

    first = [load(n, n) for n in range(2)]
    K.braid(prepare(0, 0, first[0]), None)
    K.pipeline(KD, front, back, before=prepare(1, 1, first[1]))


def columns_of(K, name, n):
    a = K.cols[name][0] + n * KD
    return K.columns[:, a:a + KD]


def post_and_ple(K, A, n, w_out, src):
    nc, V, S, prog = K.nc, K.DVE, K.ACT, K.prog
    stt, tt = nc.vector.scalar_tensor_tensor, nc.vector.tensor_tensor
    out = K.carve(KD, T)
    pT = K.carve(2, T)
    sig = Ring(prog, [Slot(prog, K.carve(T)) for _ in range(2)])
    p_in = A["p_2"][n, 0]
    s = K.wring.take()
    m = K.SP.dma(s, s[:, 0:4 * 256].rearrange("p (t d) -> p t d", d=256), p_in.rearrange("(t p) d -> p t d", p=P),
                 after=s.free)
    for j in range(2):
        b = K.bank()
        m1 = K.transposes([(b[:, t * P:(t + 1) * P], s[:, t * 256 + j * P:t * 256 + (j + 1) * P]) for t in range(NT)], b,
                          after=m)
        m1 = V.run(nc.vector.tensor_copy, pT[:, j, :], b[:, :], after=m1)
        b.free = [m1]
    s.free = [m1]
    wv = w_out.rearrange("(k p) n -> p k n", p=P)

    def add_normed(gains):
        marks = []
        for k in range(KD):
            V.run(tt, out[:, k, :], out[:, k, :], K.rstd[:, :], ALU.mult)
            marks.append(V.run(stt, K.h[:, k, :], out[:, k, :], gains[:, k:k + 1], K.h[:, k, :], ALU.mult, ALU.add))
        return marks

    prog.phase()
    sums = Squares(K)
    for i in range(KD // 2):
        s, w, m_w = K.weights(wv[:, :, ds(i * 256, 256)], None)
        for j in range(2):
            b, m = K.project(w, j, src, m_in=m_w)
            s.free = [m]
            m = S.run(nc.scalar.activation, out[:, 2 * i + j, :], b[:, :], ACT.Copy, after=m)
            b.free = [m]
            sums.square(out[:, 2 * i + j, :], m)
    sums.rstd()
    new_h = add_normed(columns_of(K, "norm_post", n))
    sums = Squares(K)
    pgv = A["ple_gate_2"][n].rearrange("(k p) n -> p k n", p=P)
    pwv = A["ple_w_2"][n].rearrange("(k p) n -> p k n", p=P)

    s2, w2, m_w2 = K.weights(pwv, None, rows=2)
    for i in range(KD // 2):
        s, w, m_w = K.weights(pgv[:, :, ds(i * 256, 256)], None)
        for j in range(2):
            b, m = K.project(w, j, K.h, m_in=m_w, each=new_h if i + j == 0 else None)
            b2, m2 = K.project(w2, 2 * i + j, pT, k=2, m_in=m_w2)
            s.free, s2.free = [m], [m2]
            a = sig.take()
            m = S.run(nc.scalar.activation, a[:, :], b[:, :], ACT.Sigmoid, after=[m, a.free])
            b.free = [m]
            m = V.run(tt, out[:, 2 * i + j, :], a[:, :], b2[:, :], ALU.mult, after=[m, m2])
            b2.free = a.free = [m]
            sums.square(out[:, 2 * i + j, :], m)
    sums.rstd()
    new_h = add_normed(columns_of(K, "ple_norm", n))
    if n == 0:
        sums = Squares(K)
        for k in range(KD):
            sums.square(K.h[:, k, :], new_h[k])
        sums.rstd()
    K.new_phase()


LAM_INIT = 0.8 - 0.6 * float(np.exp(-0.3))


def attention(K, A, o_out):
    nc, V, S, prog = K.nc, K.DVE, K.ACT, K.prog
    ts, tt, stt = nc.vector.tensor_scalar, nc.vector.tensor_tensor, nc.vector.scalar_tensor_tensor
    act, cp = nc.scalar.activation, nc.vector.tensor_copy
    K.fetch("cos", "sin", "turn", "future")
    hk = K.carve(KD, T)
    chunks = [K.h[:, k, :] for k in range(KD)]
    K.scaled(K.u, chunks, columns_of(K, "norm_pre", 1))
    K.scaled(hk, chunks, columns_of(K, "kv_norm", 0))
    lq = K.carve(4, HEAD)
    lam = K.carve(8)
    m = S.dma(prog.arrivals("lambda"), lq.rearrange("p a d -> p (a d)"),
                 A["b_lambda_2"][0].rearrange("a d -> (a d)").partition_broadcast(P))
    V.run(tt, lq[:, 0:2, :], lq[:, 0:4:2, :], lq[:, 1:4:2, :], ALU.mult, after=m)
    m = V.run(nc.vector.tensor_reduce, lam[:, 0:2], lq[:, 0:2, :], AX.X, ALU.add)
    m = S.run(act, lam[:, 0:2], lam[:, 0:2], ACT.Exp, after=m)
    V.run(tt, lam[:, 2:3], lam[:, 1:2], lam[:, 0:1], ALU.subtract, after=m)
    V.run(ts, lam[:, 2:3], lam[:, 2:3], LAM_INIT, None, ALU.subtract)
    V.run(ts, lam[:, 3:4], K.col("subln"), 1.0 - LAM_INIT, None, ALU.mult)
    left = [[K.carve(T) for _ in range(4)] for _ in range(2)]
    turned, of, sq = K.carve(T), K.carve(T), K.carve(T)
    probs = [Slot(prog, K.carve(T)) for _ in range(4)]
    pT = [Slot(prog, K.carve(T)) for _ in range(2)]
    st = K.carve(4, 2, 4)
    prog.phase()
    qv = A["b_w_in_2"][0].rearrange("(k p) n -> p k n", p=P)
    kv = A["kv_w_2"].rearrange("(k p) n -> p k n", p=P)

    def front(h, n, start):
        q, k, vtok, gate = left[n]
        slots = K.wslots[2 * n:2 * n + 2]
        w, m_w = [], []
        for s, v in zip(slots, (qv, kv)):
            w.append(s[:, :].rearrange("p (a k n) -> p a k n", a=2, k=KD))
            K.SP.dma(s, w[-1][:, 0], v[:, :, ds(h * P, P)], after=s.free)
            m_w.append(K.SP.dma(s, w[-1][:, 1], v[:, :, ds(D + h * P, P)]))
        for dst, wi, src, scale in ((q, w[0], K.u, HEAD ** -0.5), (k, w[1], hk, 1.0)):
            b, m = yield from K.project_in_two(wi[:, 0], 0, src, m_in=m_w)
            m = S.run(act, dst, b[:, :], ACT.Copy, scale=scale, after=m)
            b.free = [m]
            yield
            b = K.bank()
            m = K.matmuls(b[:, :], [(K.c("turn"), dst)], after=[m, b.free])
            V.run(tt, turned, b[:, :], K.c("sin"), ALU.mult, after=m)
            b.free = [V.count.mark()]
            V.run(tt, dst, dst, K.c("cos"), ALU.mult)
            V.run(tt, dst, dst, turned, ALU.add)
        b, m = yield from K.project_in_two(w[0][:, 1], 0, K.u)
        slots[0].free = [m]
        m = S.run(act, gate, b[:, :], ACT.Silu, after=m)
        b.free = [m]
        b = K.bank()
        for t in range(NT):
            m = K.matmuls(b[:, t * P:(t + 1) * P], [(hk[:, i, t * P:(t + 1) * P], w[1][:, 1, i, :]) for i in range(KD)],
                          after=b.free if t == 0 else ())
            if t % 2:
                yield
        slots[1].free = [m]
        m = S.run(act, vtok, b[:, :], ACT.Copy, after=m)
        b.free = [m]

    def back(h, n, start, ahead):
        q, k, vtok, gate = left[n]
        ob = K.bank()
        other_bank = lambda b: K.bank() if b is ob else b

        def scores(qb):
            b2, n = [], (qb + 1) * P
            for c in range(2):
                rows = slice(HEAD * c, HEAD * c + HEAD)
                b = other_bank(K.bank())
                m = K.matmuls(b[:, 0:n], [(q[rows, qb * P:n], k[rows, 0:n])], after=[start, b.free])
                b2.append((b, m))
            return b2

        b2 = scores(0)
        for qb in range(NT):
            n = (qb + 1) * P
            pr = probs[2 * (qb % 2):2 * (qb % 2) + 2]
            for c, (b, m) in enumerate(b2):
                m = V.run(tt, b[:, qb * P:n], b[:, qb * P:n], K.c("future"), ALU.add, after=m)
                m = V.run(nc.vector.tensor_reduce, st[:, qb, c, 0:1], b[:, 0:n], AX.X, ALU.max, negate=True)
                m = S.run(act, pr[c][:, 0:n], b[:, 0:n], ACT.Exp, bias=st[:, qb, c, 0:1], accum_out=st[:, qb, c, 1:2],
                          after=[m, pr[c].free])
                b.free = [m]
            yield
            V.run(nc.vector.reciprocal, st[:, qb, :, 2:3], st[:, qb, :, 1:2], after=m)
            V.run(tt, st[:, qb, 1, 3:4], st[:, qb, 1, 2:3], lam[:, 2:3], ALU.mult)
            V.run(ts, pr[0][:, 0:n], pr[0][:, 0:n], st[:, qb, 0, 2:3], None, ALU.mult)
            m_p = V.run(stt, pr[0][:, 0:n], pr[1][:, 0:n], st[:, qb, 1, 3:4], pr[0][:, 0:n], ALU.mult, ALU.add)
            if qb < NT - 1:
                b2 = scores(qb + 1)
            yield
            b = other_bank(K.bank())
            m = K.transposes([(b[:, kb * P:(kb + 1) * P], pr[0][:, kb * P:(kb + 1) * P]) for kb in range(qb + 1)], b,
                             after=m_p)
            pr[0].free = pr[1].free = [m]
            pt = pT[qb % 2]
            m = S.run(act, pt[:, 0:n], b[:, 0:n], ACT.Copy, after=[m, pt.free])
            b.free = [m]
            yield
            m = K.matmuls(ob[:, qb * P:n], [(vtok[:, kb * P:(kb + 1) * P], pt[:, kb * P:(kb + 1) * P])
                                            for kb in range(qb + 1)], after=[m, ob.free if qb == 0 else ()])
            pt.free = [m]
        m = V.run(cp, of, ob[:, :], after=m)
        ob.free = [m]
        m = S.run(act, sq, of, ACT.Square, after=m)
        yield
        b = K.bank()
        m = K.matmuls(b[:, :], [(K.c("ones"), sq)], after=[m, b.free])
        m = V.run(ts, sq, b[:, :], 1.0 / P, 1e-5, ALU.mult, ALU.add, after=m)
        b.free = [m]
        m = S.run(act, sq, sq, ACT.Sqrt, after=m)
        V.run(nc.vector.reciprocal, sq, sq, after=m)
        V.run(tt, of, of, sq, ALU.mult)
        V.run(stt, o_out[:, ds(h, 1), :], of.unsqueeze(1), lam[:, 3:4], gate.unsqueeze(1), ALU.mult, ALU.mult)

    K.pipeline(KD, front, back)
    K.prog.phase()


def block2(K, A, scratch):
    inputs_stored = rwkv_inputs(K, A, scratch)
    K.new_phase()
    K.prog.join(K.SP)
    K.SP.wait(inputs_stored)
    rwkv_pairs(K, scratch, K.u)
    K.new_phase()
    for s in K.wslots:
        s.free = [e.count.mark() for e in (K.PE, K.ACT, K.DVE)]
    post_and_ple(K, A, 0, A["a_w_out_2"][0], K.u)
    o_out = K.carve(KD, T)
    attention(K, A, o_out)
    K.big_at = KD * T
    post_and_ple(K, A, 1, A["b_w_out_2"][0], o_out)
def block1_mixer(K, A):
    r = lambda a: a.rearrange("(k p) -> k p", p=P)
    K.rms([K.h[:, k, :] for k in range(KD)])
    adaln_start(K, A["w_ada"][0])
    K.new_phase()
    modulated_norm(K, "norm_mix_g", 0, 8, K.u)
    K.new_phase()
    w_in = A["w_in"][0]
    K.fetch("upper")
    K.big_const = K.big_at
    y = K.carve(16, T)
    K.y_ssd = y
    keep_y = K.big_at
    ssd_decays(K, w_in, A["dt_bias"][0], A["A_log"][0], K.cs_dram, None)
    K.new_phase(K.kept_ssd, K.m_cs)
    ssd_groups(K, w_in, K.cs_dram, A["D_skip"][0], y)
    K.new_phase(keep_y)
    K.fetch("inv2", "inv4", "inv8", "inv16")
    used = K.big_at
    pooled = K.carve(KD, T)
    merged = K.carve(KD, T)
    pool_branch(K, w_in, A["pool_w"][0], pooled)
    K.prog.phase()
    K.big_at = used + 16 * T
    combine(K, w_in, A["w_br_ssd"][0], A["w_br_pool"][0], A["w_out"][0], y, pooled, merged)
    K.new_phase()


def vector_list(A):
    f = lambda a: a.rearrange("(k p) -> k p", p=P)
    f2 = lambda a: a.rearrange("i (k p) -> (i k) p", p=P)
    names = [("conv_w", f2(A["conv_w"][0])), ("conv_b", f(A["conv_b"][0])), ("ssd_norm_g", f(A["ssd_norm_g"][0])),
             ("b_ada", f(A["b_ada"][0])), ("c", f2(A["c"])), ("norm_mix_g", f(A["norm_mix_g"][0])),
             ("norm_ffn_g", f(A["norm_ffn_g"][0])), ("final_norm_g", f(A["final_norm_g"])),
             ("pool_scale", f(A["pool_scale"][0]))]
    names += [("a_mu", A["a_mu_2"][0].rearrange("i (k p) -> (i k) p", p=P)),
              ("norm_pre", f2(A["norm_pre_2"])), ("norm_post", f2(A["norm_post_2"])), ("ple_norm", f2(A["ple_norm_2"])),
              ("kv_norm", f(A["kv_norm_2"])), ("subln", f2(A["b_subln_2"]))]
    names += [(n, f(A[f"a_{n}_2"][0])) for n in ("w0", "a0", "k_k", "k_a", "lnx_g", "lnx_b")]
    names += [("r_k", A["a_r_k_2"][0].rearrange("(k a) n -> k (a n)", a=2))]
    return names


def build_program(nc, A, consts, out):
    K = Kernel(nc, consts)
    K.cs_dram = nc.dram_tensor("ssd_sums", [32, T], F32, kind="Internal").ap()
    K.u_rows = nc.dram_tensor("u_rows", [T, D], F32, kind="Internal").ap()
    K.total_rows = nc.dram_tensor("total_rows", [T + P, D], F32, kind="Internal").ap()
    rwkv_dram = nc.dram_tensor("rwkv_inputs", [KD, P, 6, T], F32, kind="Internal").ap()
    K.prog.start()
    K.fetch("ident", "ones")
    K.load_columns(vector_list(A))
    K.load_x(A["x"][0])
    K.prog.phase()
    block1_mixer(K, A)
    moe(K, A)
    block2(K, A, rwkv_dram)
    K.SP.wait(K.store_rows(K.h, out[0]))


def kernel(**inputs):
    import concourse.bacc as bacc
    from concourse.bass_utils import run_bass_kernel_spmd

    nc = bacc.Bacc("TRN2", target_bir_lowering=False, num_devices=1)
    arrays, A = {}, {}
    for name, value in inputs.items():
        arrays[f"in_{name}"] = np.ascontiguousarray(value)
        A[name] = nc.dram_tensor(f"in_{name}", arrays[f"in_{name}"].shape, F32, kind="ExternalInput").ap()
    arrays["shape_consts"] = const_table()
    consts = nc.dram_tensor("shape_consts", arrays["shape_consts"].shape, F32, kind="ExternalInput").ap()
    out = nc.dram_tensor("out_h", (1, T, D), F32, kind="ExternalOutput").ap()
    build_program(nc, A, consts, out)
    r = run_bass_kernel_spmd(nc, [arrays], core_ids=[0])
    return r.results[0]["out_h"]
```
